# Optimizing a Trainium2 kernel written in Bass

```python
import jax, jax.numpy as jnp
from jax import lax
import numpy as np
import math

D_MODEL = 1024
BATCH = 1
SEQ = 512
DEPTH = 2

HEAD_DIM = 64
BLOCK = 128
A_Q_HEADS = 8
A_KV_HEADS = 2
A_WINDOW = 128
B_Q_HEADS = 8
B_KV_HEADS = 2
CMP_LEN = 32
CMP_STRIDE = 16
CMP_HIDDEN = 128
SLC_LEN = 64
N_SLC = 16
N_LOCAL_SLC = 2
B_WINDOW = 512
D_FF = 2816
CONV_WIDTH = 3
ROPE_THETA = 10000.0
EPS = 1e-6
TINY = 1e-30

A_WIDTH = A_Q_HEADS * HEAD_DIM
A_KV_WIDTH = A_KV_HEADS * HEAD_DIM
B_WIDTH = B_Q_HEADS * HEAD_DIM
B_KV_WIDTH = B_KV_HEADS * HEAD_DIM
N_NSA_GATES = 3 * B_Q_HEADS
IN_SIZES = (A_WIDTH, A_KV_WIDTH, A_KV_WIDTH,
            B_WIDTH, B_KV_WIDTH, B_KV_WIDTH, B_KV_WIDTH, B_KV_WIDTH, B_KV_WIDTH, B_KV_WIDTH,
            N_NSA_GATES, D_MODEL, D_MODEL)
IN_COLS = sum(IN_SIZES)


def rms_norm(x, gain):
    xf = x.astype(jnp.float32)
    y = xf * lax.rsqrt(jnp.mean(xf * xf, axis=-1, keepdims=True) + EPS)
    return (y * gain.astype(jnp.float32)).astype(x.dtype)

def apply_rope(x, positions):
    half = HEAD_DIM // 2
    inv_freq = ROPE_THETA ** (-jnp.arange(half, dtype=jnp.float32) / half)
    ang = positions.astype(jnp.float32)[..., None] * inv_freq
    cos = jnp.cos(ang)[:, :, None, :]
    sin = jnp.sin(ang)[:, :, None, :]
    xf = x.astype(jnp.float32)
    x1, x2 = xf[..., :half], xf[..., half:]
    return jnp.concatenate([x1 * cos - x2 * sin, x2 * cos + x1 * sin], axis=-1).astype(x.dtype)

def masked_softmax(s, mask):
    s = jnp.where(mask, s, -jnp.inf)
    m = jnp.max(s, axis=-1, keepdims=True)
    m = jnp.where(jnp.isfinite(m), m, 0.0)
    p = jnp.exp(s - m)
    return p / jnp.maximum(jnp.sum(p, axis=-1, keepdims=True), TINY)

def band_context(t, n_prev):
    nb = t.shape[1]
    pad = [(0, 0)] * t.ndim
    pad[1] = (n_prev, 0)
    tp = jnp.pad(t, pad)
    return jnp.concatenate([tp[:, j:j + nb] for j in range(n_prev + 1)], axis=2)

def swa_sink_attention(q, k, v, sinks):
    b, s, g, r, d = q.shape
    nb = s // BLOCK
    n_prev = -(-A_WINDOW // BLOCK)
    qb = q.reshape(b, nb, BLOCK, g, r, d)
    kc = band_context(k.reshape(b, nb, BLOCK, g, d), n_prev)
    vc = band_context(v.reshape(b, nb, BLOCK, g, d), n_prev)
    scores = jnp.einsum('bnqgrd,bnkgd->bngrqk', qb, kc).astype(jnp.float32) * (d ** -0.5)
    blk = jnp.arange(nb)[:, None, None] * BLOCK
    qpos = blk + jnp.arange(BLOCK)[None, :, None]
    kpos = blk - n_prev * BLOCK + jnp.arange((n_prev + 1) * BLOCK)[None, None, :]
    rel = qpos - kpos
    mask = (rel >= 0) & (rel < A_WINDOW) & (kpos >= 0)
    scores = jnp.where(mask[None, :, None, None], scores, -jnp.inf)
    sink = sinks.astype(jnp.float32).reshape(1, 1, g, r, 1, 1)
    m = jnp.maximum(jnp.max(scores, axis=-1, keepdims=True), sink)
    p = jnp.exp(scores - m)
    p = p / (jnp.sum(p, axis=-1, keepdims=True) + jnp.exp(sink - m))
    o = jnp.einsum('bngrqk,bnkgd->bnqgrd', p.astype(v.dtype), vc)
    return o.reshape(b, s, g * r * d)

def compress(t, pos_emb, w1, b1, w2):
    b, s, g, d = t.shape
    ratio = CMP_LEN // CMP_STRIDE
    chunks = t.reshape(b, s // CMP_STRIDE, CMP_STRIDE, g, d)
    nc = s // CMP_STRIDE - ratio + 1
    blocks = jnp.concatenate([chunks[:, j:j + nc] for j in range(ratio)], axis=2)
    blocks = blocks + pos_emb[None, None, :, None, :]
    flat = blocks.transpose(0, 1, 3, 2, 4).reshape(b, nc, g, CMP_LEN * d)
    hid = jax.nn.gelu(flat @ w1 + b1, approximate=True)
    return hid @ w2

def nsa_attention(q_raw, q_rot, k_cmp, v_cmp, k_slc, v_slc, k_win, v_win, gates):
    b, s, g, r, d = q_rot.shape
    nb = s // BLOCK
    nc = k_cmp.shape[1]
    ns = s // SLC_LEN
    n_sel = min(N_SLC, ns)
    scale = d ** -0.5
    ratio_c = CMP_LEN // CMP_STRIDE
    ratio_s = SLC_LEN // CMP_STRIDE
    ks_blocks = k_slc.reshape(b, ns, SLC_LEN, g, d).transpose(0, 3, 1, 2, 4)
    vs_blocks = v_slc.reshape(b, ns, SLC_LEN, g, d).transpose(0, 3, 1, 2, 4)
    kw_pad = jnp.pad(k_win, ((0, 0), (B_WINDOW, 0), (0, 0), (0, 0)))
    vw_pad = jnp.pad(v_win, ((0, 0), (B_WINDOW, 0), (0, 0), (0, 0)))
    cmp_end = jnp.arange(nc) * CMP_STRIDE + CMP_LEN - 1
    blk_ids = jnp.arange(ns)
    gather = jax.vmap(jax.vmap(lambda blocks, ix: blocks[ix]))

    def one_block(i):
        start = i * BLOCK
        t = start + jnp.arange(BLOCK)
        qr = lax.dynamic_slice_in_dim(q_rot, start, BLOCK, axis=1)
        qn = lax.dynamic_slice_in_dim(q_raw, start, BLOCK, axis=1)
        gt = lax.dynamic_slice_in_dim(gates, start, BLOCK, axis=1)
        s_c = jnp.einsum('bqgrd,bcgd->bgrqc', qn, k_cmp).astype(jnp.float32) * scale
        p_c = masked_softmax(s_c, cmp_end[None, :] <= t[:, None])
        o_c = jnp.einsum('bgrqc,bcgd->bqgrd', p_c.astype(v_cmp.dtype), v_cmp)
        imp = jnp.sum(p_c, axis=2)
        imp = jnp.pad(imp, ((0, 0), (0, 0), (0, 0), (ratio_c - 1, ratio_s * ns - nc)))
        imp_s = jnp.zeros(imp.shape[:-1] + (ns,), jnp.float32)
        for m in range(ratio_s):
            for n in range(ratio_c):
                off = m - n + ratio_c - 1
                imp_s = imp_s + imp[..., off:off + ratio_s * ns:ratio_s]
        cur = t // SLC_LEN
        valid = blk_ids[None, :] <= cur[:, None]
        forced = (blk_ids[None, :] == 0) | (valid & (blk_ids[None, :] > cur[:, None] - N_LOCAL_SLC))
        imp_s = jnp.where(forced, jnp.inf, jnp.where(valid, imp_s, -jnp.inf))
        _, idx = lax.top_k(imp_s, n_sel)
        k_sel = gather(ks_blocks, idx)
        v_sel = gather(vs_blocks, idx)
        s_s = jnp.einsum('bqgrd,bgqkld->bgrqkl', qr, k_sel).astype(jnp.float32) * scale
        tok = idx[..., None] * SLC_LEN + jnp.arange(SLC_LEN)
        mask_s = (tok <= t[None, None, :, None, None]).reshape(b, g, 1, BLOCK, n_sel * SLC_LEN)
        p_s = masked_softmax(s_s.reshape(b, g, r, BLOCK, n_sel * SLC_LEN), mask_s)
        o_s = jnp.einsum('bgrqn,bgqnd->bqgrd', p_s.astype(v_slc.dtype),
                         v_sel.reshape(b, g, BLOCK, n_sel * SLC_LEN, d))
        kwin = lax.dynamic_slice_in_dim(kw_pad, start, BLOCK + B_WINDOW, axis=1)
        vwin = lax.dynamic_slice_in_dim(vw_pad, start, BLOCK + B_WINDOW, axis=1)
        kpos = start - B_WINDOW + jnp.arange(BLOCK + B_WINDOW)
        rel = t[:, None] - kpos[None, :]
        mask_w = (rel >= 0) & (rel < B_WINDOW) & (kpos[None, :] >= 0)
        s_w = jnp.einsum('bqgrd,bkgd->bgrqk', qr, kwin).astype(jnp.float32) * scale
        p_w = masked_softmax(s_w, mask_w)
        o_w = jnp.einsum('bgrqk,bkgd->bqgrd', p_w.astype(v_win.dtype), vwin)
        return gt[..., 0:1] * o_c + gt[..., 1:2] * o_s + gt[..., 2:3] * o_w

    out = lax.map(one_block, jnp.arange(nb))
    return out.transpose(1, 0, 2, 3, 4, 5).reshape(b, s, g * r * d)

def conv_ffn(h, w_up, conv_w, conv_b, w_down):
    u = h @ w_up
    s = u.shape[1]
    up = jnp.pad(u, ((0, 0), (CONV_WIDTH - 1, 0), (0, 0)))
    c = conv_b
    for k in range(CONV_WIDTH):
        c = c + conv_w[k] * up[:, k:k + s]
    a, val = jnp.split(c, 2, axis=-1)
    return (jax.nn.gelu(a, approximate=True) * val) @ w_down

def hybrid_layer(x, positions, attn_pre_gain, attn_post_gain, ffn_pre_gain, ffn_post_gain,
                 w_in, attn_sinks, cmp_pos_emb, cmp_w1, cmp_b1, cmp_w2,
                 w_branch_a, w_branch_b, w_out, ffn_w_up, ffn_conv_w, ffn_conv_b, ffn_w_down):
    b, s, _ = x.shape
    hd = HEAD_DIM
    h = rms_norm(x, attn_pre_gain)
    u = h @ w_in
    offsets = np.cumsum(np.array(IN_SIZES))[:-1].tolist()
    (qa, ka, va, qb, kcb, vcb, ksb, vsb, kwb, vwb, g_nsa, g_a, g_b) = jnp.split(u, offsets, axis=-1)
    ra = A_Q_HEADS // A_KV_HEADS
    qa = apply_rope(qa.reshape(b, s, A_Q_HEADS, hd), positions).reshape(b, s, A_KV_HEADS, ra, hd)
    ka = apply_rope(ka.reshape(b, s, A_KV_HEADS, hd), positions)
    va = va.reshape(b, s, A_KV_HEADS, hd)
    o_a = swa_sink_attention(qa, ka, va, attn_sinks)
    rb = B_Q_HEADS // B_KV_HEADS
    qb = qb.reshape(b, s, B_Q_HEADS, hd)
    qb_rot = apply_rope(qb, positions).reshape(b, s, B_KV_HEADS, rb, hd)
    qb_raw = qb.reshape(b, s, B_KV_HEADS, rb, hd)
    kc = compress(kcb.reshape(b, s, B_KV_HEADS, hd), cmp_pos_emb[0], cmp_w1[0], cmp_b1[0], cmp_w2[0])
    vc = compress(vcb.reshape(b, s, B_KV_HEADS, hd), cmp_pos_emb[1], cmp_w1[1], cmp_b1[1], cmp_w2[1])
    ks = apply_rope(ksb.reshape(b, s, B_KV_HEADS, hd), positions)
    kw = apply_rope(kwb.reshape(b, s, B_KV_HEADS, hd), positions)
    vs = vsb.reshape(b, s, B_KV_HEADS, hd)
    vw = vwb.reshape(b, s, B_KV_HEADS, hd)
    gates = jax.nn.sigmoid(g_nsa).reshape(b, s, B_KV_HEADS, rb, 3)
    o_b = nsa_attention(qb_raw, qb_rot, kc, vc, ks, vs, kw, vw, gates)
    mixed = jax.nn.sigmoid(g_a) * (o_a @ w_branch_a) + jax.nn.sigmoid(g_b) * (o_b @ w_branch_b)
    x = x + rms_norm(mixed @ w_out, attn_post_gain)
    h = rms_norm(x, ffn_pre_gain)
    x = x + rms_norm(conv_ffn(h, ffn_w_up, ffn_conv_w, ffn_conv_b, ffn_w_down), ffn_post_gain)
    return x

def first_inputs(seed: int = 0) -> dict:
    key = jax.random.key(seed)
    ks = jax.random.split(key, 20)
    f32 = jnp.float32

    def nrm(k, shape, scale):
        return scale * jax.random.normal(k, shape, f32)

    x = nrm(ks[0], (BATCH, SEQ, D_MODEL), 1.0)
    positions = jnp.broadcast_to(jnp.arange(SEQ, dtype=jnp.int32)[None, :], (BATCH, SEQ))
    return {
        'x': x,
        'positions': positions,
        'attn_pre_gain': 1.0 + nrm(ks[1], (DEPTH, D_MODEL), 0.05),
        'attn_post_gain': 1.0 + nrm(ks[2], (DEPTH, D_MODEL), 0.05),
        'ffn_pre_gain': 1.0 + nrm(ks[3], (DEPTH, D_MODEL), 0.05),
        'ffn_post_gain': 1.0 + nrm(ks[4], (DEPTH, D_MODEL), 0.05),
        'w_in': nrm(ks[5], (DEPTH, D_MODEL, IN_COLS), D_MODEL ** -0.5),
        'attn_sinks': nrm(ks[6], (DEPTH, A_Q_HEADS), 1.0),
        'cmp_pos_emb': nrm(ks[7], (DEPTH, 2, CMP_LEN, HEAD_DIM), 0.1),
        'cmp_w1': nrm(ks[8], (DEPTH, 2, CMP_LEN * HEAD_DIM, CMP_HIDDEN), (CMP_LEN * HEAD_DIM) ** -0.5),
        'cmp_b1': nrm(ks[9], (DEPTH, 2, CMP_HIDDEN), 0.01),
        'cmp_w2': nrm(ks[10], (DEPTH, 2, CMP_HIDDEN, HEAD_DIM), CMP_HIDDEN ** -0.5),
        'w_branch_a': nrm(ks[11], (DEPTH, A_WIDTH, D_MODEL), A_WIDTH ** -0.5),
        'w_branch_b': nrm(ks[12], (DEPTH, B_WIDTH, D_MODEL), B_WIDTH ** -0.5),
        'w_out': nrm(ks[13], (DEPTH, D_MODEL, D_MODEL), D_MODEL ** -0.5),
        'ffn_w_up': nrm(ks[14], (DEPTH, D_MODEL, 2 * D_FF), D_MODEL ** -0.5),
        'ffn_conv_w': nrm(ks[15], (DEPTH, CONV_WIDTH, 2 * D_FF), CONV_WIDTH ** -0.5),
        'ffn_conv_b': nrm(ks[16], (DEPTH, 2 * D_FF), 0.01),
        'ffn_w_down': nrm(ks[17], (DEPTH, D_FF, D_MODEL), D_FF ** -0.5),
    }

def first_block(x, positions, attn_pre_gain, attn_post_gain, ffn_pre_gain, ffn_post_gain,
              w_in, attn_sinks, cmp_pos_emb, cmp_w1, cmp_b1, cmp_w2,
              w_branch_a, w_branch_b, w_out, ffn_w_up, ffn_conv_w, ffn_conv_b, ffn_w_down):
    for l in range(DEPTH):
        x = hybrid_layer(x, positions, attn_pre_gain[l], attn_post_gain[l], ffn_pre_gain[l],
                         ffn_post_gain[l], w_in[l], attn_sinks[l], cmp_pos_emb[l], cmp_w1[l],
                         cmp_b1[l], cmp_w2[l], w_branch_a[l], w_branch_b[l], w_out[l],
                         ffn_w_up[l], ffn_conv_w[l], ffn_conv_b[l], ffn_w_down[l])
    return x


N_A_LAYERS = DEPTH // 2
N_B_LAYERS = DEPTH - N_A_LAYERS

DN_HEADS = 8
DN_HEAD_DIM = D_MODEL // DN_HEADS
DN_WIDTH = DN_HEADS * DN_HEAD_DIM
CONV_K = 4
DN_CHUNK = 64

DA_HEADS = 8
DA_HEAD_DIM = D_MODEL // (2 * DA_HEADS)
DA_V_DIM = 2 * DA_HEAD_DIM
DA_QK_WIDTH = 2 * DA_HEADS * DA_HEAD_DIM
DA_WIDTH = DA_HEADS * DA_V_DIM
Q_BLOCK = 128

N_GROUPS = 4
EXPERTS_PER_GROUP = 8
N_EXPERTS = N_GROUPS * EXPERTS_PER_GROUP
TOP_K = 2
EXPERT_FF = D_MODEL // 2
MOE_BLOCK = 128

ALPHA = (2 * DEPTH) ** 0.25
BETA_INIT = (8 * DEPTH) ** -0.25
LN_EPS = 1e-5
RMS_EPS = 1e-6


def layer_norm(x, g, b):
    xf = x.astype(jnp.float32)
    mu = jnp.mean(xf, axis=-1, keepdims=True)
    var = jnp.mean(jnp.square(xf - mu), axis=-1, keepdims=True)
    return ((xf - mu) * lax.rsqrt(var + LN_EPS) * g + b).astype(x.dtype)

def rms_norm_2(x, w):
    xf = x.astype(jnp.float32)
    return xf * lax.rsqrt(jnp.mean(jnp.square(xf), axis=-1, keepdims=True) + RMS_EPS) * w.astype(jnp.float32)

def l2_normalize(x):
    xf = x.astype(jnp.float32)
    return xf * lax.rsqrt(jnp.sum(jnp.square(xf), axis=-1, keepdims=True) + RMS_EPS)

def causal_depthwise_conv(x, w):
    k_width, t = w.shape[0], x.shape[1]
    xp = jnp.pad(x, ((0, 0), (k_width - 1, 0), (0, 0)))
    y = xp[:, 0:t] * w[0]
    for j in range(1, k_width):
        y = y + xp[:, j:j + t] * w[j]
    return y

def chunked_gated_delta_rule(q, k, v, g, beta):
    b, t, h, dk = q.shape
    dv = v.shape[-1]
    n, c = t // DN_CHUNK, DN_CHUNK

    def to_chunks(a):
        return jnp.moveaxis(a.reshape((b, n, c, h) + a.shape[3:]), 3, 1)

    q = to_chunks(q * dk ** -0.5)
    k = to_chunks(k)
    v = to_chunks(v.astype(jnp.float32))
    gc = jnp.cumsum(to_chunks(g), axis=-1)
    beta = to_chunks(beta)
    idx = jnp.arange(c)
    causal = idx[:, None] >= idx[None, :]
    strict = idx[:, None] > idx[None, :]
    decay = jnp.exp(jnp.where(causal, gc[..., :, None] - gc[..., None, :], -jnp.inf))
    k_beta = k * beta[..., None]
    a_mat = jnp.where(strict, jnp.einsum('bhnid,bhnjd->bhnij', k_beta, k) * decay, 0.0)
    rhs = jnp.concatenate([v * beta[..., None], k_beta * jnp.exp(gc)[..., None]], axis=-1)
    sol = lax.linalg.triangular_solve(a_mat + jnp.eye(c, dtype=jnp.float32), rhs,
                                      left_side=True, lower=True, unit_diagonal=True)
    u, w = sol[..., :dv], sol[..., dv:]
    attn = jnp.where(causal, jnp.einsum('bhnid,bhnjd->bhnij', q, k) * decay, 0.0)
    q_dec = q * jnp.exp(gc)[..., None]
    k_dec = k * jnp.exp(gc[..., -1:] - gc)[..., None]
    g_last = jnp.exp(gc[..., -1])

    def step(state, xs):
        u_i, w_i, q_i, k_i, attn_i, gl_i = xs
        v_new = u_i - jnp.einsum('bhcd,bhdv->bhcv', w_i, state)
        o_i = jnp.einsum('bhcd,bhdv->bhcv', q_i, state) + jnp.einsum('bhij,bhjv->bhiv', attn_i, v_new)
        state = state * gl_i[..., None, None] + jnp.einsum('bhcd,bhcv->bhdv', k_i, v_new)
        return state, o_i

    xs = tuple(jnp.moveaxis(a, 2, 0) for a in (u, w, q_dec, k_dec, attn, g_last))
    state0 = jnp.zeros((b, h, dk, dv), jnp.float32)
    _, o = lax.scan(step, state0, xs)
    return o.transpose(1, 0, 3, 2, 4).reshape(b, t, h, dv)

def gated_deltanet(x, w_in, conv_w, a_log, dt_bias, norm_w, w_out):
    b, t, _ = x.shape
    proj = x @ w_in
    qkv = jax.nn.silu(causal_depthwise_conv(proj[..., :3 * DN_WIDTH], conv_w))
    qkv = qkv.reshape(b, t, 3, DN_HEADS, DN_HEAD_DIM)
    q = l2_normalize(qkv[:, :, 0])
    k = l2_normalize(qkv[:, :, 1])
    v = qkv[:, :, 2]
    z = proj[..., 3 * DN_WIDTH:4 * DN_WIDTH].reshape(b, t, DN_HEADS, DN_HEAD_DIM)
    beta = jax.nn.sigmoid(proj[..., 4 * DN_WIDTH:4 * DN_WIDTH + DN_HEADS].astype(jnp.float32))
    alpha_logit = proj[..., 4 * DN_WIDTH + DN_HEADS:].astype(jnp.float32)
    g = -jnp.exp(a_log.astype(jnp.float32)) * jax.nn.softplus(alpha_logit + dt_bias.astype(jnp.float32))
    o = chunked_gated_delta_rule(q, k, v, g, beta)
    o = rms_norm_2(o, norm_w) * jax.nn.silu(z.astype(jnp.float32))
    return o.reshape(b, t, DN_WIDTH).astype(x.dtype) @ w_out

def shared_kv(x, kv_w):
    b, t, _ = x.shape
    kv = x @ kv_w
    keys = kv[..., :DA_QK_WIDTH].reshape(b, t, DA_HEADS, 2, DA_HEAD_DIM).transpose(3, 0, 2, 1, 4)
    vals = kv[..., DA_QK_WIDTH:].reshape(b, t, DA_HEADS, DA_V_DIM).transpose(0, 2, 1, 3)
    return keys, vals

def differential_attention(x, keys, vals, w_q, lam_p, subln_w, w_out, lam_init):
    b, t, _ = x.shape
    nb = t // Q_BLOCK
    q = (x @ w_q).reshape(b, nb, Q_BLOCK, DA_HEADS, 2, DA_HEAD_DIM).transpose(1, 4, 0, 3, 2, 5)
    lp = lam_p.astype(jnp.float32)
    lam = jnp.exp(jnp.sum(lp[0] * lp[1])) - jnp.exp(jnp.sum(lp[2] * lp[3])) + lam_init
    key_pos = jnp.arange(t)
    scale = DA_HEAD_DIM ** -0.5

    def block(args):
        q_blk, blk = args
        query_pos = blk * Q_BLOCK + jnp.arange(Q_BLOCK)
        mask = key_pos[None, :] <= query_pos[:, None]
        s = jnp.einsum('sbhqd,sbhkd->sbhqk', q_blk, keys).astype(jnp.float32) * scale
        p = jax.nn.softmax(jnp.where(mask, s, -jnp.inf), axis=-1)
        a = p[0] - lam * p[1]
        return jnp.einsum('bhqk,bhkv->bhqv', a.astype(vals.dtype), vals)

    o = lax.map(block, (q, jnp.arange(nb)))
    o = o.transpose(1, 0, 3, 2, 4).reshape(b, t, DA_HEADS, DA_V_DIM)
    o = rms_norm_2(o, subln_w) * (1.0 - lam_init)
    return o.reshape(b, t, DA_WIDTH).astype(x.dtype) @ w_out

def hierarchical_moe(x, w_group, w_expert, w13, w2):
    b, t, d = x.shape
    n = b * t
    m = n * TOP_K
    xf = x.reshape(n, d)
    group_prob = jax.nn.softmax((xf @ w_group).astype(jnp.float32), axis=-1)
    p_group, group_idx = lax.top_k(group_prob, 1)
    expert_logits = (xf @ w_expert).astype(jnp.float32).reshape(n, N_GROUPS, EXPERTS_PER_GROUP)
    in_group = expert_logits[jnp.arange(n), group_idx[:, 0]]
    top_p, top_i = lax.top_k(jax.nn.softmax(in_group, axis=-1), TOP_K)
    gate = (p_group * top_p / jnp.sum(top_p, axis=-1, keepdims=True)).reshape(m)
    expert_id = (group_idx * EXPERTS_PER_GROUP + top_i).reshape(m)
    token_id = jnp.repeat(jnp.arange(n), TOP_K)
    order = jnp.argsort(expert_id)
    eid_s, tok_s, gate_s = expert_id[order], token_id[order], gate[order]
    counts = jnp.bincount(expert_id, length=N_EXPERTS)
    start = jnp.cumsum(counts) - counts
    padded = (counts + MOE_BLOCK - 1) // MOE_BLOCK * MOE_BLOCK
    pad_end = jnp.cumsum(padded)
    pad_start = pad_end - padded
    dest = pad_start[eid_s] + jnp.arange(m) - start[eid_s]
    n_rows = (m + N_EXPERTS * (MOE_BLOCK - 1) + MOE_BLOCK - 1) // MOE_BLOCK * MOE_BLOCK
    n_blocks = n_rows // MOE_BLOCK
    row_tok = jnp.zeros((n_rows,), jnp.int32).at[dest].set(tok_s)
    row_gate = jnp.zeros((n_rows,), x.dtype).at[dest].set(gate_s.astype(x.dtype))
    block_eid = jnp.minimum(jnp.searchsorted(pad_end, jnp.arange(n_blocks) * MOE_BLOCK, side='right'),
                            N_EXPERTS - 1)
    x_rows = xf[row_tok].reshape(n_blocks, MOE_BLOCK, d)

    def expert_block(args):
        xb, e = args
        hcat = xb @ w13[e]
        hid = jax.nn.silu(hcat[:, :EXPERT_FF]) * hcat[:, EXPERT_FF:]
        return hid @ w2[e]

    y_rows = lax.map(expert_block, (x_rows, block_eid)).reshape(n_rows, d)
    y = jax.ops.segment_sum(y_rows * row_gate[:, None], row_tok, num_segments=n)
    return y.reshape(b, t, d)

def lambda_init(layer_idx):
    return 0.8 - 0.6 * math.exp(-0.3 * layer_idx)

def second_inputs(seed: int = 0) -> dict:
    key = jax.random.key(seed)
    ks = jax.random.split(key, 24)
    f32 = jnp.float32
    D = D_MODEL

    def nrm(k, shape, scale):
        return jax.random.normal(k, shape, f32) * scale

    in_a = 4 * DN_WIDTH + 2 * DN_HEADS
    x = nrm(ks[0], (BATCH, SEQ, D), 1.0)
    a_w_in = nrm(ks[1], (N_A_LAYERS, D, in_a), D ** -0.5)
    a_conv_w = nrm(ks[2], (N_A_LAYERS, CONV_K, 3 * DN_WIDTH), CONV_K ** -0.5)
    a_a_log = jnp.log(jax.random.uniform(ks[3], (N_A_LAYERS, DN_HEADS), f32, 1.0, 16.0))
    dt = jnp.exp(jax.random.uniform(ks[4], (N_A_LAYERS, DN_HEADS), f32, math.log(1e-3), math.log(1e-1)))
    a_dt_bias = dt + jnp.log(-jnp.expm1(-dt))
    a_norm_w = 1.0 + nrm(ks[5], (N_A_LAYERS, DN_HEAD_DIM), 0.02)
    a_w_out = nrm(ks[6], (N_A_LAYERS, DN_WIDTH, D), DN_WIDTH ** -0.5 * BETA_INIT)
    kv_w = nrm(ks[7], (D, DA_QK_WIDTH + DA_WIDTH), D ** -0.5)
    b_w_q = nrm(ks[8], (N_B_LAYERS, D, DA_QK_WIDTH), D ** -0.5)
    b_lambda = nrm(ks[9], (N_B_LAYERS, 4, DA_HEAD_DIM), 0.1)
    b_subln_w = 1.0 + nrm(ks[10], (N_B_LAYERS, DA_V_DIM), 0.02)
    b_w_out = nrm(ks[11], (N_B_LAYERS, DA_WIDTH, D), DA_WIDTH ** -0.5 * BETA_INIT)
    ln_mix_g = 1.0 + nrm(ks[12], (DEPTH, D), 0.02)
    ln_mix_b = nrm(ks[13], (DEPTH, D), 0.02)
    ln_ffn_g = 1.0 + nrm(ks[14], (DEPTH, D), 0.02)
    ln_ffn_b = nrm(ks[15], (DEPTH, D), 0.02)
    moe_w_group = nrm(ks[16], (DEPTH, D, N_GROUPS), D ** -0.5)
    moe_w_expert = nrm(ks[17], (DEPTH, D, N_EXPERTS), D ** -0.5)
    moe_w13 = nrm(ks[18], (DEPTH, N_EXPERTS, D, 2 * EXPERT_FF), D ** -0.5)
    moe_w2 = nrm(ks[19], (DEPTH, N_EXPERTS, EXPERT_FF, D), EXPERT_FF ** -0.5 * BETA_INIT)
    return {'x': x, 'a_w_in': a_w_in, 'a_conv_w': a_conv_w, 'a_a_log': a_a_log, 'a_dt_bias': a_dt_bias,
            'a_norm_w': a_norm_w, 'a_w_out': a_w_out, 'kv_w': kv_w, 'b_w_q': b_w_q, 'b_lambda': b_lambda,
            'b_subln_w': b_subln_w, 'b_w_out': b_w_out, 'ln_mix_g': ln_mix_g, 'ln_mix_b': ln_mix_b,
            'ln_ffn_g': ln_ffn_g, 'ln_ffn_b': ln_ffn_b, 'moe_w_group': moe_w_group,
            'moe_w_expert': moe_w_expert, 'moe_w13': moe_w13, 'moe_w2': moe_w2}

def second_block(x, a_w_in, a_conv_w, a_a_log, a_dt_bias, a_norm_w, a_w_out, kv_w, b_w_q, b_lambda,
              b_subln_w, b_w_out, ln_mix_g, ln_mix_b, ln_ffn_g, ln_ffn_b, moe_w_group, moe_w_expert,
              moe_w13, moe_w2):
    h = x
    keys, vals = None, None
    for layer in range(DEPTH):
        if layer < N_A_LAYERS:
            mix = gated_deltanet(h, a_w_in[layer], a_conv_w[layer], a_a_log[layer], a_dt_bias[layer],
                                 a_norm_w[layer], a_w_out[layer])
        else:
            j = layer - N_A_LAYERS
            if j == 0:
                keys, vals = shared_kv(h, kv_w)
            mix = differential_attention(h, keys, vals, b_w_q[j], b_lambda[j], b_subln_w[j], b_w_out[j],
                                         lambda_init(layer))
        h = layer_norm(ALPHA * h + mix, ln_mix_g[layer], ln_mix_b[layer])
        ffn = hierarchical_moe(h, moe_w_group[layer], moe_w_expert[layer], moe_w13[layer], moe_w2[layer])
        h = layer_norm(ALPHA * h + ffn, ln_ffn_g[layer], ln_ffn_b[layer])
    return h


def setup_inputs(seed=0):
    out = dict(first_inputs(seed))
    for name, value in second_inputs(seed + 1).items():
        if name != "x":
            out[name + "_2"] = value
    return out


def reference(
    x, positions, attn_pre_gain, attn_post_gain, ffn_pre_gain, ffn_post_gain, w_in, attn_sinks,
    cmp_pos_emb, cmp_w1, cmp_b1, cmp_w2, w_branch_a, w_branch_b, w_out, ffn_w_up, ffn_conv_w,
    ffn_conv_b, ffn_w_down, a_w_in_2, a_conv_w_2, a_a_log_2, a_dt_bias_2, a_norm_w_2, a_w_out_2,
    kv_w_2, b_w_q_2, b_lambda_2, b_subln_w_2, b_w_out_2, ln_mix_g_2, ln_mix_b_2, ln_ffn_g_2,
    ln_ffn_b_2, moe_w_group_2, moe_w_expert_2, moe_w13_2, moe_w2_2,
):
    x = first_block(
        x, positions, attn_pre_gain, attn_post_gain, ffn_pre_gain, ffn_post_gain, w_in,
        attn_sinks, cmp_pos_emb, cmp_w1, cmp_b1, cmp_w2, w_branch_a, w_branch_b, w_out,
        ffn_w_up, ffn_conv_w, ffn_conv_b, ffn_w_down,
    )
    return second_block(
        x, a_w_in_2, a_conv_w_2, a_a_log_2, a_dt_bias_2, a_norm_w_2, a_w_out_2, kv_w_2, b_w_q_2,
        b_lambda_2, b_subln_w_2, b_w_out_2, ln_mix_g_2, ln_mix_b_2, ln_ffn_g_2, ln_ffn_b_2,
        moe_w_group_2, moe_w_expert_2, moe_w13_2, moe_w2_2,
    )


_drawn_inputs = setup_inputs


def setup_inputs(seed=0):
    import zlib

    import numpy as np

    out = dict(_drawn_inputs(seed))
    spreads = {}
    factors = {'cmp_b1': 3.075,
     'ffn_conv_b': 3.242,
     'a_norm_w_2': 6.255,
     'b_lambda_2': 7.12,
     'b_subln_w_2': 6.424}
    for name, (base, spread) in spreads.items():
        noise = np.random.default_rng([zlib.crc32(name.encode()), seed]).standard_normal(out[name].shape)
        drawn = base * np.exp(spread * noise) if base else spread * noise
        out[name] = __import__('jax').numpy.asarray(drawn.astype(out[name].dtype))
    for name, factor in factors.items():
        out[name] = (out[name] * factor).astype(out[name].dtype)
    return out
```

```python
from contextlib import ExitStack, contextmanager
import math

import numpy as np
import concourse.bass as bass
from concourse import mybir

F32 = mybir.dt.float32
I32 = mybir.dt.int32
U32 = mybir.dt.uint32
ALU = mybir.AluOpType
ACT = mybir.ActivationFunctionType
AX = mybir.AxisListType.X

P = 128
T = 512
NT = T // P
D = 1024
KD = D // P
LAYERS = 2
HD = 64
R = 8
FF = 2816
PAIRS = FF // P
NC = 31
BIG = 1e30
TINY = 1e-30
EPS = 1e-6
LN_EPS = 1e-5
ALPHA = (2 * LAYERS) ** 0.25
SCALE = HD ** -0.5

QA, KA, QB, KS, KW, KC, VC, NFM = 0, 4, 5, 9, 10, 11, 12, 13
VA_C, VS_C, VW_C, GATE_C, TM_COLS = 0, 128, 256, 384, 408
S_LAYER = [16, 13, 4, 8, 8, 8, 2 * PAIRS, 2 * (PAIRS // 2)]
LAYER_SLOTS = -(-sum(S_LAYER) // R) * R
LAYER_PAD = LAYER_SLOTS - sum(S_LAYER)

DH = 8
CH = 128
NG, EPG, NE = 4, 8, 32
JOBS = 48
ROUNDS_MAX = 20
EFF = 512

SM = {}
_o = 0
for _n, _w in (("gains", 32), ("sinks", 8), ("conv", 4 * 2 * PAIRS), ("b1", 2), ("pos", 64),
               ("w2k", 256), ("w2v", 256)):
    SM[_n] = (_o, _o + _w)
    _o += _w
SM_COLS = _o
S2 = {}
_o = 0
for _n, _w in (("ab", 8 * 16), ("conv", 24 * 4), ("alog", 8), ("dtb", 8), ("normw", 1), ("ln", 64),
               ("router", 2 * 8 * 36), ("lam", 4 * HD), ("subln", 1)):
    S2[_n] = (_o, _o + _w)
    _o += _w
S2_COLS = _o
CC = {}
_o = 0
for _n, _w in (("ident", 128), ("ones", 128), ("perm", 128), ("tri", 128), ("causal", 128),
               ("band", 128), ("cmp", 4 * NC), ("strictT", 128), ("levels", 7 * 128),
               ("invf", 1), ("eps", 1), ("lneps", 1), ("one", 1), ("iota8", 8), ("iota32", 32), ("jobs", 48)):
    CC[_n] = (_o, _o + _w)
    _o += _w
CC_COLS = _o


class Book:

    def __init__(self):
        self.marks, self.per, self.count = {}, {}, {}


class Sequence:

    def __init__(self, eng, settled, old, new, *channels):
        self.eng, self.settled, self.old, self.new = eng, settled, old, new
        self.n = {c: 0 for c in channels}
        self.chief, self.loops = channels[0], []
        self.passed, self.extra = [], {}

    def step(self, mark=None, ch=None, inc=1):
        ch = ch or self.chief
        self.n[ch] = self.n.get(ch, 0) + inc
        if mark:
            self.new.marks[mark] = {ch: (self.n[ch], [name for name, _ in self.loops], list(self.passed))}
        return inc

    def note(self, mark):
        self.new.marks[mark] = {ch: (n, [name for name, _ in self.loops], list(self.passed))
                                for ch, n in self.n.items() if not ch.startswith("dma")}

    def value(self, ch, n, loops, passed, back=None):
        active = dict(self.loops)
        total, moving = n, None
        for name in list(passed) + list(loops):
            per = self.old.per.get((ch, name), 0)
            if name == back:
                total -= per
            if not per:
                continue
            if name in active:
                more = active[name] * per
            elif name in self.extra:
                more = self.extra[name] * per
            else:
                total += (self.old.count.get(name, 1) - 1) * per
                continue
            moving = more if moving is None else moving + more
        assert total > 0, (ch, n)
        return total if moving is None else moving + total

    def at(self, mark, of=None, back=None, first=False):
        counts = self.old.marks.get(mark)
        if counts is None:
            return 1
        ch = of or next(iter(counts))
        n, loops, passed = counts[ch]
        return self.value(ch, n, [] if first else loops, passed, back)

    def so_far(self, ch=None):
        ch = ch or self.chief
        return self.value(ch, self.n[ch], [name for name, _ in self.loops], self.passed)

    @contextmanager
    def loop(self, name, count):
        start = dict(self.n)
        self.eng.sem_inc(self.settled, 1)
        with self.eng.Fori(0, count) as v:
            self.loops.append((name, v))
            yield v
            self.loops.pop()
        self.new.count[name] = count
        for ch, n in self.n.items():
            per = n - start.get(ch, 0)
            self.new.per[(ch, name)] = per
            self.n[ch] = start.get(ch, 0) + per * count

    def count_of(self, tile, low, high):
        self.eng.sem_inc(self.settled, 1)
        return self.eng.value_load(tile, min_val=low, max_val=high)

    @contextmanager
    def rounds(self, name, count):
        start = dict(self.n)
        self.eng.sem_inc(self.settled, 1)
        self.extra[name] = self.eng.snap(count - 1)
        with self.eng.Fori(0, count) as v:
            self.loops.append((name, v))
            yield v
            self.loops.pop()
        self.new.count[name] = 1
        for ch, n in self.n.items():
            self.new.per[(ch, name)] = n - start.get(ch, 0)
        self.passed.append(name)


def build(nc, ins, out, old, new):
    ctx = ExitStack()
    with ctx:
        def sb(name, shape, dt=F32):
            return ctx.enter_context(nc.sbuf_tensor(name, shape, dt))

        def semaphore(name):
            return ctx.enter_context(nc.semaphore(name))

        pe_done, act_done, dve_done, pool_done = (semaphore(n) for n in ("pe_done", "act_done", "dve_done", "pool_done"))
        slot_used = semaphore("slot_used")
        settled = semaphore("settled")
        const_in, positions_in, x_in, small_in, ids_in, result_out = (
            semaphore(n) for n in ("const_in", "positions_in", "x_in", "small_in", "ids_in", "result_out"))
        numbers_placed, table_read = semaphore("numbers_placed"), semaphore("table_read")
        table_filled, rows_gathered, rows_scattered, rows_written, rows_back = (
            [semaphore(f"{n}{i}") for i in range(2)]
            for n in ("table_filled", "rows_gathered", "rows_scattered", "rows_written", "rows_back"))
        slot_in = [semaphore(f"slot_in{r}") for r in range(R)]
        psum = ctx.enter_context(nc.psum_tensor("psum", [P, 8, 512], F32))

        const = sb("const", [P, CC_COLS])
        def cc(name):
            return const[:, CC[name][0]:CC[name][1]]
        ident, ones, perm = cc("ident"), cc("ones"), cc("perm")
        small = sb("small", [P, max(SM_COLS, S2_COLS)])
        ids = sb("ids", [P, 8], I32)
        scratch = sb("scratch", [P, 4, 8], I32)
        def s2(name):
            return small[:, S2[name][0]:S2[name][1]]
        def sm(name):
            return small[:, SM[name][0]:SM[name][1]]
        gains = sm("gains").rearrange("p (a k) -> p a k", a=4)
        sinks = sm("sinks").rearrange("p (j g) -> p j g", j=4)
        conv = sm("conv").rearrange("p (t c) -> p t c", c=4)

        ring = sb("ring", [P, R, D])
        x = sb("x", [P, KD, T])
        ARENA = 37710
        arena = sb("arena", [P, ARENA])
        used = [0]

        def take(*dims):
            n = int(np.prod(dims))
            used[0] += n
            assert used[0] <= ARENA, used[0]
            part = arena[:, used[0] - n:used[0]]
            if len(dims) > 1:
                letters = "abcd"[:len(dims)]
                part = part.rearrange(f"p ({' '.join(letters)}) -> p {' '.join(letters)}",
                                      **dict(zip(letters, dims)))
            return part

        big = take(29 * T)
        siga = big[:, 0:8 * T].rearrange("p (a t) -> p a t", t=T)
        sigb = big[:, 8 * T:16 * T].rearrange("p (a t) -> p a t", t=T)
        fm = big[:, 16 * T:29 * T].rearrange("p (a t) -> p a t", t=T)
        g_ff = big[:, 0:PAIRS * T].rearrange("p (a t) -> p a t", t=T)
        y = siga
        sq = sigb
        h = take(KD, T)
        pads = take(3, NT, 192)
        kpad = take(3, 2, T)
        U = take(4, T + 2)
        zeroed = arena[:, used[0] - 4 * (T + 2) - 3 * 2 * T - 3 * NT * 192:used[0]]
        kcp = take(2, NC)
        vcp = take(2, P)
        gate = take(NT, 24)
        oab = take(2, 4, T)
        blocks = oab.rearrange("p a b t -> p (a b t)")[:, 0:2 * NC * 32] \
            .rearrange("p (l g c) -> p l g c", l=32, g=2)
        cosT, sinT, rs = take(T), take(T), take(T)
        tmp = take(9, T)
        hid = take(2, 2 * NC)
        cols = take(4, 8)
        qs = tmp[:, 0:3]
        rot = tmp[:, 3]
        pbuf = tmp[:, 4:7]
        ptbuf = tmp[:, 7:9]
        gj = take(NT, 6)
        sj = take(2, 2)
        cj = take(8, 4)
        posi = tmp[:, 5].bitcast(I32)

        used[0] = 0
        qkvz = take(32 * T)
        sq2 = qkvz[:, 0:KD * T].rearrange("p (a t) -> p a t", t=T)
        zt = qkvz.rearrange("p (h c t) -> p h c t", c=4, t=T)
        U3 = take(4, T + 3)
        cdn = take(4, T)
        rs2 = take(T)
        bg = take(6, 32)
        cj_dn = take(6, 4)
        BETA, G, GC, EKD, EL, NBE = range(6)
        sc = take(6, 32)
        hb = [dict(zip(("qn", "kn", "qd", "dm", "at", "lt", "M", "X", "T1", "kd", "vb", "ta", "tb"),
                       [take(T) for _ in range(13)])) for _ in range(2)]
        for b_ in hb:
            b_["c"] = take(6, 4)
            b_["R"], b_["vn"], b_["S"] = take(P), take(P), take(P)
            b_["K"] = [b_["ta"], b_["tb"]]

        used[0] = 0
        sq3 = take(KD, T)
        kda = take(KD * T)
        vda = take(NT, D)
        qda = take(KD * T)
        oda = take(KD, T)
        da_t = take(12, T)
        qz = da_t[:, 0:4]
        pda = da_t[:, 4:10]
        ptd = da_t[:, 10:12]
        va_h = take(2, NT, P)
        rs3 = take(T)
        lam = take(160)
        dcols = take(4, 16)

        used[0] = 0
        sq4 = take(KD, T)
        htm = take(NT, D)
        rs4 = take(T)
        lg = take(NT, 36)
        rt = [take(NT, 32) for _ in range(6)]
        rc = take(24, NT)
        idx = take(JOBS)
        jobs = take(JOBS)
        jwork = take(JOBS, NE)
        dest = take(2, NT)
        gidx = take(2, 1)
        sidx = take(2, 1)
        rnd = take(4)
        xg = take(2, D)
        xT = take(2, KD, P)
        sg = take(2, EFF)
        hs = take(2, EFF)
        hT = take(2, 4, P)
        ym = take(2, D)
        y2 = take(2, 2, D)
        yt = take(NT, D)

        blk = ctx.enter_context(nc.Block())

        tab = {m: nc.dram_tensor(f"table_{m}", (P * JOBS, 1), I32, kind="Internal").ap() for m in ("m0", "m1")}
        hd = {m: nc.dram_tensor(f"rows_in_{m}", (2 * T, D), F32, kind="Internal").ap() for m in ("m0", "m1")}
        yd = {m: nc.dram_tensor(f"rows_out_{m}", (2 * T, D), F32, kind="Internal").ap() for m in ("m0", "m1")}
        wstream = ins["wstream"]

        def units():
            found = []
            for qt in range(NT):
                for g in range(2):
                    found.append(("A", g, qt, [k for k in (qt - 1, qt) if k >= 0]))
                for kind in ("cmp", "slc", "win"):
                    for g in range(2):
                        found.append((kind, g, qt, list(range(qt + 1))))
            return found

        UNITS = units()
        NU = len(UNITS)

        def width(u):
            kind, g, qt, kts = UNITS[u]
            return NC if kind == "cmp" else P * len(kts)

        @blk.sync
        def _(sp):
            seq = Sequence(sp, settled, old, new, "dma_const", "dma_pos", "dma_x", "dma_out", "dma_small")
            sp.dma_start(const[:], ins["const"]).then_inc(const_in, seq.step("const", inc=16))
            sp.dma_start(posi, ins["positions"]).then_inc(positions_in, seq.step("posi", ch="dma_pos", inc=16))
            sp.dma_start(small[:, 0:SM_COLS], ins["small"][0]).then_inc(small_in, seq.step(ch="dma_small", inc=16))
            new.marks["small"] = {"dma_small": (16, ["layer"], [])}
            new.per[("dma_small", "layer")] = 16
            sp.dma_start(x[:], ins["xT"]).then_inc(x_in, seq.step("x0", ch="dma_x", inc=16))
            for r in range(R):
                sp.dma_start(ring[:, r, :], wstream[r]).then_inc(slot_in[r], 16)
            sp.dma_start(ids[:], ins["ids"]).then_inc(ids_in, seq.step("ids", ch="dma_ids", inc=16))
            for i, m in enumerate(("m0", "m1")):
                sp.dma_start(tab[m].rearrange("(p n) o -> p (n o)", p=P), ins["oob"]) \
                    .then_inc(table_filled[i], seq.step(f"{m}.table", ch=f"dma_tab{i}", inc=16))
            per_layer = LAYER_SLOTS // R
            w13 = ins["moe_w13"].rearrange("(n p) c -> n p c", p=P)
            w2 = ins["moe_w2"].rearrange("(n p) c -> n p c", p=P)
            more = []

            def used(turn, r):
                value = turn * R + (r + 1)
                for v in more:
                    value = v + value
                sp.wait_ge(slot_used, value)

            def fill(i0, i1):
                with sp.Fori(i0, i1) as i:
                    for r in range(R):
                        used(i + shift, r)
                        sp.dma_start(ring[:, r, :], wstream[bass.ds(i * R + r, 1)]
                                     .rearrange("o p n -> (o p) n")).then_inc(slot_in[r], 16)

            def fill_experts(m, turn):
                sp.wait_ge(dve_done, seq.at(f"m{m}.rnd"))
                rounds = seq.count_of(rnd[0:1, 0:1].bitcast(I32), 1, ROUNDS_MAX)
                with sp.Fori(0, rounds) as i:
                    n = 0
                    for ee in range(2):
                        expert = sp.value_load(jobs[0:1, bass.ds(i * 2 + ee, 1)].bitcast(I32), min_val=0, max_val=NE - 1)
                        for k in range(12):
                            used(i * 3 + turn + n // R, n % R)
                            if k < 8:
                                src = w13[bass.ds(expert * 8 + (m * NE * 8 + k), 1)]
                            else:
                                src = w2[bass.ds(expert * 4 + (m * NE * 4 + k - 8), 1)]
                            sp.dma_start(ring[:, n % R, :], src.rearrange("o p n -> (o p) n")) \
                                .then_inc(slot_in[n % R], 16)
                            n += 1
                return rounds

            shift = 0
            fill(1, per_layer + 1)
            sp.wait_ge(pe_done, seq.at("layer_end.begin.pe", first=True))
            sp.wait_ge(slot_used, seq.at("layer_end.begin.pe", first=True, of="slot"))
            sp.wait_ge(act_done, seq.at("layer_end.begin.act", first=True))
            sp.wait_ge(dve_done, seq.at("layer_end.begin.dve", first=True))
            sp.dma_start(small[:, 0:SM_COLS], ins["small"][1]).then_inc(small_in, seq.step(ch="dma_small", inc=16))
            fill(per_layer + 1, 2 * per_layer)
            sp.wait_ge(pe_done, seq.at("layer_end.begin.pe"))
            sp.wait_ge(slot_used, seq.at("layer_end.begin.pe", of="slot"))
            sp.wait_ge(act_done, seq.at("layer_end.begin.act"))
            sp.wait_ge(dve_done, seq.at("layer_end.begin.dve"))
            sp.dma_start(small[:, 0:S2_COLS], ins["small2"]) \
                .then_inc(small_in, seq.step("small2", ch="dma_small", inc=16))
            turns_pair = 2 * 12 // R
            at_stream = 2 * per_layer
            for m, before in ((0, 40 // R), (1, 32 // R)):
                fill(at_stream, at_stream + before)
                at_stream += before
                turn = at_stream + shift
                rounds = fill_experts(m, turn)
                seq.extra[f"m{m}.ex"] = sp.snap(rounds - 1)
                more.append(sp.snap((rounds - 1) * (turns_pair * R)))
                shift += turns_pair
            sp.wait_ge(dve_done, seq.at("result"))
            sp.dma_start(out, x[:]).then_inc(result_out, seq.step(ch="dma_out", inc=16))
            sp.wait_ge(result_out, seq.so_far("dma_out"))

        @blk.gpsimd
        def _(pool):
            seq = Sequence(pool, settled, old, new, "pool", "dma_t", "dma_i", "dma_g0", "dma_g1", "dma_y0", "dma_y1")
            pool.sem_inc(pool_done, seq.step(inc=16))
            for i in range(2):
                pool.dma_start(scratch[:, i, :], ins["ids"]).then_inc(rows_gathered[i], seq.step(ch=f"dma_g{i}", inc=16))
                pool.dma_start(scratch[:, 2 + i, :], ins["ids"]) \
                    .then_inc(rows_scattered[i], seq.step(ch=f"dma_y{i}", inc=16))
            pool.memset(zeroed, 0.0).then_inc(pool_done, seq.step())
            seq.note("zeroed")

            def at(table):
                return bass.IndirectOffsetOnAxis(ap=table, axis=0)

            for m in ("m0", "m1"):
                pool.wait_ge(dve_done, seq.at(f"{m}.dest"))
                pool.wait_ge(ids_in, seq.at("ids"))
                pool.wait_ge(table_filled[int(m[1])], seq.at(f"{m}.table"))
                pool.sem_inc(settled, 1)
                for c in range(2):
                    for t in range(NT):
                        pool.indirect_dma_start(out=tab[m], out_offset=at(dest[:, c, t:t + 1].bitcast(U32)),
                                                     in_=ids[:, c * NT + t:c * NT + t + 1], in_offset=None) \
                            .then_inc(numbers_placed, seq.step(ch="dma_t", inc=16))
                pool.wait_ge(numbers_placed, seq.so_far("dma_t"))
                pool.memset(xg, 0.0).then_inc(pool_done, seq.step())
                pool.dma_start(idx.bitcast(I32), tab[m].rearrange("(p n) o -> p (n o)", p=P)) \
                    .then_inc(table_read, seq.step(ch="dma_i", inc=16))
                pool.wait_ge(table_read, seq.so_far("dma_i"))
                pool.wait_ge(pool_done, seq.so_far())
                pool.wait_ge(rows_written[0], seq.at(f"{m}.hd0"))
                pool.wait_ge(rows_written[1], seq.at(f"{m}.hd1"))
                pool.wait_ge(dve_done, seq.at(f"{m}.rnd"))
                pool.wait_ge(pe_done, seq.at(f"{m}.ex.begin.pe"))
                pool.wait_ge(slot_used, seq.at(f"{m}.ex.begin.pe", of="slot"))
                pool.wait_ge(act_done, seq.at(f"{m}.ex.begin.act"))
                pool.wait_ge(dve_done, seq.at(f"{m}.ex.begin.dve"))
                rounds = seq.count_of(rnd[0:1, 0:1].bitcast(I32), 1, ROUNDS_MAX)
                L = f"{m}.ex"

                def number(dst, job):
                    pool.sem_inc(settled, 1)
                    pool.tensor_copy(dst.bitcast(I32), idx[:, bass.ds(job, 1)].bitcast(I32)) \
                        .then_inc(pool_done, seq.step())
                    pool.wait_ge(pool_done, seq.so_far())
                    pool.sem_inc(settled, 1)

                def gather(ee, mark):
                    pool.indirect_dma_start(out=xg[:, ee, :], out_offset=None, in_=hd[m],
                                                 in_offset=at(gidx[:, ee, :].bitcast(U32)),
                                                 bounds_check=2 * T - 1, oob_is_err=False) \
                        .then_inc(rows_gathered[ee], seq.step(f"{m}.{mark}", ch=f"dma_g{ee}", inc=16))

                for ee in range(2):
                    number(gidx[:, ee, :], ee)
                    gather(ee, f"Gpre{ee}")
                with seq.rounds(L, rounds) as i:
                    for ee in range(2):
                        if ee:
                            pool.wait_ge(pe_done, seq.at(f"{m}.T1"))
                        else:
                            pool.wait_ge(pe_done, seq.at(f"{m}.Tpre"))
                            pool.wait_ge(pe_done, seq.at(f"{m}.T0n", back=L))
                        pool.wait_ge(rows_gathered[ee], seq.so_far(f"dma_g{ee}"))
                        number(gidx[:, ee, :], i * 2 + (ee + 2))
                        gather(ee, f"G{ee}")
                        pool.wait_ge(rows_scattered[ee], seq.so_far(f"dma_y{ee}"))
                        number(sidx[:, ee, :], i * 2 + ee)
                        pool.wait_ge(act_done, seq.at(f"{m}.ya{ee}"))
                        pool.wait_ge(dve_done, seq.at(f"{m}.yd{ee}"))
                        pool.sem_inc(settled, 1)
                        pool.indirect_dma_start(out=yd[m], out_offset=at(sidx[:, ee, :].bitcast(U32)),
                                                     in_=ym[:, ee, :], in_offset=None,
                                                     bounds_check=2 * T - 1, oob_is_err=False) \
                            .then_inc(rows_scattered[ee], seq.step(f"{m}.sc{ee}", ch=f"dma_y{ee}", inc=16))
                for ee in range(2):
                    pool.wait_ge(rows_gathered[ee], seq.so_far(f"dma_g{ee}"))
                    pool.wait_ge(rows_scattered[ee], seq.so_far(f"dma_y{ee}"))

        @blk.tensor
        def _(pe):
            seq = Sequence(pe, settled, old, new, "pe", "slot")
            pe.sem_inc(pe_done, seq.step(inc=64))
            pe.sem_inc(slot_used, seq.step(ch="slot", inc=R))

            def meet(stage):
                seq.note(f"{stage}.begin.pe")
                pe.wait_ge(act_done, seq.at(f"{stage}.begin.act"))
                pe.wait_ge(dve_done, seq.at(f"{stage}.begin.dve"))

            def slot():
                n, r = seq.n["slot"], seq.n["slot"] % R
                value, moving = 16 * (n // R), None
                for name, v in seq.loops + [(name, seq.extra[name]) for name in seq.passed]:
                    per = old.per.get(("slot", name), 0)
                    if per:
                        assert per % R == 0, name
                        moving = v * (16 * per // R) if moving is None else moving + v * (16 * per // R)
                pe.wait_ge(slot_in[r], value if moving is None else moving + value)
                return ring[:, r, :]

            def tile(stage, r, src, inloop=None, drained=act_done):
                if r >= 4:
                    pe.wait_ge(drained, seq.at(f"{stage}.d{r - 4}"))
                elif inloop:
                    pe.wait_ge(act_done, seq.at(f"{stage}.d{r + 4}", back=inloop))
                w = slot().rearrange("p (k c) -> p k c", c=P)
                for k in range(KD):
                    mm = pe.matmul(psum[:, r % 4, :], w[:, k, :], src[:, k, :],
                                   start=(k == 0), stop=(k == KD - 1))
                mm.then_inc(slot_used, seq.step(f"{stage}.t{r}", ch="slot"))

            def token_major(stage, src, width, banks=(0, 1, 2, 3)):
                for s in range(4):
                    w = slot().rearrange("p (k c) -> p k c", c=512)
                    for kk in range(2):
                        for t in range(NT):
                            k = 2 * s + kk
                            mm = pe.matmul(psum[:, banks[t], 0:width], src[:, k, t * P:(t + 1) * P],
                                           w[:, kk, 0:width], start=(k == 0), stop=(k == KD - 1))
                    mm.then_inc(slot_used, seq.step(f"{stage}.s{s}", ch="slot"))

            def column_sums(stage, src, bank=7, pre="sq", done="ss", written=act_done):
                for k in range(KD):
                    pe.wait_ge(written, seq.at(f"{stage}.{pre}{k}"))
                    mm = pe.matmul(psum[:, bank, :], ones, src[:, k, :], start=(k == 0), stop=(k == KD - 1))
                mm.then_inc(pe_done, seq.step(f"{stage}.{done}"))

            pe.wait_ge(const_in, seq.at("const"))
            pe.wait_ge(x_in, seq.at("x0"))
            with seq.loop("layer", LAYERS):
                meet("n1")
                column_sums("n1", sq)
                pe.wait_ge(dve_done, seq.at("n1.h"))
                meet("gates")
                with seq.loop("gates", 2):
                    for r in range(8):
                        tile("gates", r, h, inloop="gates")
                meet("fm")
                for r in range(NFM):
                    tile("fm", r, h)
                meet("tm")
                token_major("tm", h, TM_COLS)
                meet("cmp")
                for kv in range(2):
                    pe.wait_ge(dve_done, seq.at(f"cmp.b{kv}"))
                    for s in range(4):
                        w = slot().rearrange("p (l c) -> p l c", c=P)
                        for i in range(8):
                            l = 8 * s + i
                            mm = pe.matmul(psum[:, kv, 0:2 * NC], w[:, i, :],
                                           blocks[:, l, :, :].rearrange("p g c -> p (g c)"),
                                           start=(l == 0), stop=(l == 31))
                        mm.then_inc(slot_used, seq.step(f"cmp.u{kv}" if s == 3 else None, ch="slot"))
                pe.wait_ge(act_done, seq.at("cmp.hid1"))
                for g in range(2):
                    w2k = sm("w2k")[:, g * P:(g + 1) * P]
                    w2v = sm("w2v")[:, g * P:(g + 1) * P]
                    pe.matmul(psum[:, 2, g * NC:(g + 1) * NC], w2k, hid[:, 0, g * NC:(g + 1) * NC],
                              start=True, stop=True)
                    mm = pe.matmul(psum[0:NC, 3, g * P:(g + 1) * P], hid[:, 1, g * NC:(g + 1) * NC],
                                   w2v, start=True, stop=True)
                mm.then_inc(pe_done, seq.step("cmp.kv"))
                for i, kt in enumerate((KA, KS, KW)):
                    mm = pe.matmul(psum[:, 4 + i, :], perm, fm[:, kt, :], start=True, stop=True)
                    mm.then_inc(pe_done, seq.step(f"rk{i}"))
                with seq.loop("heads", 4) as j:
                    meet("heads")
                    for i, base in enumerate((QA, QB)):
                        mm = pe.matmul(psum[:, 5 + i, :], perm,
                                       fm[:, bass.ds(j + base, 1), :].rearrange("p o t -> p (o t)"),
                                       start=True, stop=True)
                        mm.then_inc(pe_done, seq.step(f"rq{i}"))

                    def scores(u):
                        kind, g, qt, kts = UNITS[u]
                        q = qs[:, {"A": 0, "cmp": 2}.get(kind, 1), qt * P:(qt + 1) * P]
                        if kind == "cmp":
                            keys = kcp[:, g, :]
                        else:
                            b = {"A": 0, "slc": 1, "win": 2}[kind]
                            keys = kpad[:, b, g, kts[0] * P:(kts[-1] + 1) * P]
                        if u >= 3:
                            pe.wait_ge(act_done, seq.at(f"u{u - 3}.e"))
                        mm = pe.matmul(psum[:, u % 3, 0:width(u)], q, keys, start=True, stop=True)
                        mm.then_inc(pe_done, seq.step(f"u{u}.S"))

                    def turn(u):
                        kind, g, qt, kts = UNITS[u]
                        pe.wait_ge(dve_done, seq.at(f"u{u}.p"))
                        if u >= 2:
                            pe.wait_ge(act_done, seq.at(f"u{u - 2}.t"))
                        if kind == "cmp":
                            mm = pe.transpose(psum[0:NC, 3 + u % 2, 0:P], pbuf[:, u % 3, 0:NC], ident)
                        else:
                            for i in range(len(kts)):
                                mm = pe.transpose(psum[:, 3 + u % 2, i * P:(i + 1) * P],
                                                  pbuf[:, u % 3, i * P:(i + 1) * P], ident)
                        mm.then_inc(pe_done, seq.step(f"u{u}.T"))

                    def weigh(u):
                        kind, g, qt, kts = UNITS[u]
                        pe.wait_ge(act_done, seq.at(f"u{u}.t"))
                        ob = 6 if kind == "A" else 7
                        group = [w for w in range(NU) if UNITS[w][2] == qt and (UNITS[w][0] == "A") == (kind == "A")]
                        acc = psum[:, ob, qt * P:(qt + 1) * P]
                        if kind == "cmp":
                            mm = pe.matmul(acc, vcp[0:NC, g, :], ptbuf[0:NC, u % 2, 0:P],
                                           start=(u == group[0]), stop=False)
                        else:
                            b = {"A": 0, "slc": 1, "win": 2}[kind]
                            for i, kt in enumerate(kts):
                                mm = pe.matmul(acc, pads[:, b, kt, HD * g:HD * g + P],
                                               ptbuf[:, u % 2, i * P:(i + 1) * P],
                                               start=(u == group[0] and i == 0),
                                               stop=(u == group[-1] and i == len(kts) - 1))
                        mm.then_inc(pe_done, seq.step(f"u{u}.o"))

                    pe.wait_ge(dve_done, seq.at("rq.done"))
                    pe.wait_ge(act_done, seq.at("qraw"))
                    scores(0)
                    scores(1)
                    for u in range(NU):
                        if u + 2 < NU:
                            scores(u + 2)
                        turn(u)
                        if u >= 1:
                            weigh(u - 1)
                    weigh(NU - 1)
                meet("branch")
                for r in range(8):
                    a, b = 2 * (r % 2), 2 * (r % 2) + 1
                    if r >= 2:
                        pe.wait_ge(dve_done, seq.at(f"branch.d{r - 2}"))
                    w = slot().rearrange("p (k c) -> p k c", c=P)
                    for br in range(2):
                        for k in range(4):
                            mm = pe.matmul(psum[:, (a, b)[br], :], w[:, 4 * br + k, :], oab[:, br, k, :],
                                           start=(k == 0), stop=(k == 3))
                    mm.then_inc(slot_used, seq.step(f"branch.t{r}", ch="slot"))
                meet("out")
                for r in range(8):
                    tile("out", r, h)
                column_sums("n2", sq)
                meet("n3")
                column_sums("n3", sq)
                pe.wait_ge(dve_done, seq.at("n3.h"))
                meet("up")
                with seq.loop("up", 5):
                    for r in range(8):
                        tile("up", r, h, inloop="up")
                meet("up2")
                for r in range(4):
                    tile("up2", r, h)
                meet("down")
                for half in range(2):
                    for s in range(PAIRS // 2):
                        w = slot().rearrange("p (k c) -> p k c", c=512)
                        for kk in range(2):
                            k = 2 * s + kk
                            for c in range(4):
                                mm = pe.matmul(psum[:, 4 * half + c, :], w[:, kk, c * P:(c + 1) * P],
                                               g_ff[:, k, :], start=(k == 0), stop=(k == PAIRS - 1))
                        mm.then_inc(slot_used, seq.step(f"down.s{half}" if k == PAIRS - 1 else None, ch="slot"))
                pe.wait_ge(act_done, seq.at("down.d3"))
                for _ in range(LAYER_PAD):
                    pe.matmul(psum[:, 0, 0:2], ident, slot()[:, 0:2], start=True, stop=True) \
                        .then_inc(slot_used, seq.step(ch="slot"))
                meet("n4")
                column_sums("n4", sq)
                meet("layer_end")

            def layer_norm_sums(stage, sq):
                column_sums(stage, x, 7, "r", "sum", written=dve_done)
                column_sums(stage, sq, 6)

            meet("ab")
            pe.wait_ge(small_in, seq.at("small2"))
            for t in range(NT):
                for k in range(KD):
                    mm = pe.matmul(psum[:, 0, t * 16:(t + 1) * 16], x[:, k, t * P:(t + 1) * P],
                                   s2("ab")[:, k * 16:(k + 1) * 16], start=(k == 0), stop=(k == KD - 1))
            mm.then_inc(pe_done, seq.step("ab.t"))
            pe.wait_ge(dve_done, seq.at("ab.g"))
            pe.matmul(psum[:, 1, 0:32], cc("tri"), bg[:, G, :], start=True, stop=True)
            pe.matmul(psum[:, 1, 32:64], ones, bg[:, G, :], start=True, stop=True) \
                .then_inc(pe_done, seq.step("ab.gc"))
            meet("dn")
            with seq.loop("dn", 4):
                for r in range(8):
                    tile("dn", r, x, inloop="dn")
            with seq.loop("delta", 4):
                meet("delta")

                def four(hh, bank, lhsT, rhs, mark):
                    for t in range(NT):
                        c = slice(t * P, (t + 1) * P)
                        mm = pe.matmul(psum[:, 4 * hh + bank, c], lhsT[:, c], rhs[:, c], start=True, stop=True)
                    mm.then_inc(pe_done, seq.step(f"d{hh}.{mark}"))

                def turn4(hh, bank, src, mark):
                    for t in range(NT):
                        c = slice(t * P, (t + 1) * P)
                        mm = pe.transpose(psum[:, 4 * hh + bank, c], src[:, c], ident)
                    mm.then_inc(pe_done, seq.step(f"d{hh}.{mark}"))

                for hh in range(2):
                    b = hb[hh]
                    pe.wait_ge(act_done, seq.at(f"d{hh}.sq"))
                    pe.matmul(psum[:, 4 * hh, :], ones, b["ta"], start=True, stop=True)
                    pe.matmul(psum[:, 4 * hh + 1, :], ones, b["tb"], start=True, stop=True) \
                        .then_inc(pe_done, seq.step(f"d{hh}.ss"))
                for hh in range(2):
                    b = hb[hh]
                    pe.wait_ge(dve_done, seq.at(f"d{hh}.norm"))
                    pe.wait_ge(act_done, seq.at(f"d{hh}.vst"))
                    turn4(hh, 2, b["kn"], "kT")
                    turn4(hh, 3, b["vb"], "vT")
                    pe.wait_ge(dve_done, seq.at(f"d{hh}.TG"))
                    pe.matmul(psum[:, 4 * hh, :], ones, b["X"], start=True, stop=True)
                    pe.matmul(psum[:, 4 * hh + 1, :], ones, b["M"], start=True, stop=True) \
                        .then_inc(pe_done, seq.step(f"d{hh}.rows"))
                for hh in range(2):
                    b = hb[hh]
                    pe.wait_ge(dve_done, seq.at(f"d{hh}.kv"))
                    four(hh, 2, b["kn"], b["kn"], "KK")
                    four(hh, 3, b["kn"], b["qn"], "QK")
                for hh in range(2):
                    pe.wait_ge(dve_done, seq.at(f"d{hh}.K0"))
                    turn4(hh, 0, hb[hh]["K"][0], "K0T")
                for lev in range(1, 7):
                    for hh in range(2):
                        b = hb[hh]
                        pe.wait_ge(dve_done, seq.at(f"d{hh}.K{lev}"))
                        pe.wait_ge(dve_done, seq.at(f"d{hh}.X{lev - 1}"))
                        four(hh, 0, b["K"][lev % 2], b["M"], f"T{lev}")
                    for hh in range(2):
                        b = hb[hh]
                        pe.wait_ge(act_done, seq.at(f"d{hh}.Ts{lev}"))
                        four(hh, 1, b["T1"], b["X"], f"XT{lev}")
                        if lev < 6:
                            four(hh, 2, b["X"], b["T1"], f"MT{lev}")
                for t in range(NT):
                    c = slice(t * P, (t + 1) * P)
                    for hh in range(2):
                        b = hb[hh]
                        if t:
                            pe.wait_ge(dve_done, seq.at(f"d{hh}.S{t - 1}"))
                            pe.matmul(psum[:, 4 * hh, 0:P], b["kn"][:, c], b["S"], start=True, stop=True) \
                                .then_inc(pe_done, seq.step(f"d{hh}.kS{t}"))
                    for hh in range(2):
                        b = hb[hh]
                        pe.wait_ge(dve_done, seq.at(f"d{hh}.R{t}"))
                        pe.matmul(psum[:, 4 * hh + 1, 0:P], b["X"][:, c], b["R"] if t else b["vb"][:, c],
                                       start=True, stop=True).then_inc(pe_done, seq.step(f"d{hh}.v{t}"))
                    for hh in range(2):
                        b = hb[hh]
                        pe.wait_ge(act_done, seq.at(f"d{hh}.vn{t}"))
                        if t < NT - 1:
                            pe.matmul(psum[:, 4 * hh + 3, 0:P], b["kd"][:, c], b["vn"], start=True, stop=True) \
                                .then_inc(pe_done, seq.step(f"d{hh}.dS{t}"))
                        if t:
                            pe.matmul(psum[:, 4 * hh + 2, c], b["S"], b["qd"][:, c], start=True, stop=False)
                        pe.matmul(psum[:, 4 * hh + 2, c], b["vn"], b["at"][:, c], start=(t == 0), stop=True) \
                            .then_inc(pe_done, seq.step(f"d{hh}.o{t}"))
                for hh in range(2):
                    pe.wait_ge(act_done, seq.at(f"d{hh}.osq"))
                    pe.matmul(psum[:, 4 * hh, :], ones, hb[hh]["ta"], start=True, stop=True) \
                        .then_inc(pe_done, seq.step(f"d{hh}.oss"))
            meet("wo")
            for r in range(8):
                tile("wo", r, zt[:, :, 3, :], drained=dve_done)
            layer_norm_sums("l0", sq2)

            def experts(m, xsrc):
                meet(f"{m}.route")
                w = s2("router").rearrange("p (l k c) -> p l k c", l=2, c=36)[:, int(m[1])]
                for t in range(NT):
                    for k in range(KD):
                        mm = pe.matmul(psum[:, 0, t * 36:(t + 1) * 36], x[:, k, t * P:(t + 1) * P], w[:, k, :],
                                       start=(k == 0), stop=(k == KD - 1))
                mm.then_inc(pe_done, seq.step(f"{m}.lg"))
                for i in range(8):
                    t, half = i // 2, i % 2
                    if i >= 4:
                        pe.wait_ge(act_done, seq.at(f"{m}.h{i - 4}"))
                    for k in range(4):
                        mm = pe.transpose(psum[:, 4 + i % 4, k * P:(k + 1) * P],
                                          x[:, 4 * half + k, t * P:(t + 1) * P], ident)
                    mm.then_inc(pe_done, seq.step(f"{m}.tm{i}"))
                pe.wait_ge(dve_done, seq.at(f"{m}.chosen"))
                for t in range(NT):
                    for u in range(t):
                        pe.matmul(psum[:, 1, t * 32:(t + 1) * 32], ones, rt[2][:, u, :], start=(u == 0), stop=False)
                    pe.matmul(psum[:, 1, t * 32:(t + 1) * 32], cc("strictT"), rt[2][:, t, :],
                              start=(t == 0), stop=True)
                for t in range(NT):
                    mm = pe.matmul(psum[:, 2, 0:32], ones, rt[2][:, t, :], start=(t == 0), stop=(t == NT - 1))
                mm.then_inc(pe_done, seq.step(f"{m}.rank"))
                pe.wait_ge(dve_done, seq.at(f"{m}.rnd"))
                rounds = seq.count_of(rnd[0:1, 0:1].bitcast(I32), 1, ROUNDS_MAX)
                meet(f"{m}.ex")

                def turn_x(ee, mark):
                    for k in range(KD):
                        mm = pe.transpose(psum[:, k // 4, (k % 4) * P:(k % 4 + 1) * P],
                                          xg[:, ee, k * P:(k + 1) * P], ident)
                    mm.then_inc(pe_done, seq.step(f"{m}.{mark}"))

                L = f"{m}.ex"
                pe.wait_ge(rows_gathered[0], seq.at(f"{m}.Gpre0"))
                turn_x(0, "Tpre")
                pe.wait_ge(dve_done, seq.at(f"{m}.xTpre"))
                with seq.rounds(L, rounds):
                    for ee in range(2):
                        if ee:
                            pe.wait_ge(dve_done, seq.at(f"{m}.xT1"))
                            pe.wait_ge(dve_done, seq.at(f"{m}.hs0"))
                        else:
                            pe.wait_ge(dve_done, seq.at(f"{m}.xT0n", back=L))
                            pe.wait_ge(dve_done, seq.at(f"{m}.hs1", back=L))
                        for k in range(KD):
                            w = slot()
                            for half in range(2):
                                mm = pe.matmul(psum[:, 2 + half, :], xT[:, ee, k, :],
                                               w[:, half * EFF:(half + 1) * EFF], start=(k == 0), stop=(k == KD - 1))
                            mm.then_inc(slot_used, seq.step(f"{m}.g{ee}", ch="slot"))
                        if ee:
                            pe.wait_ge(rows_gathered[0], seq.at(f"{m}.G0"))
                            turn_x(0, "T0n")
                        else:
                            pe.wait_ge(rows_gathered[1], seq.at(f"{m}.G1", back=L))
                            turn_x(1, "T1")
                        pe.wait_ge(dve_done, seq.at(f"{m}.hs{ee}"))
                        for f in range(4):
                            mm = pe.transpose(psum[:, 4, f * P:(f + 1) * P], hs[:, ee, f * P:(f + 1) * P], ident)
                        mm.then_inc(pe_done, seq.step(f"{m}.HT{ee}"))
                        pe.wait_ge(act_done, seq.at(f"{m}.hT{ee}"))
                        pe.wait_ge(act_done, seq.at(f"{m}.ya{1 - ee}", back=None if ee else L))
                        pe.wait_ge(dve_done, seq.at(f"{m}.yd{1 - ee}", back=None if ee else L))
                        for f in range(4):
                            w = slot()
                            for half in range(2):
                                mm = pe.matmul(psum[:, 5 + half, :], hT[:, ee, f, :],
                                               w[:, half * 512:(half + 1) * 512], start=(f == 0), stop=(f == 3))
                            mm.then_inc(slot_used, seq.step(f"{m}.z{ee}", ch="slot"))
                meet(f"{m}.back")
                for k in range(KD):
                    if k >= 4:
                        pe.wait_ge(dve_done, seq.at(f"{m}.r{k - 4}"))
                    for t in range(NT):
                        if k == 0:
                            pe.wait_ge(dve_done, seq.at(f"{m}.yt{t}"))
                        mm = pe.transpose(psum[:, k % 4, t * P:(t + 1) * P], yt[:, t, k * P:(k + 1) * P], ident)
                    mm.then_inc(pe_done, seq.step(f"{m}.f{k}"))
                layer_norm_sums(m, sq4)

            experts("m0", x)
            meet("kda")
            for r in range(8):
                tile("kda", r, x)
            meet("vda")
            token_major("vda0", x, 512)
            token_major("vda1", x, 512, (4, 5, 6, 7))
            meet("qda")
            for r in range(8):
                tile("qda", r, x)
            with seq.loop("da", 4) as j:
                meet("da")
                pe.wait_ge(act_done, seq.at("da.q"))
                pe.wait_ge(dve_done, seq.at("da.v"))

                def scores2(u):
                    hh, qt = u // 4, u % 4
                    if u >= 2:
                        pe.wait_ge(act_done, seq.at(f"a{u - 2}.e"))
                    for s_ in range(2):
                        mm = pe.matmul(psum[:, 2 * (u % 2) + s_, 0:(qt + 1) * P],
                                       qz[:, 2 * hh + s_, qt * P:(qt + 1) * P],
                                       kda[:, bass.ds(j * (2 * T) + hh * T, (qt + 1) * P)], start=True, stop=True)
                    mm.then_inc(pe_done, seq.step(f"a{u}.S"))

                def turn2(u):
                    pe.wait_ge(dve_done, seq.at(f"a{u}.p"))
                    if u >= 2:
                        pe.wait_ge(act_done, seq.at(f"a{u - 2}.t"))
                    for i in range(u % 4 + 1):
                        mm = pe.transpose(psum[:, 4 + u % 2, i * P:(i + 1) * P],
                                          pda[:, 2 * (u % 3), i * P:(i + 1) * P], ident)
                    mm.then_inc(pe_done, seq.step(f"a{u}.T"))

                def weigh2(u):
                    hh, qt = u // 4, u % 4
                    pe.wait_ge(act_done, seq.at(f"a{u}.t"))
                    for i in range(qt + 1):
                        mm = pe.matmul(psum[:, 6 + hh, qt * P:(qt + 1) * P], va_h[:, hh, i, :],
                                       ptd[:, u % 2, i * P:(i + 1) * P], start=(i == 0), stop=(i == qt))
                    mm.then_inc(pe_done, seq.step(f"a{u}.o"))

                scores2(0)
                for u in range(8):
                    if u + 1 < 8:
                        scores2(u + 1)
                    turn2(u)
                    if u:
                        weigh2(u - 1)
                weigh2(7)
            meet("dan")
            for hd in range(8):
                pe.wait_ge(act_done, seq.at(f"dan.sq{hd}"))
                pe.matmul(psum[:, hd, :], ones, sq3[:, hd, :], start=True, stop=True) \
                    .then_inc(pe_done, seq.step(f"dan.ss{hd}"))
            pe.wait_ge(dve_done, seq.at("dan.o"))
            meet("wo2")
            for r in range(8):
                tile("wo2", r, oda, drained=dve_done)
            layer_norm_sums("l1", sq3)
            experts("m1", x)

        @blk.scalar
        def _(act):
            seq = Sequence(act, settled, old, new, "act", "dma_h0", "dma_h1", "dma_b0", "dma_b1")
            act.sem_inc(act_done, seq.step(inc=64))

            def meet(stage):
                seq.note(f"{stage}.begin.act")
                act.wait_ge(act_done, seq.so_far())
                act.wait_ge(pe_done, seq.at(f"{stage}.begin.pe"))
                act.wait_ge(slot_used, seq.at(f"{stage}.begin.pe", of="slot"))
                act.wait_ge(dve_done, seq.at(f"{stage}.begin.dve"))

            def squares(stage, src):
                for k in range(KD):
                    act.activation(sq[:, k, :], src[:, k, :], ACT.Square) \
                        .then_inc(act_done, seq.step(f"{stage}.sq{k}"))

            def rstd(stage, div=D, eps="eps", bank=7):
                act.wait_ge(pe_done, seq.at(f"{stage}.ss"))
                act.activation(rs, psum[:, bank, :], ACT.Ln, bias=cc(eps), scale=1.0 / div) \
                    .then_inc(act_done, seq.step())
                act.wait_ge(act_done, seq.so_far())
                act.activation(rs, rs, ACT.Exp, scale=-0.5).then_inc(act_done, seq.step(f"{stage}.rs"))

            act.wait_ge(const_in, seq.at("const"))
            act.wait_ge(dve_done, seq.at("angle"))
            act.activation(sinT, tmp[:, 0, :], ACT.Sin).then_inc(act_done, seq.step())
            act.activation(cosT, tmp[:, 1, :], ACT.Sin).then_inc(act_done, seq.step("trig"))
            act.wait_ge(x_in, seq.at("x0"))
            with seq.loop("layer", LAYERS):
                meet("n1")
                squares("n1", x)
                rstd("n1")
                meet("gates")
                with seq.loop("gates", 2) as i:
                    for r in range(8):
                        act.wait_ge(slot_used, seq.at(f"gates.t{r}"))
                        act.activation(big[:, bass.ds(i * (8 * T) + r * T, T)], psum[:, r % 4, :],
                                            ACT.Sigmoid).then_inc(act_done, seq.step(f"gates.d{r}"))
                meet("fm")
                for r in range(NFM):
                    act.wait_ge(slot_used, seq.at(f"fm.t{r}"))
                    act.activation(fm[:, r, :], psum[:, r % 4, :], ACT.Copy) \
                        .then_inc(act_done, seq.step(f"fm.d{r}"))
                meet("tm")
                act.wait_ge(slot_used, seq.at("tm.s3"))
                act.wait_ge(pool_done, seq.at("zeroed"))
                for t in range(NT):
                    for b in range(3):
                        act.activation(
                            pads[:, b, t, :].rearrange("p (a c) -> p a c", c=HD)[:, 0:3:2, :],
                            psum[:, t, b * P:(b + 1) * P].rearrange("p (g c) -> p g c", c=HD), ACT.Copy) \
                            .then_inc(act_done, seq.step())
                    act.activation(gate[:, t, :], psum[:, t, GATE_C:TM_COLS], ACT.Sigmoid) \
                        .then_inc(act_done, seq.step())
                meet("cmp")
                for kv in range(2):
                    act.wait_ge(slot_used, seq.at(f"cmp.u{kv}"))
                    act.activation(hid[:, kv, :], psum[:, kv, 0:2 * NC], ACT.Gelu_apprx_tanh,
                                        bias=sm("b1")[:, kv:kv + 1]).then_inc(act_done, seq.step(f"cmp.hid{kv}"))
                act.wait_ge(pe_done, seq.at("cmp.kv"))
                act.activation(kcp.rearrange("p g c -> p (g c)"), psum[:, 2, 0:2 * NC], ACT.Copy) \
                    .then_inc(act_done, seq.step())
                act.activation(vcp[0:NC].rearrange("p g c -> p (g c)"), psum[0:NC, 3, 0:2 * P], ACT.Copy) \
                    .then_inc(act_done, seq.step())
                with seq.loop("heads", 4) as j:
                    meet("heads")
                    act.activation(qs[:, 2, :], fm[:, bass.ds(j + QB, 1), :].rearrange("p o t -> p (o t)"),
                                        ACT.Copy).then_inc(act_done, seq.step("qraw"))

                    def exps(u):
                        kind, g, qt, kts = UNITS[u]
                        act.wait_ge(dve_done, seq.at(f"u{u}.m"))
                        if u >= 3:
                            act.wait_ge(pe_done, seq.at(f"u{u - 3}.T"))
                        if kind == "A":
                            act.activation(cols[:, u % 4, 3:4], cols[:, u % 4, 1:2], ACT.Exp,
                                                bias=sj[:, 0, g:g + 1]).then_inc(act_done, seq.step())
                        act.activation(pbuf[:, u % 3, 0:width(u)], psum[:, u % 3, 0:width(u)], ACT.Exp,
                                            bias=cols[:, u % 4, 1:2], scale=SCALE,
                                            accum_out=cols[:, u % 4, 2:3]).then_inc(act_done, seq.step(f"u{u}.e"))

                    def evict(u):
                        kind, g, qt, kts = UNITS[u]
                        act.wait_ge(pe_done, seq.at(f"u{u}.T"))
                        if u >= 2:
                            act.wait_ge(pe_done, seq.at(f"u{u - 2}.o"))
                        if kind == "cmp":
                            o, i = ptbuf[0:NC, u % 2, 0:P], psum[0:NC, 3 + u % 2, 0:P]
                        else:
                            o, i = ptbuf[:, u % 2, 0:width(u)], psum[:, 3 + u % 2, 0:width(u)]
                        act.activation(o, i, ACT.Copy).then_inc(act_done, seq.step(f"u{u}.t"))

                    exps(0)
                    for u in range(NU):
                        if u + 1 < NU:
                            exps(u + 1)
                        evict(u)
                    act.wait_ge(pe_done, seq.at(f"u{NU - 1}.o"))
                    for br in range(2):
                        act.activation(oab[:, br, bass.ds(j, 1), :].rearrange("p o t -> p (o t)"),
                                            psum[:, 6 + br, :], ACT.Copy).then_inc(act_done, seq.step())
                meet("branch")
                meet("out")
                for r in range(8):
                    act.wait_ge(slot_used, seq.at(f"out.t{r}"))
                    act.activation(y[:, r, :], psum[:, r % 4, :], ACT.Copy).then_inc(act_done, seq.step())
                    act.activation(sq[:, r, :], psum[:, r % 4, :], ACT.Square) \
                        .then_inc(act_done, seq.step(f"out.d{r}"))
                    seq.note(f"n2.sq{r}")
                rstd("n2")
                meet("n3")
                squares("n3", x)
                rstd("n3")
                meet("up")

                def gelu(stage, i, dst):
                    act.wait_ge(dve_done, seq.at(f"{stage}.c{i}"))
                    act.activation(dst, tmp[:, 2 * (i % 2), :], ACT.Gelu_apprx_tanh) \
                        .then_inc(act_done, seq.step(f"{stage}.g{i}"))

                def up_pairs(stage, n, inloop):
                    for r in range(n):
                        act.wait_ge(slot_used, seq.at(f"{stage}.t{r}"))
                        if r >= 4:
                            act.wait_ge(dve_done, seq.at(f"{stage}.v{r - 4}"))
                        elif inloop:
                            act.wait_ge(dve_done, seq.at(f"{stage}.v{r + 4}", back=inloop))
                        act.activation(U[:, r % 4, 2:T + 2], psum[:, r % 4, :], ACT.Copy) \
                            .then_inc(act_done, seq.step(f"{stage}.d{r}"))
                        if r % 2 == 1 and r >= 3:
                            pair = (r - 3) // 2
                            gelu(stage, pair, tmp[:, 4 + pair % 2, :])
                    gelu(stage, n // 2 - 1, tmp[:, 4 + (n // 2 - 1) % 2, :])

                with seq.loop("up", 5):
                    up_pairs("up", 8, "up")
                meet("up2")
                up_pairs("up2", 4, None)
                meet("down")
                for half in range(2):
                    act.wait_ge(slot_used, seq.at(f"down.s{half}"))
                    for c in range(4):
                        b = 4 * half + c
                        act.activation(h[:, b, :], psum[:, b, :], ACT.Copy) \
                            .then_inc(act_done, seq.step(f"down.d{b}"))
                meet("n4")
                squares("n4", h)
                rstd("n4")
                meet("layer_end")

            def layer_norm(stage, sq_, rs_):
                act.wait_ge(pe_done, seq.at(f"{stage}.sum"))
                act.activation(rs_, psum[:, 7, :], ACT.Copy, scale=1.0 / D) \
                    .then_inc(act_done, seq.step(f"{stage}.mu"))
                for k in range(KD):
                    act.wait_ge(dve_done, seq.at(f"{stage}.c{k}"))
                    act.activation(sq_[:, k, :], x[:, k, :], ACT.Square) \
                        .then_inc(act_done, seq.step(f"{stage}.sq{k}"))
                act.wait_ge(pe_done, seq.at(f"{stage}.ss"))
                act.activation(rs_, psum[:, 6, :], ACT.Ln, bias=cc("lneps"), scale=1.0 / D) \
                    .then_inc(act_done, seq.step())
                act.wait_ge(act_done, seq.so_far())
                act.activation(rs_, rs_, ACT.Exp, scale=-0.5).then_inc(act_done, seq.step(f"{stage}.rs"))

            meet("ab")
            act.wait_ge(small_in, seq.at("small2"))
            act.wait_ge(pe_done, seq.at("ab.t"))
            ab = psum[:, 0, 0:64].rearrange("p (t c) -> p t c", c=16)
            def th(v):
                return v.rearrange("p (t h) -> p t h", h=8)
            act.activation(th(bg[:, BETA, :]), ab[:, :, 0:8], ACT.Sigmoid).then_inc(act_done, seq.step("ab.beta"))
            act.activation(sc[:, 3, 0:8], s2("alog"), ACT.Exp).then_inc(act_done, seq.step())
            act.wait_ge(dve_done, seq.at("ab.abs"))
            act.activation(sc[:, 2, :], sc[:, 1, :], ACT.Exp, scale=-1.0).then_inc(act_done, seq.step())
            act.wait_ge(act_done, seq.so_far())
            act.activation(sc[:, 2, :], sc[:, 2, :], ACT.Ln, bias=cc("one")).then_inc(act_done, seq.step("ab.sp"))
            act.wait_ge(pe_done, seq.at("ab.gc"))
            act.activation(bg[:, GC, :], psum[:, 1, 0:32], ACT.Copy).then_inc(act_done, seq.step("ab.gcc"))
            act.activation(bg[:, EL, :], psum[:, 1, 32:64], ACT.Exp).then_inc(act_done, seq.step("ab.el"))
            act.activation(sc[:, 4, :], psum[:, 1, 0:32], ACT.Exp).then_inc(act_done, seq.step("ab.egc"))
            act.wait_ge(dve_done, seq.at("ab.dif"))
            act.activation(bg[:, EKD, :], sc[:, 5, :], ACT.Exp).then_inc(act_done, seq.step())
            meet("dn")
            with seq.loop("dn", 4) as i:
                def silu(r):
                    act.wait_ge(dve_done, seq.at(f"dn.v{r}"))
                    act.activation(qkvz[:, bass.ds(i * (8 * T) + r * T, T)], cdn[:, r % 4, :], ACT.Silu) \
                        .then_inc(act_done, seq.step(f"dn.s{r}"))
                for r in range(8):
                    act.wait_ge(slot_used, seq.at(f"dn.t{r}"))
                    if r % 4 == 3:
                        act.activation(qkvz[:, bass.ds(i * (8 * T) + r * T, T)], psum[:, r % 4, :], ACT.Silu) \
                            .then_inc(act_done, seq.step(f"dn.d{r}"))
                    else:
                        if r >= 4:
                            act.wait_ge(dve_done, seq.at(f"dn.v{r - 4}"))
                        else:
                            act.wait_ge(dve_done, seq.at(f"dn.v{r + 4}", back="dn"))
                        act.activation(U3[:, r % 4, 3:T + 3], psum[:, r % 4, :], ACT.Copy) \
                            .then_inc(act_done, seq.step(f"dn.d{r}"))
                    if r % 4:
                        silu(r - 1)
            with seq.loop("delta", 4) as i:
                meet("delta")
                for hh in range(2):
                    b = hb[hh]
                    for c, dst in ((0, "ta"), (1, "tb")):
                        act.activation(b[dst], qkvz[:, bass.ds(i * (8 * T) + (4 * hh + c) * T, T)], ACT.Square) \
                            .then_inc(act_done, seq.step())
                    seq.note(f"d{hh}.sq")
                    act.activation(b["vb"], qkvz[:, bass.ds(i * (8 * T) + (4 * hh + 2) * T, T)], ACT.Copy) \
                        .then_inc(act_done, seq.step(f"d{hh}.vst"))
                for hh in range(2):
                    b = hb[hh]
                    act.wait_ge(pe_done, seq.at(f"d{hh}.ss"))
                    for c, dst in ((0, "ta"), (1, "tb")):
                        act.activation(b[dst], psum[:, 4 * hh + c, :], ACT.Ln, bias=cc("eps")) \
                            .then_inc(act_done, seq.step())
                act.wait_ge(act_done, seq.so_far())
                for hh in range(2):
                    b = hb[hh]
                    for dst in ("ta", "tb"):
                        act.activation(b[dst], b[dst], ACT.Exp, scale=-0.5).then_inc(act_done, seq.step())
                    seq.note(f"d{hh}.rs")
                for hh in range(2):
                    b = hb[hh]
                    act.wait_ge(pe_done, seq.at(f"d{hh}.rows"))
                    act.wait_ge(dve_done, seq.at(f"d{hh}.norm"))
                    act.activation(b["ta"], psum[:, 4 * hh, :], ACT.Exp).then_inc(act_done, seq.step(f"d{hh}.egb"))
                for hh in range(2):
                    b = hb[hh]
                    act.wait_ge(dve_done, seq.at(f"d{hh}.dif"))
                    act.activation(b["dm"], b["dm"], ACT.Exp).then_inc(act_done, seq.step(f"d{hh}.dec"))
                for lev in range(1, 7):
                    for hh in range(2):
                        act.wait_ge(pe_done, seq.at(f"d{hh}.T{lev}"))
                        act.activation(hb[hh]["T1"], psum[:, 4 * hh, :], ACT.Copy) \
                            .then_inc(act_done, seq.step(f"d{hh}.Ts{lev}"))
                for t in range(NT):
                    for hh in range(2):
                        act.wait_ge(pe_done, seq.at(f"d{hh}.v{t}"))
                        if t:
                            act.wait_ge(pe_done, seq.at(f"d{hh}.o{t - 1}"))
                        act.activation(hb[hh]["vn"], psum[:, 4 * hh + 1, 0:P], ACT.Copy) \
                            .then_inc(act_done, seq.step(f"d{hh}.vn{t}"))
                for hh in range(2):
                    act.wait_ge(pe_done, seq.at(f"d{hh}.o{NT - 1}"))
                    act.activation(hb[hh]["ta"], psum[:, 4 * hh + 2, :], ACT.Square) \
                        .then_inc(act_done, seq.step(f"d{hh}.osq"))
                for hh in range(2):
                    act.wait_ge(pe_done, seq.at(f"d{hh}.oss"))
                    act.activation(hb[hh]["tb"], psum[:, 4 * hh, :], ACT.Ln, bias=cc("eps"), scale=1.0 / P) \
                        .then_inc(act_done, seq.step())
                act.wait_ge(act_done, seq.so_far())
                for hh in range(2):
                    act.activation(hb[hh]["tb"], hb[hh]["tb"], ACT.Exp, scale=-0.5) \
                        .then_inc(act_done, seq.step(f"d{hh}.ors"))
            meet("wo")
            layer_norm("l0", sq2, rs2)

            def experts(m):
                meet(f"{m}.route")
                act.wait_ge(pe_done, seq.at(f"{m}.lg"))
                act.activation(lg.rearrange("p t c -> p (t c)"), psum[:, 0, 0:NT * 36], ACT.Copy) \
                    .then_inc(act_done, seq.step(f"{m}.lgs"))
                for i in range(8):
                    t, half = i // 2, i % 2
                    act.wait_ge(pe_done, seq.at(f"{m}.tm{i}"))
                    act.activation(htm[:, t, 512 * half:512 * half + 512], psum[:, 4 + i % 4, :], ACT.Copy) \
                        .then_inc(act_done, seq.step(f"{m}.h{i}"))
                act.wait_ge(act_done, seq.so_far())
                rows = hd[m].rearrange("(t p c) d -> c p t d", p=P, c=2)
                for c in range(2):
                    act.dma_start(rows[c], htm) \
                        .then_inc(rows_written[c], seq.step(f"{m}.hd{c}", ch=f"dma_h{c}", inc=16))
                act.wait_ge(dve_done, seq.at(f"{m}.ge"))
                act.activation(rt[1][:, :, 0:NG], rt[0][:, :, 0:NG], ACT.Exp) \
                    .then_inc(act_done, seq.step(f"{m}.gx"))
                act.wait_ge(dve_done, seq.at(f"{m}.d"))
                act.activation(rc[:, 9, :], rc[:, 8, :], ACT.Exp).then_inc(act_done, seq.step(f"{m}.e2"))
                act.wait_ge(dve_done, seq.at(f"{m}.rnd"))
                rounds = seq.count_of(rnd[0:1, 0:1].bitcast(I32), 1, ROUNDS_MAX)
                meet(f"{m}.ex")
                L = f"{m}.ex"
                with seq.rounds(L, rounds):
                    for ee in range(2):
                        act.wait_ge(slot_used, seq.at(f"{m}.g{ee}"))
                        act.activation(sg[:, ee, :], psum[:, 2, :], ACT.Silu) \
                            .then_inc(act_done, seq.step(f"{m}.sg{ee}"))
                        act.wait_ge(pe_done, seq.at(f"{m}.HT{ee}"))
                        act.activation(hT[:, ee].rearrange("p f c -> p (f c)"), psum[:, 4, :], ACT.Copy) \
                            .then_inc(act_done, seq.step(f"{m}.hT{ee}"))
                        act.wait_ge(slot_used, seq.at(f"{m}.z{ee}"))
                        act.wait_ge(rows_scattered[ee], seq.at(f"{m}.sc{ee}", back=L))
                        act.activation(ym[:, ee, 0:512], psum[:, 5, :], ACT.Copy) \
                            .then_inc(act_done, seq.step(f"{m}.ya{ee}"))
                meet(f"{m}.back")
                act.wait_ge(rows_scattered[0], seq.at(f"{m}.sc0"))
                act.wait_ge(rows_scattered[1], seq.at(f"{m}.sc1"))
                rows = yd[m].rearrange("(t p c) d -> t p c d", p=P, c=2)
                for t in range(NT):
                    if t >= 2:
                        act.wait_ge(dve_done, seq.at(f"{m}.yt{t - 2}"))
                    act.dma_start(y2[:, t % 2], rows[t]) \
                        .then_inc(rows_back[t % 2], seq.step(f"{m}.y2{t}", ch=f"dma_b{t % 2}", inc=16))
                layer_norm(m, sq4, rs4)

            experts("m0")
            meet("kda")
            for r in range(8):
                act.wait_ge(slot_used, seq.at(f"kda.t{r}"))
                act.activation(kda[:, r * T:(r + 1) * T], psum[:, r % 4, :], ACT.Copy) \
                    .then_inc(act_done, seq.step(f"kda.d{r}"))
            meet("vda")
            for half in range(2):
                act.wait_ge(slot_used, seq.at(f"vda{half}.s3"))
                for t in range(NT):
                    act.activation(vda[:, t, 512 * half:512 * half + 512], psum[:, 4 * half + t, :], ACT.Copy) \
                        .then_inc(act_done, seq.step())
            meet("qda")
            for r in range(8):
                act.wait_ge(slot_used, seq.at(f"qda.t{r}"))
                act.activation(qda[:, r * T:(r + 1) * T], psum[:, r % 4, :], ACT.Copy) \
                    .then_inc(act_done, seq.step(f"qda.d{r}"))
            act.wait_ge(dve_done, seq.at("lam.s"))
            act.activation(lam[:, 132:134], lam[:, 130:132], ACT.Exp).then_inc(act_done, seq.step("lam.e"))
            with seq.loop("da", 4) as j:
                meet("da")
                for hh in range(2):
                    src = qda[:, bass.ds(j * (2 * T) + hh * T, T)]
                    for s_ in range(2):
                        p0 = HD * s_
                        act.activation(qz[p0:p0 + HD, 2 * hh + s_, :], src[p0:p0 + HD, :], ACT.Copy) \
                            .then_inc(act_done, seq.step())
                seq.note("da.q")
                def exps2(u):
                    w = (u % 4 + 1) * P
                    act.wait_ge(dve_done, seq.at(f"a{u}.m"))
                    if u >= 3:
                        act.wait_ge(pe_done, seq.at(f"a{u - 3}.T"))
                    c = dcols[:, u % 4, :]
                    for s_ in range(2):
                        act.activation(pda[:, 2 * (u % 3) + s_, 0:w], psum[:, 2 * (u % 2) + s_, 0:w], ACT.Exp,
                                            bias=c[:, 2 + s_:3 + s_], scale=SCALE, accum_out=c[:, 4 + s_:5 + s_]) \
                            .then_inc(act_done, seq.step())
                    seq.note(f"a{u}.e")
                exps2(0)
                for u in range(8):
                    if u + 1 < 8:
                        exps2(u + 1)
                    w = (u % 4 + 1) * P
                    act.wait_ge(pe_done, seq.at(f"a{u}.T"))
                    if u >= 2:
                        act.wait_ge(pe_done, seq.at(f"a{u - 2}.o"))
                    act.activation(ptd[:, u % 2, 0:w], psum[:, 4 + u % 2, 0:w], ACT.Copy) \
                        .then_inc(act_done, seq.step(f"a{u}.t"))
                act.wait_ge(pe_done, seq.at("a7.o"))
                for hh in range(2):
                    act.activation(oda.rearrange("p a t -> p (a t)")[:, bass.ds(j * (2 * T) + hh * T, T)],
                                        psum[:, 6 + hh, :], ACT.Copy).then_inc(act_done, seq.step())
            meet("dan")
            for hd_ in range(8):
                act.activation(sq3[:, hd_, :], oda[:, hd_, :], ACT.Square) \
                    .then_inc(act_done, seq.step(f"dan.sq{hd_}"))
            for hd_ in range(8):
                act.wait_ge(pe_done, seq.at(f"dan.ss{hd_}"))
                act.activation(sq3[:, hd_, :], psum[:, hd_, :], ACT.Ln, bias=cc("eps"), scale=1.0 / P) \
                    .then_inc(act_done, seq.step())
            act.wait_ge(act_done, seq.so_far())
            for hd_ in range(8):
                act.activation(sq3[:, hd_, :], sq3[:, hd_, :], ACT.Exp, scale=-0.5) \
                    .then_inc(act_done, seq.step(f"dan.rs{hd_}"))
            meet("wo2")
            layer_norm("l1", sq3, rs3)
            experts("m1")

        @blk.vector
        def _(dve):
            seq = Sequence(dve, settled, old, new, "dve")
            dve.sem_inc(dve_done, seq.step(inc=64))

            def meet(stage):
                seq.note(f"{stage}.begin.dve")
                dve.wait_ge(dve_done, seq.so_far())
                dve.wait_ge(pe_done, seq.at(f"{stage}.begin.pe"))
                dve.wait_ge(slot_used, seq.at(f"{stage}.begin.pe", of="slot"))
                dve.wait_ge(act_done, seq.at(f"{stage}.begin.act"))

            def scaled(stage, dst, src, gain):
                dve.wait_ge(act_done, seq.at(f"{stage}.rs"))
                for k in range(KD):
                    dve.scalar_tensor_tensor(dst[:, k, :], src[:, k, :], gains[:, gain, k:k + 1], rs,
                                                  ALU.mult, ALU.mult).then_inc(dve_done, seq.step())
                seq.note(f"{stage}.h")

            def residual(stage, src, gain):
                scaled(stage, src, src, gain)
                dve.wait_ge(dve_done, seq.so_far())
                for k in range(KD):
                    dve.tensor_tensor(x[:, k, :], x[:, k, :], src[:, k, :], ALU.add).then_inc(dve_done, seq.step())
                dve.wait_ge(dve_done, seq.so_far())

            dve.wait_ge(const_in, seq.at("const"))
            dve.wait_ge(positions_in, seq.at("posi"))
            pf, ang, turns, red = tmp[:, 2, :], tmp[:, 3, :], tmp[:, 4, :], tmp[:, 0, :]
            dve.tensor_copy(pf, posi).then_inc(dve_done, seq.step())
            dve.wait_ge(dve_done, seq.so_far())
            dve.tensor_scalar(ang, pf, cc("invf"), None, ALU.mult).then_inc(dve_done, seq.step())
            dve.wait_ge(dve_done, seq.so_far())
            MAGIC = 12582912.0
            dve.tensor_scalar(turns, ang, 1.0 / (2 * math.pi), MAGIC, ALU.mult, ALU.add) \
                .then_inc(dve_done, seq.step())
            dve.wait_ge(dve_done, seq.so_far())
            dve.tensor_scalar(turns, turns, MAGIC, None, ALU.subtract).then_inc(dve_done, seq.step())
            dve.wait_ge(dve_done, seq.so_far())
            c1 = 6.28125
            c2 = float(np.float32(2 * math.pi - c1).view(np.int32).__and__(~0xFFF).view(np.float32))
            c3 = 2 * math.pi - c1 - c2
            src = ang
            for c in (c1, c2, c3):
                dve.scalar_tensor_tensor(red, turns, -c, src, ALU.mult, ALU.add).then_inc(dve_done, seq.step())
                dve.wait_ge(dve_done, seq.so_far())
                src = red
            dve.tensor_scalar(red, red, math.pi - 1e-6, -(math.pi - 1e-6), ALU.min, ALU.max) \
                .then_inc(dve_done, seq.step())
            dve.wait_ge(dve_done, seq.so_far())
            dve.tensor_scalar(ang, red, -1.0, None, ALU.mult).then_inc(dve_done, seq.step())
            dve.wait_ge(dve_done, seq.so_far())
            dve.tensor_tensor(ang, ang, red, ALU.min).then_inc(dve_done, seq.step())
            dve.wait_ge(dve_done, seq.so_far())
            dve.tensor_scalar(tmp[:, 1, :], ang, math.pi / 2, None, ALU.add).then_inc(dve_done, seq.step("angle"))
            dve.wait_ge(x_in, seq.at("x0"))
            dve.wait_ge(pool_done, seq.at("zeroed"))
            with seq.loop("layer", LAYERS):
                meet("n1")
                dve.wait_ge(small_in, seq.at("small"))
                scaled("n1", h, x, 0)
                meet("gates")
                meet("fm")
                meet("tm")
                meet("cmp")
                for kv in range(2):
                    if kv:
                        dve.wait_ge(slot_used, seq.at("cmp.u0"))
                    else:
                        dve.memset(blocks, 0.0).then_inc(dve_done, seq.step())
                        dve.wait_ge(dve_done, seq.so_far())
                    for g in range(2):
                        p0 = HD * g
                        for half in range(2):
                            src = fm[p0:p0 + HD, (KC, VC)[kv], 16 * half:16 * half + 16 * NC] \
                                .rearrange("p (c l) -> p l c", l=16)
                            pos = sm("pos")[p0:p0 + HD, 32 * kv + 16 * half:32 * kv + 16 * half + 16]
                            dve.tensor_tensor(blocks[p0:p0 + HD, 16 * half:16 * half + 16, g, :], src,
                                                   pos.unsqueeze(2).to_broadcast([HD, 16, NC]), ALU.add) \
                                .then_inc(dve_done, seq.step())
                    seq.note(f"cmp.b{kv}")
                dve.wait_ge(dve_done, seq.so_far())
                for i, kt in enumerate((KA, KS, KW)):
                    dve.wait_ge(pe_done, seq.at(f"rk{i}"))
                    dve.tensor_tensor(rot, psum[:, 4 + i, :], sinT, ALU.mult).then_inc(dve_done, seq.step())
                    dve.tensor_tensor(fm[:, kt, :], fm[:, kt, :], cosT, ALU.mult).then_inc(dve_done, seq.step())
                    dve.wait_ge(dve_done, seq.so_far())
                    for g in range(2):
                        p0 = HD * g
                        dve.tensor_tensor(kpad[p0:p0 + HD, i, g, :], fm[p0:p0 + HD, kt, :],
                                               rot[p0:p0 + HD, :], ALU.add).then_inc(dve_done, seq.step())
                    dve.wait_ge(dve_done, seq.so_far())
                with seq.loop("heads", 4) as j:
                    meet("heads")
                    for i, base in enumerate((QA, QB)):
                        dve.wait_ge(pe_done, seq.at(f"rq{i}"))
                        dve.tensor_tensor(rot, psum[:, 5 + i, :], sinT, ALU.mult).then_inc(dve_done, seq.step())
                        dve.tensor_tensor(qs[:, i, :], fm[:, bass.ds(j + base, 1), :]
                                               .rearrange("p o t -> p (o t)"), cosT, ALU.mult) \
                            .then_inc(dve_done, seq.step())
                        dve.wait_ge(dve_done, seq.so_far())
                        dve.tensor_tensor(qs[:, i, :], qs[:, i, :], rot, ALU.add).then_inc(dve_done, seq.step())
                        dve.wait_ge(dve_done, seq.so_far())
                    dve.tensor_copy(gj, gate[:, :, bass.ds(j * 6, 6)]).then_inc(dve_done, seq.step())
                    dve.tensor_copy(sj[:, 0, :], sinks[:, bass.ds(j, 1), :].rearrange("p o g -> p (o g)")) \
                        .then_inc(dve_done, seq.step())
                    dve.wait_ge(dve_done, seq.so_far())
                    dve.tensor_scalar(sj[:, 1, :], sj[:, 0, :], -1.0, None, ALU.mult).then_inc(dve_done, seq.step())
                    dve.wait_ge(dve_done, seq.so_far())
                    seq.note("rq.done")

                    def maxima(u):
                        kind, g, qt, kts = UNITS[u]
                        dve.wait_ge(pe_done, seq.at(f"u{u}.S"))
                        s = psum[:, u % 3, 0:width(u)]
                        if kind == "cmp":
                            m = cc("cmp")[:, NC * qt:NC * (qt + 1)]
                            dve.tensor_tensor(s, s, m, ALU.add).then_inc(dve_done, seq.step())
                        else:
                            d = psum[:, u % 3, width(u) - P:width(u)]
                            dve.tensor_tensor(d, d, cc("causal"), ALU.add).then_inc(dve_done, seq.step())
                            if kind == "A" and qt:
                                d = psum[:, u % 3, 0:P]
                                dve.tensor_tensor(d, d, cc("band"), ALU.add).then_inc(dve_done, seq.step())
                        dve.wait_ge(dve_done, seq.so_far())
                        c = cols[:, u % 4, :]
                        dve.tensor_reduce(c[:, 0:1], s, AX, ALU.max).then_inc(dve_done, seq.step())
                        dve.wait_ge(dve_done, seq.so_far())
                        if kind == "A":
                            dve.tensor_scalar(c[:, 1:2], c[:, 0:1], -SCALE, sj[:, 1, g:g + 1],
                                                   ALU.mult, ALU.min).then_inc(dve_done, seq.step(f"u{u}.m"))
                        else:
                            dve.tensor_scalar(c[:, 1:2], c[:, 0:1], -SCALE, 1e24,
                                                   ALU.mult, ALU.min).then_inc(dve_done, seq.step(f"u{u}.m"))

                    def normalise(u):
                        kind, g, qt, kts = UNITS[u]
                        dve.wait_ge(act_done, seq.at(f"u{u}.e"))
                        c = cols[:, u % 4, :]
                        if kind == "A":
                            dve.tensor_tensor(c[:, 4:5], c[:, 2:3], c[:, 3:4], ALU.add) \
                                .then_inc(dve_done, seq.step())
                            dve.wait_ge(dve_done, seq.so_far())
                            dve.reciprocal(c[:, 6:7], c[:, 4:5]).then_inc(dve_done, seq.step())
                        else:
                            br = {"cmp": 0, "slc": 1, "win": 2}[kind]
                            dve.tensor_scalar(c[:, 4:5], c[:, 2:3], TINY, None, ALU.max) \
                                .then_inc(dve_done, seq.step())
                            dve.wait_ge(dve_done, seq.so_far())
                            dve.reciprocal(c[:, 5:6], c[:, 4:5]).then_inc(dve_done, seq.step())
                            dve.wait_ge(dve_done, seq.so_far())
                            dve.tensor_tensor(c[:, 6:7], c[:, 5:6], gj[:, qt, 3 * g + br:3 * g + br + 1],
                                                   ALU.mult).then_inc(dve_done, seq.step())
                        dve.wait_ge(dve_done, seq.so_far())
                        pb = pbuf[:, u % 3, 0:width(u)]
                        dve.tensor_scalar(pb, pb, c[:, 6:7], None, ALU.mult).then_inc(dve_done, seq.step(f"u{u}.p"))

                    maxima(0)
                    for u in range(NU):
                        if u + 1 < NU:
                            maxima(u + 1)
                        normalise(u)
                meet("branch")
                for r in range(8):
                    a, b = 2 * (r % 2), 2 * (r % 2) + 1
                    dve.wait_ge(slot_used, seq.at(f"branch.t{r}"))
                    dve.tensor_tensor(tmp[:, r % 2, :], psum[:, a, :], siga[:, r, :], ALU.mult) \
                        .then_inc(dve_done, seq.step())
                    dve.tensor_tensor(h[:, r, :], psum[:, b, :], sigb[:, r, :], ALU.mult) \
                        .then_inc(dve_done, seq.step(f"branch.d{r}"))
                    dve.wait_ge(dve_done, seq.so_far())
                    dve.tensor_tensor(h[:, r, :], h[:, r, :], tmp[:, r % 2, :], ALU.add) \
                        .then_inc(dve_done, seq.step())
                meet("out")
                residual("n2", y, 1)
                meet("n3")
                scaled("n3", h, x, 2)
                meet("up")

                def convolve(stage, n, inloop, base):
                    dve.tensor_copy(cj[:, 0:n, :], conv[:, bass.ds(base, n), :] if inloop
                                         else conv[:, base:base + n, :]).then_inc(dve_done, seq.step())
                    dve.wait_ge(dve_done, seq.so_far())

                    def finish(i):
                        dve.wait_ge(act_done, seq.at(f"{stage}.g{i}"))
                        dve.wait_ge(dve_done, seq.so_far())
                        if inloop:
                            dst = big[:, bass.ds(base * (T // 2) + i * T, T)]
                        else:
                            dst = g_ff[:, base // 2 + i, :]
                        dve.tensor_tensor(dst, tmp[:, 4 + i % 2, :], tmp[:, 2 * (i % 2) + 1, :], ALU.mult) \
                            .then_inc(dve_done, seq.step())

                    for r in range(n):
                        pair, half = r // 2, r % 2
                        u, c = U[:, r % 4, :], tmp[:, 2 * (pair % 2) + half, :]
                        w = cj[:, r, :]
                        dve.wait_ge(act_done, seq.at(f"{stage}.d{r}"))
                        dve.wait_ge(dve_done, seq.so_far())
                        dve.tensor_scalar(c, u[:, 2:T + 2], w[:, 2:3], w[:, 3:4], ALU.mult, ALU.add) \
                            .then_inc(dve_done, seq.step())
                        dve.wait_ge(dve_done, seq.so_far())
                        dve.scalar_tensor_tensor(c, u[:, 1:T + 1], w[:, 1:2], c, ALU.mult, ALU.add) \
                            .then_inc(dve_done, seq.step())
                        dve.wait_ge(dve_done, seq.so_far())
                        dve.scalar_tensor_tensor(c, u[:, 0:T], w[:, 0:1], c, ALU.mult, ALU.add) \
                            .then_inc(dve_done, seq.step(f"{stage}.v{r}"))
                        if half == 0:
                            seq.note(f"{stage}.c{pair}")
                        elif pair:
                            finish(pair - 1)
                    finish(n // 2 - 1)
                    dve.wait_ge(dve_done, seq.so_far())

                with seq.loop("up", 5) as i:
                    convolve("up", 8, "up", i * 8)
                meet("up2")
                convolve("up2", 4, None, 40)
                meet("down")
                meet("n4")
                residual("n4", h, 3)
                meet("layer_end")

            def layer_norm(stage, which, rs_):
                g = s2("ln").rearrange("p (a k) -> p a k", k=KD)
                dve.wait_ge(act_done, seq.at(f"{stage}.mu"))
                for k in range(KD):
                    dve.tensor_tensor(x[:, k, :], x[:, k, :], rs_, ALU.subtract) \
                        .then_inc(dve_done, seq.step(f"{stage}.c{k}"))
                dve.wait_ge(act_done, seq.at(f"{stage}.rs"))
                dve.wait_ge(dve_done, seq.so_far())
                for k in range(KD):
                    dve.scalar_tensor_tensor(x[:, k, :], x[:, k, :], g[:, 2 * which, k:k + 1], rs_,
                                                  ALU.mult, ALU.mult).then_inc(dve_done, seq.step())
                dve.wait_ge(dve_done, seq.so_far())
                for k in range(KD):
                    dve.tensor_scalar(x[:, k, :], x[:, k, :], g[:, 2 * which + 1, k:k + 1], None, ALU.add) \
                        .then_inc(dve_done, seq.step())
                seq.note(f"{stage}.x")

            def th(v):
                return v.rearrange("p (t h) -> p t h", h=8)

            def rows(v, n=NT):
                return v.unsqueeze(1).to_broadcast([P, n, v.shape[1]])

            def across(v, w):
                return v.unsqueeze(2).to_broadcast([P, v.shape[1], w])

            def chunks(v):
                return v.rearrange("p (t c) -> p t c", c=P)

            def step(*args, mark=None, op=None):
                op(*args).then_inc(dve_done, seq.step(mark))
                dve.wait_ge(dve_done, seq.so_far())

            meet("ab")
            dve.wait_ge(small_in, seq.at("small2"))
            dve.wait_ge(pe_done, seq.at("ab.t"))
            ab = psum[:, 0, 0:64].rearrange("p (t c) -> p t c", c=16)
            dve.wait_ge(act_done, seq.at("ab.beta"))
            step(th(sc[:, 0, :]), ab[:, :, 8:16], rows(s2("dtb")), ALU.add, op=dve.tensor_tensor)
            step(sc[:, 1, :], sc[:, 0, :], -1.0, None, ALU.mult, op=dve.tensor_scalar)
            step(sc[:, 1, :], sc[:, 1, :], sc[:, 0, :], ALU.max, op=dve.tensor_tensor, mark="ab.abs")
            step(sc[:, 0, :], sc[:, 0, :], 0.0, None, ALU.max, op=dve.tensor_scalar)
            dve.wait_ge(act_done, seq.at("ab.sp"))
            step(sc[:, 0, :], sc[:, 0, :], sc[:, 2, :], ALU.add, op=dve.tensor_tensor)
            step(th(sc[:, 0, :]), th(sc[:, 0, :]), rows(sc[:, 3, 0:8]), ALU.mult, op=dve.tensor_tensor)
            step(bg[:, G, :], sc[:, 0, :], -1.0, None, ALU.mult, op=dve.tensor_scalar, mark="ab.g")
            dve.wait_ge(act_done, seq.at("ab.gcc"))
            dve.wait_ge(act_done, seq.at("ab.egc"))
            step(sc[:, 5, :], psum[:, 1, 32:64], bg[:, GC, :], ALU.subtract, op=dve.tensor_tensor, mark="ab.dif")
            step(bg[:, NBE, :], sc[:, 4, :], bg[:, BETA, :], ALU.mult, op=dve.tensor_tensor)
            step(bg[:, NBE, :], bg[:, NBE, :], -1.0, None, ALU.mult, op=dve.tensor_scalar)
            dve.memset(U3, 0.0).then_inc(dve_done, seq.step())
            meet("dn")
            cw = s2("conv").rearrange("p (t c) -> p t c", c=4)
            with seq.loop("dn", 4) as i:
                dve.wait_ge(dve_done, seq.so_far())
                dve.tensor_copy(cj_dn, cw[:, bass.ds(i * 6, 6), :]).then_inc(dve_done, seq.step())
                dve.wait_ge(dve_done, seq.so_far())
                for r in range(8):
                    if r % 4 == 3:
                        continue
                    u, c, w = U3[:, r % 4, :], cdn[:, r % 4, :], cj_dn[:, 3 * (r // 4) + r % 4, :]
                    dve.wait_ge(act_done, seq.at(f"dn.d{r}"))
                    if r >= 4:
                        dve.wait_ge(act_done, seq.at(f"dn.s{r - 4}"))
                    else:
                        dve.wait_ge(act_done, seq.at(f"dn.s{r + 4}", back="dn"))
                    dve.tensor_scalar(c, u[:, 3:T + 3], w[:, 3:4], None, ALU.mult).then_inc(dve_done, seq.step())
                    for q in (2, 1, 0):
                        dve.wait_ge(dve_done, seq.so_far())
                        dve.scalar_tensor_tensor(c, u[:, q:T + q], w[:, q:q + 1], c, ALU.mult, ALU.add) \
                            .then_inc(dve_done, seq.step(f"dn.v{r}"))
            with seq.loop("delta", 4) as i:
                meet("delta")
                tri, strict = rows(cc("tri")), rows(cc("strictT"))
                levels = cc("levels").rearrange("p (s c) -> p s c", s=7)
                for hh in range(2):
                    b = hb[hh]
                    dve.tensor_copy(b["c"].unsqueeze(3), bg.rearrange("p q (t h) -> p q t h", h=8)
                                         [:, :, :, bass.ds(i * 2 + hh, 1)]).then_inc(dve_done, seq.step())
                dve.wait_ge(dve_done, seq.so_far())
                for hh in range(2):
                    b, c = hb[hh], hb[hh]["c"]
                    dve.tensor_tensor(chunks(b["X"]), tri, across(c[:, G, :], P), ALU.mult) \
                        .then_inc(dve_done, seq.step())
                    dve.tensor_tensor(chunks(b["M"]), rows(ident), across(c[:, BETA, :], P), ALU.mult) \
                        .then_inc(dve_done, seq.step(f"d{hh}.TG"))
                for hh in range(2):
                    b = hb[hh]
                    dve.wait_ge(act_done, seq.at(f"d{hh}.rs"))
                    qkv = lambda c: qkvz[:, bass.ds(i * (8 * T) + (4 * hh + c) * T, T)]
                    dve.scalar_tensor_tensor(b["qn"], qkv(0), P ** -0.5, b["ta"], ALU.mult, ALU.mult) \
                        .then_inc(dve_done, seq.step())
                    dve.tensor_tensor(b["kn"], qkv(1), b["tb"], ALU.mult) \
                        .then_inc(dve_done, seq.step(f"d{hh}.norm"))
                for hh in range(2):
                    b, c = hb[hh], hb[hh]["c"]
                    dve.wait_ge(pe_done, seq.at(f"d{hh}.kT"))
                    dve.wait_ge(pe_done, seq.at(f"d{hh}.vT"))
                    dve.tensor_tensor(chunks(b["kd"]), chunks(psum[:, 4 * hh + 2, :]), across(c[:, EKD, :], P), ALU.mult) \
                        .then_inc(dve_done, seq.step())
                    dve.tensor_tensor(chunks(b["vb"]), chunks(psum[:, 4 * hh + 3, :]), across(c[:, BETA, :], P), ALU.mult) \
                        .then_inc(dve_done, seq.step(f"d{hh}.kv"))
                for hh in range(2):
                    b, c = hb[hh], hb[hh]["c"]
                    dve.wait_ge(act_done, seq.at(f"d{hh}.egb"))
                    dve.tensor_tensor(chunks(b["dm"]), chunks(psum[:, 4 * hh, :]), across(c[:, GC, :], P), ALU.subtract) \
                        .then_inc(dve_done, seq.step())
                    dve.wait_ge(dve_done, seq.so_far())
                    dve.tensor_scalar(b["dm"], b["dm"], 0.0, None, ALU.min) \
                        .then_inc(dve_done, seq.step(f"d{hh}.dif"))
                    dve.tensor_tensor(b["qd"], b["qn"], b["ta"], ALU.mult).then_inc(dve_done, seq.step(f"d{hh}.qd"))
                for hh in range(2):
                    b = hb[hh]
                    dve.wait_ge(act_done, seq.at(f"d{hh}.dec"))
                    dve.wait_ge(pe_done, seq.at(f"d{hh}.KK"))
                    dve.wait_ge(pe_done, seq.at(f"d{hh}.QK"))
                    step(chunks(b["dm"]), chunks(b["dm"]), tri, ALU.mult, op=dve.tensor_tensor)
                    dve.tensor_tensor(b["at"], psum[:, 4 * hh + 3, :], b["dm"], ALU.mult) \
                        .then_inc(dve_done, seq.step())
                    step(chunks(b["lt"]), chunks(b["dm"]), strict, ALU.mult, op=dve.tensor_tensor)
                    step(b["lt"], psum[:, 4 * hh + 1, :], b["lt"], ALU.mult, op=dve.tensor_tensor)
                    step(b["lt"], psum[:, 4 * hh + 2, :], b["lt"], ALU.mult, op=dve.tensor_tensor)
                    step(chunks(b["K"][0]), chunks(b["lt"]), rows(levels[:, 0, :]), ALU.mult,
                         op=dve.tensor_tensor, mark=f"d{hh}.K0")
                    dve.tensor_tensor(chunks(b["K"][1]), chunks(b["lt"]), rows(levels[:, 1, :]), ALU.mult) \
                        .then_inc(dve_done, seq.step(f"d{hh}.K1"))
                    dve.tensor_tensor(chunks(b["X"]), rows(ident), chunks(b["K"][0]), ALU.subtract) \
                        .then_inc(dve_done, seq.step())
                    dve.wait_ge(pe_done, seq.at(f"d{hh}.K0T"))
                    dve.tensor_tensor(chunks(b["M"]), rows(ident), chunks(psum[:, 4 * hh, :]), ALU.subtract) \
                        .then_inc(dve_done, seq.step(f"d{hh}.X0"))
                for lev in range(1, 7):
                    for hh in range(2):
                        b = hb[hh]
                        if lev < 6:
                            if lev >= 2:
                                dve.wait_ge(pe_done, seq.at(f"d{hh}.T{lev - 1}"))
                            dve.tensor_tensor(chunks(b["K"][(lev + 1) % 2]), chunks(b["lt"]),
                                                   rows(levels[:, lev + 1, :]), ALU.mult) \
                                .then_inc(dve_done, seq.step(f"d{hh}.K{lev + 1}"))
                        dve.wait_ge(pe_done, seq.at(f"d{hh}.XT{lev}"))
                        if lev < 6:
                            dve.wait_ge(pe_done, seq.at(f"d{hh}.MT{lev}"))
                            dve.tensor_tensor(b["M"], b["M"], psum[:, 4 * hh + 2, :], ALU.subtract) \
                                .then_inc(dve_done, seq.step())
                        dve.wait_ge(dve_done, seq.so_far())
                        dve.tensor_tensor(b["X"], b["X"], psum[:, 4 * hh + 1, :], ALU.subtract) \
                            .then_inc(dve_done, seq.step(f"d{hh}.X{lev}"))
                for hh in range(2):
                    seq.note(f"d{hh}.R0")
                for t in range(NT):
                    cs = slice(t * P, (t + 1) * P)
                    if t:
                        for hh in range(2):
                            b, c = hb[hh], hb[hh]["c"]
                            dve.wait_ge(pe_done, seq.at(f"d{hh}.kS{t}"))
                            dve.scalar_tensor_tensor(b["R"], psum[:, 4 * hh, 0:P], c[:, NBE, t:t + 1],
                                                          b["vb"][:, cs], ALU.mult, ALU.add) \
                                .then_inc(dve_done, seq.step(f"d{hh}.R{t}"))
                    if t < NT - 1:
                        for hh in range(2):
                            b, c = hb[hh], hb[hh]["c"]
                            dve.wait_ge(pe_done, seq.at(f"d{hh}.dS{t}"))
                            dve.wait_ge(pe_done, seq.at(f"d{hh}.o{t}"))
                            if t:
                                dve.scalar_tensor_tensor(b["S"], b["S"], c[:, EL, t:t + 1], psum[:, 4 * hh + 3, 0:P],
                                                              ALU.mult, ALU.add) \
                                    .then_inc(dve_done, seq.step(f"d{hh}.S{t}"))
                            else:
                                dve.tensor_copy(b["S"], psum[:, 4 * hh + 3, 0:P]) \
                                    .then_inc(dve_done, seq.step(f"d{hh}.S{t}"))
                for hh in range(2):
                    b = hb[hh]
                    dve.wait_ge(act_done, seq.at(f"d{hh}.ors"))
                    dve.scalar_tensor_tensor(b["tb"], psum[:, 4 * hh + 2, :], s2("normw"), b["tb"], ALU.mult, ALU.mult) \
                        .then_inc(dve_done, seq.step())
                    dve.wait_ge(dve_done, seq.so_far())
                    z = qkvz[:, bass.ds(i * (8 * T) + (4 * hh + 3) * T, T)]
                    dve.tensor_tensor(z, z, b["tb"], ALU.mult).then_inc(dve_done, seq.step())
            meet("wo")

            def add_mix(stage, r, ps):
                dve.scalar_tensor_tensor(x[:, r, :], x[:, r, :], ALPHA, ps, ALU.mult, ALU.add) \
                    .then_inc(dve_done, seq.step(f"{stage}.r{r}"))

            for r in range(8):
                dve.wait_ge(slot_used, seq.at(f"wo.t{r}"))
                add_mix("l0", r, psum[:, r % 4, :])
                seq.note(f"wo.d{r}")
            layer_norm("l0", 0, rs2)

            def experts(m, which):
                meet(f"{m}.route")
                dve.wait_ge(act_done, seq.at(f"{m}.lgs"))
                TT, TS = dve.tensor_tensor, dve.tensor_scalar
                gl, el = lg[:, :, 0:NG], lg[:, :, NG:NG + NE]
                def col(i):
                    return rc[:, i, :]
                def reduce(dst, src, op):
                    dve.tensor_reduce(dst, src, AX, op).then_inc(dve_done, seq.step())
                    dve.wait_ge(dve_done, seq.so_far())
                g0, g1, g2, g3 = (rt[i][:, :, 0:NG] for i in range(4))
                reduce(col(0), gl, ALU.max)
                step(g0, gl, across(col(0), NG), ALU.subtract, op=TT, mark=f"{m}.ge")
                step(g2, gl, across(col(0), NG), ALU.is_equal, op=TT)
                step(g2, g2, rows(cc("iota8")[:, 0:NG]), ALU.mult, op=TT)
                reduce(col(3), g2, ALU.max)
                step(g2, g2, across(col(3), NG), ALU.is_equal, op=TT)
                step(g3, g2, 1.0, BIG, ALU.subtract, ALU.mult, op=TS)
                dve.wait_ge(act_done, seq.at(f"{m}.gx"))
                reduce(col(1), g1, ALU.add)
                dve.reciprocal(col(2), col(1)).then_inc(dve_done, seq.step())
                dve.wait_ge(dve_done, seq.so_far())
                for g in range(NG):
                    cs = slice(g * EPG, (g + 1) * EPG)
                    step(rt[4][:, :, cs], el[:, :, cs], g2[:, :, g:g + 1].to_broadcast([P, NT, EPG]), ALU.mult, op=TT)
                    step(rt[4][:, :, cs], rt[4][:, :, cs], g3[:, :, g:g + 1].to_broadcast([P, NT, EPG]), ALU.add, op=TT)
                for c in range(2):
                    oh = rt[c]
                    reduce(col(4 + c), rt[4], ALU.max)
                    step(oh, rt[4], across(col(4 + c), NE), ALU.is_equal, op=TT)
                    step(oh, oh, rows(cc("iota32")), ALU.mult, op=TT)
                    reduce(col(6 + c), oh, ALU.max)
                    step(oh, oh, across(col(6 + c), NE), ALU.is_equal, op=TT)
                    if c == 0:
                        flat = lambda v: v.rearrange("p t c -> p (t c)")
                        step(flat(rt[4]), flat(oh), -3 * BIG, flat(rt[4]), ALU.mult, ALU.add,
                             op=dve.scalar_tensor_tensor)
                step(rt[2], rt[0], rt[1], ALU.add, op=TT, mark=f"{m}.chosen")
                step(col(8), col(5), col(4), ALU.subtract, op=TT, mark=f"{m}.d")
                dve.wait_ge(act_done, seq.at(f"{m}.e2"))
                step(col(10), col(9), 1.0, None, ALU.add, op=TS)
                dve.reciprocal(col(11), col(10)).then_inc(dve_done, seq.step())
                dve.wait_ge(dve_done, seq.so_far())
                step(col(12), col(2), col(11), ALU.mult, op=TT)
                step(col(13), col(12), col(9), ALU.mult, op=TT)
                dve.wait_ge(pe_done, seq.at(f"{m}.rank"))
                rank = psum[:, 1, 0:NT * NE].rearrange("p (t c) -> p t c", c=NE)
                count, n_jobs, ends, starts = (psum[:, 2, 0:NE], *(rt[5][:, q, :] for q in range(3)))
                step(n_jobs, count, 1.0, None, ALU.is_ge, op=TS)
                for n in (1, 2, 3):
                    step(starts, count, float(n * P + 1), None, ALU.is_ge, op=TS)
                    step(n_jobs, n_jobs, starts, ALU.add, op=TT)
                step(ends, ones[:, 0:NE], n_jobs, 0.0, ALU.mult, ALU.add, op=dve.tensor_tensor_scan)
                step(starts, ends, n_jobs, ALU.subtract, op=TT)
                step(jwork, cc("jobs").unsqueeze(2).to_broadcast([P, JOBS, NE]),
                     ends.unsqueeze(1).to_broadcast([P, JOBS, NE]), ALU.is_ge, op=TT)
                reduce(jobs, jwork, ALU.add)
                step(jobs, jobs, float(NE - 1), None, ALU.min, op=TS)
                dve.tensor_copy(idx.bitcast(I32), jobs).then_inc(dve_done, seq.step())
                dve.wait_ge(dve_done, seq.so_far())
                step(jobs.bitcast(I32), idx.bitcast(I32), op=dve.tensor_copy)
                step(rc[:, 20, 0:1], ends[:, NE - 1:NE], 1.0, None, ALU.add, op=TS)
                step(rnd[:, 1:2].bitcast(I32), rc[:, 20, 0:1], op=dve.tensor_copy)
                step(rnd[:, 0:1].bitcast(I32), rnd[:, 1:2].bitcast(I32), 1, None, ALU.logical_shift_right,
                     op=TS, mark=f"{m}.rnd")
                for c in range(2):
                    rk, a, b_ = col(14 + c), col(16), col(17)
                    step(rt[3], rank, rt[c], ALU.mult, op=TT)
                    reduce(rk, rt[3], ALU.add)
                    step(a, rk, float(P), None, ALU.is_ge, op=TS)
                    for n in (2, 3):
                        step(b_, rk, float(n * P), None, ALU.is_ge, op=TS)
                        step(a, a, b_, ALU.add, op=TT)
                    step(rt[3], rows(starts), rt[c], ALU.mult, op=TT)
                    reduce(b_, rt[3], ALU.add)
                    step(b_, rk, float(JOBS), b_, ALU.mult, ALU.add, op=dve.scalar_tensor_tensor)
                    step(b_, a, -float(P * JOBS - 1), b_, ALU.mult, ALU.add, op=dve.scalar_tensor_tensor)
                    dve.tensor_copy(dest[:, c, :].bitcast(I32), b_).then_inc(dve_done, seq.step(f"{m}.dest"))
                    dve.wait_ge(dve_done, seq.so_far())
                rounds = seq.count_of(rnd[0:1, 0:1].bitcast(I32), 1, ROUNDS_MAX)
                meet(f"{m}.ex")
                L = f"{m}.ex"

                def x_out(ee, mark):
                    for half in range(2):
                        dve.tensor_copy(xT[:, ee].rearrange("p k c -> p (k c)")[:, 512 * half:512 * half + 512],
                                             psum[:, half, :]).then_inc(dve_done, seq.step(f"{m}.{mark}"))

                dve.wait_ge(pe_done, seq.at(f"{m}.Tpre"))
                x_out(0, "xTpre")
                with seq.rounds(L, rounds):
                    for ee in range(2):
                        dve.wait_ge(slot_used, seq.at(f"{m}.g{ee}"))
                        dve.wait_ge(act_done, seq.at(f"{m}.sg{ee}"))
                        TT(hs[:, ee, :], sg[:, ee, :], psum[:, 3, :], ALU.mult) \
                            .then_inc(dve_done, seq.step(f"{m}.hs{ee}"))
                        if ee:
                            dve.wait_ge(pe_done, seq.at(f"{m}.T0n"))
                            x_out(0, "xT0n")
                        else:
                            dve.wait_ge(pe_done, seq.at(f"{m}.T1"))
                            x_out(1, "xT1")
                        dve.wait_ge(slot_used, seq.at(f"{m}.z{ee}"))
                        dve.wait_ge(rows_scattered[ee], seq.at(f"{m}.sc{ee}", back=L))
                        dve.tensor_copy(ym[:, ee, 512:D], psum[:, 6, :]).then_inc(dve_done, seq.step(f"{m}.yd{ee}"))
                meet(f"{m}.back")
                for t in range(NT):
                    dve.wait_ge(rows_back[t % 2], seq.at(f"{m}.y2{t}"))
                    step(yt[:, t, :], y2[:, t % 2, 0, :], col(12)[:, t:t + 1], None, ALU.mult, op=TS)
                    dve.scalar_tensor_tensor(yt[:, t, :], y2[:, t % 2, 1, :], col(13)[:, t:t + 1], yt[:, t, :],
                                                  ALU.mult, ALU.add).then_inc(dve_done, seq.step(f"{m}.yt{t}"))
                for k in range(KD):
                    dve.wait_ge(pe_done, seq.at(f"{m}.f{k}"))
                    add_mix(m, k, psum[:, k % 4, :])
                layer_norm(m, which, rs4)

            experts("m0", 1)
            meet("kda")
            meet("vda")
            meet("qda")
            LAM_INIT = 0.8 - 0.6 * math.exp(-0.3 * 1)
            lp = s2("lam").rearrange("p (a b d) -> p a b d", a=2, b=2)
            dve.memset(qz, 0.0).then_inc(dve_done, seq.step())
            step(lam[:, 0:128].rearrange("p (a d) -> p a d", a=2), lp[:, :, 0, :], lp[:, :, 1, :], ALU.mult,
                 op=dve.tensor_tensor)
            dve.tensor_reduce(lam[:, 130:132], lam[:, 0:128].rearrange("p (a d) -> p a d", a=2), AX, ALU.add) \
                .then_inc(dve_done, seq.step("lam.s"))
            dve.wait_ge(act_done, seq.at("lam.e"))
            step(lam[:, 134:135], lam[:, 133:134], lam[:, 132:133], ALU.subtract, op=dve.tensor_tensor)
            step(lam[:, 134:135], lam[:, 134:135], -LAM_INIT, None, ALU.add, op=dve.tensor_scalar)
            step(lam[:, 135:136], s2("subln"), 1.0 - LAM_INIT, None, ALU.mult, op=dve.tensor_scalar)
            with seq.loop("da", 4) as j:
                meet("da")
                for hh in range(2):
                    dve.tensor_copy(va_h[:, hh], vda[:, :, bass.ds(j * (2 * P) + hh * P, P)]) \
                        .then_inc(dve_done, seq.step())
                seq.note("da.v")

                def maxima2(u):
                    w = (u % 4 + 1) * P
                    dve.wait_ge(pe_done, seq.at(f"a{u}.S"))
                    c = dcols[:, u % 4, :]
                    banks = psum[:, 2 * (u % 2):2 * (u % 2) + 2, :]
                    dve.tensor_tensor(banks[:, :, w - P:w], banks[:, :, w - P:w], rows(cc("causal"), 2), ALU.add) \
                        .then_inc(dve_done, seq.step())
                    dve.wait_ge(dve_done, seq.so_far())
                    dve.tensor_reduce(c[:, 0:2], banks[:, :, 0:w], AX, ALU.max).then_inc(dve_done, seq.step())
                    dve.wait_ge(dve_done, seq.so_far())
                    dve.tensor_scalar(c[:, 2:4], c[:, 0:2], -SCALE, None, ALU.mult) \
                        .then_inc(dve_done, seq.step(f"a{u}.m"))

                def combine(u):
                    w = (u % 4 + 1) * P
                    dve.wait_ge(act_done, seq.at(f"a{u}.e"))
                    c = dcols[:, u % 4, :]
                    p0, p1 = pda[:, 2 * (u % 3), 0:w], pda[:, 2 * (u % 3) + 1, 0:w]
                    dve.reciprocal(c[:, 6:8], c[:, 4:6]).then_inc(dve_done, seq.step())
                    dve.wait_ge(dve_done, seq.so_far())
                    dve.tensor_tensor(c[:, 8:9], c[:, 7:8], lam[:, 134:135], ALU.mult) \
                        .then_inc(dve_done, seq.step())
                    dve.tensor_scalar(p0, p0, c[:, 6:7], None, ALU.mult).then_inc(dve_done, seq.step())
                    dve.wait_ge(dve_done, seq.so_far())
                    dve.scalar_tensor_tensor(p0, p1, c[:, 8:9], p0, ALU.mult, ALU.add) \
                        .then_inc(dve_done, seq.step(f"a{u}.p"))

                maxima2(0)
                for u in range(8):
                    if u + 1 < 8:
                        maxima2(u + 1)
                    combine(u)
            meet("dan")
            for hd_ in range(8):
                dve.wait_ge(act_done, seq.at(f"dan.rs{hd_}"))
                dve.scalar_tensor_tensor(oda[:, hd_, :], oda[:, hd_, :], lam[:, 135:136], sq3[:, hd_, :],
                                              ALU.mult, ALU.mult).then_inc(dve_done, seq.step("dan.o"))
            meet("wo2")
            for r in range(8):
                dve.wait_ge(slot_used, seq.at(f"wo2.t{r}"))
                add_mix("l1", r, psum[:, r % 4, :])
                seq.note(f"wo2.d{r}")
            layer_norm("l1", 2, rs3)
            experts("m1", 3)
            seq.note("result")


def constants():
    c = np.zeros((P, CC_COLS), np.float32)
    def put(name, a):
        c[:, CC[name][0]:CC[name][1]] = a
    i = np.arange(P)
    put("ident", np.eye(P))
    put("ones", np.ones((P, P)))
    perm = np.zeros((P, P))
    for m in range(P):
        b, r = m // HD * HD, m % HD
        if r < HD // 2:
            perm[b + r + HD // 2, m] = -1.0
        else:
            perm[b + r - HD // 2, m] = 1.0
    put("perm", perm)
    put("tri", i[:, None] <= i[None, :])
    put("causal", np.where(i[None, :] <= i[:, None], 0.0, -BIG))
    put("band", np.where(i[None, :] > i[:, None], 0.0, -BIG))
    t = np.arange(NT)[None, :, None] * P + i[:, None, None]
    end = np.arange(NC)[None, None, :] * 16 + 31
    put("cmp", np.where(end <= t, 0.0, -BIG).reshape(P, -1))
    put("strictT", i[:, None] < i[None, :])
    lev = np.zeros((P, 7, P))
    for s in range(7):
        w = 1 << s
        lev[:, s, :] = (i[:, None] // (2 * w) == i[None, :] // (2 * w)) & (i[:, None] // w < i[None, :] // w)
    put("levels", lev.reshape(P, -1))
    inv = 10000.0 ** (-np.arange(HD // 2, dtype=np.float32) / np.float32(HD // 2))
    put("invf", np.tile(inv.astype(np.float32), 4)[:, None])
    put("eps", EPS)
    put("lneps", LN_EPS)
    put("one", 1.0)
    put("iota8", 8.0 - np.arange(8)[None, :])
    put("jobs", np.arange(JOBS)[None, :])
    put("iota32", 32.0 - np.arange(32)[None, :])
    return c


def by_feature(w):
    k, c = w.shape
    return w.reshape(k // P, P, c // P, P).transpose(2, 1, 0, 3).reshape(c // P, P, -1)


def by_token(w, width=512):
    k, c = w.shape
    full = np.zeros((k, width), w.dtype)
    full[:, :c] = w
    return full.reshape(k // (2 * P), 2, P, width).transpose(0, 2, 1, 3).reshape(k // (2 * P), P, -1)


def head_pairs(w, axis):
    s = list(w.shape)
    split = w.reshape(s[:axis] + [2, 4, HD] + s[axis + 1:])
    return np.swapaxes(split, axis, axis + 1).reshape(s)


def lay_out(a):
    slots, smalls = [], []
    for l in range(LAYERS):
        w = a["w_in"][l]
        qa, ka, va, qb, kcb, vcb, ksb, vsb, kwb, vwb, gn, ga, gb = np.split(
            w, np.cumsum([512, 128, 128, 512, 128, 128, 128, 128, 128, 128, 24, 1024])[:12], axis=1)
        slots += [by_feature(ga), by_feature(gb), by_feature(head_pairs(qa, 1)), by_feature(ka),
                  by_feature(head_pairs(qb, 1)), by_feature(ksb), by_feature(kwb), by_feature(kcb), by_feature(vcb)]
        gn = gn.reshape(D, 2, 4, 3).transpose(0, 2, 1, 3).reshape(D, 24)
        slots.append(by_token(np.concatenate([va, vsb, vwb, gn], axis=1)))
        for kv in range(2):
            w1 = a["cmp_w1"][l, kv].reshape(4, 8, HD, P).transpose(0, 2, 1, 3).reshape(4, HD, D)
            slots.append(np.concatenate([w1, w1], axis=1))
        ba = by_feature(head_pairs(a["w_branch_a"][l], 0))
        bb = by_feature(head_pairs(a["w_branch_b"][l], 0))
        slots.append(np.concatenate([ba, bb], axis=2))
        slots.append(by_feature(a["w_out"][l]))
        up = by_feature(a["ffn_w_up"][l]).reshape(2, PAIRS, P, D).transpose(1, 0, 2, 3).reshape(2 * PAIRS, P, D)
        slots.append(up)
        for half in range(2):
            slots.append(by_token(a["ffn_w_down"][l][:, 512 * half:512 * half + 512]))
        slots.append(np.zeros((LAYER_PAD, P, D), np.float32))
        s = np.zeros((P, SM_COLS), np.float32)
        def put(name, v):
            s[:, SM[name][0]:SM[name][1]] = v
        gains = np.stack([a[n][l] for n in ("attn_pre_gain", "attn_post_gain", "ffn_pre_gain", "ffn_post_gain")])
        put("gains", gains.reshape(4, KD, P).transpose(2, 0, 1).reshape(P, -1))
        put("sinks", a["attn_sinks"][l].reshape(2, 4).T.reshape(1, 8))
        cw = np.concatenate([a["ffn_conv_w"][l], a["ffn_conv_b"][l][None]], axis=0)
        put("conv", cw.reshape(4, 2, PAIRS, P).transpose(3, 2, 1, 0).reshape(P, -1))
        put("b1", a["cmp_b1"][l].T)
        pos = a["cmp_pos_emb"][l].transpose(2, 0, 1).reshape(HD, 64)
        put("pos", np.concatenate([pos, pos], axis=0))
        for name, kv in (("w2k", 0), ("w2v", 1)):
            w2 = np.zeros((P, 2, P), np.float32)
            w2[:, 0, :HD] = a["cmp_w2"][l, kv]
            w2[:, 1, HD:] = a["cmp_w2"][l, kv]
            put(name, w2.reshape(P, -1))
        smalls.append(s)
    w = a["a_w_in_2"][0]
    heads = by_feature(w[:, :4 * D]).reshape(4, DH, P, D).transpose(1, 0, 2, 3).reshape(4 * DH, P, D)
    slots += [heads, by_feature(a["a_w_out_2"][0]), by_feature(a["kv_w_2"][:, :D])]
    slots += [by_token(a["kv_w_2"][:, D + 512 * half:D + 512 * half + 512]) for half in range(2)]
    slots += [by_feature(a["b_w_q_2"][0]), by_feature(a["b_w_out_2"][0])]
    s2 = np.zeros((P, S2_COLS), np.float32)
    def put2(name, v):
        s2[:, S2[name][0]:S2[name][1]] = v
    put2("ab", w[:, 4 * D:].reshape(KD, P, 16).transpose(1, 0, 2).reshape(P, -1))
    put2("conv", a["a_conv_w_2"][0].reshape(4, 3, DH, P).transpose(3, 2, 1, 0).reshape(P, -1))
    put2("alog", a["a_a_log_2"][0][None])
    put2("dtb", a["a_dt_bias_2"][0][None])
    put2("normw", a["a_norm_w_2"][0][:, None])
    ln = np.stack([a[n][l] for l in range(LAYERS) for n in ("ln_mix_g_2", "ln_mix_b_2", "ln_ffn_g_2", "ln_ffn_b_2")])
    put2("ln", ln.reshape(8, KD, P).transpose(2, 0, 1).reshape(P, -1))
    router = np.concatenate([a["moe_w_group_2"], a["moe_w_expert_2"]], axis=2)
    put2("router", router.reshape(LAYERS, KD, P, 36).transpose(2, 0, 1, 3).reshape(P, -1))
    put2("lam", a["b_lambda_2"][0].reshape(1, -1))
    put2("subln", a["b_subln_w_2"][0][:, None])
    row = np.arange(P)[:, None, None] + P * np.arange(NT)[None, None, :]
    ids = (2 * row + np.arange(2)[None, :, None]).reshape(P, 8).astype(np.int32)
    return {
        "small2": s2,
        "ids": ids,
        "oob": np.full((P, JOBS), 1 << 20, np.int32),
        "moe_w13": a["moe_w13_2"].reshape(-1, 2 * EFF),
        "moe_w2": a["moe_w2_2"].reshape(-1, D),
        "wstream": np.concatenate(slots, axis=0),
        "small": np.stack(smalls),
        "const": constants(),
        "positions": np.broadcast_to(a["positions"][0][None, :], (P, T)).copy(),
        "xT": a["x"][0].T.reshape(KD, P, T).transpose(1, 0, 2).copy(),
    }


def lay_out(a):
    slots, smalls = [], []
    for l in range(LAYERS):
        w = a["w_in"][l]
        qa, ka, va, qb, kcb, vcb, ksb, vsb, kwb, vwb, gn, ga, gb = np.split(
            w, np.cumsum([512, 128, 128, 512, 128, 128, 128, 128, 128, 128, 24, 1024])[:12], axis=1)
        slots += [by_feature(ga), by_feature(gb), by_feature(head_pairs(qa, 1)), by_feature(ka),
                  by_feature(head_pairs(qb, 1)), by_feature(ksb), by_feature(kwb), by_feature(kcb), by_feature(vcb)]
        gn = gn.reshape(D, 2, 4, 3).transpose(0, 2, 1, 3).reshape(D, 24)
        slots.append(by_token(np.concatenate([va, vsb, vwb, gn], axis=1)))
        for kv in range(2):
            w1 = a["cmp_w1"][l, kv].reshape(4, 8, HD, P).transpose(0, 2, 1, 3).reshape(4, HD, D)
            slots.append(np.concatenate([w1, w1], axis=1))
        ba = by_feature(head_pairs(a["w_branch_a"][l], 0))
        bb = by_feature(head_pairs(a["w_branch_b"][l], 0))
        slots.append(np.concatenate([ba, bb], axis=2))
        slots.append(by_feature(a["w_out"][l]))
        up = by_feature(a["ffn_w_up"][l]).reshape(2, PAIRS, P, D).transpose(1, 0, 2, 3).reshape(2 * PAIRS, P, D)
        slots.append(up)
        for half in range(2):
            slots.append(by_token(a["ffn_w_down"][l][:, 512 * half:512 * half + 512]))
        slots.append(np.zeros((LAYER_PAD, P, D), np.float32))
        s = np.zeros((P, SM_COLS), np.float32)
        def put(name, v):
            s[:, SM[name][0]:SM[name][1]] = v
        gains = np.stack([a[n][l] for n in ("attn_pre_gain", "attn_post_gain", "ffn_pre_gain", "ffn_post_gain")])
        put("gains", gains.reshape(4, KD, P).transpose(2, 0, 1).reshape(P, -1))
        put("sinks", a["attn_sinks"][l].reshape(2, 4).T.reshape(1, 8))
        cw = np.concatenate([a["ffn_conv_w"][l], a["ffn_conv_b"][l][None]], axis=0)
        put("conv", cw.reshape(4, 2, PAIRS, P).transpose(3, 2, 1, 0).reshape(P, -1))
        put("b1", a["cmp_b1"][l].T)
        pos = a["cmp_pos_emb"][l].transpose(2, 0, 1).reshape(HD, 64)
        put("pos", np.concatenate([pos, pos], axis=0))
        for name, kv in (("w2k", 0), ("w2v", 1)):
            w2 = np.zeros((P, 2, P), np.float32)
            w2[:, 0, :HD] = a["cmp_w2"][l, kv]
            w2[:, 1, HD:] = a["cmp_w2"][l, kv]
            put(name, w2.reshape(P, -1))
        smalls.append(s)
    w = a["a_w_in_2"][0]
    heads = by_feature(w[:, :4 * D]).reshape(4, DH, P, D).transpose(1, 0, 2, 3).reshape(4 * DH, P, D)
    slots += [heads, by_feature(a["a_w_out_2"][0]), by_feature(a["kv_w_2"][:, :D])]
    slots += [by_token(a["kv_w_2"][:, D + 512 * half:D + 512 * half + 512]) for half in range(2)]
    slots += [by_feature(a["b_w_q_2"][0]), by_feature(a["b_w_out_2"][0])]
    s2 = np.zeros((P, S2_COLS), np.float32)
    def put2(name, v):
        s2[:, S2[name][0]:S2[name][1]] = v
    put2("ab", w[:, 4 * D:].reshape(KD, P, 16).transpose(1, 0, 2).reshape(P, -1))
    put2("conv", a["a_conv_w_2"][0].reshape(4, 3, DH, P).transpose(3, 2, 1, 0).reshape(P, -1))
    put2("alog", a["a_a_log_2"][0][None])
    put2("dtb", a["a_dt_bias_2"][0][None])
    put2("normw", a["a_norm_w_2"][0][:, None])
    ln = np.stack([a[n][l] for l in range(LAYERS) for n in ("ln_mix_g_2", "ln_mix_b_2", "ln_ffn_g_2", "ln_ffn_b_2")])
    put2("ln", ln.reshape(8, KD, P).transpose(2, 0, 1).reshape(P, -1))
    router = np.concatenate([a["moe_w_group_2"], a["moe_w_expert_2"]], axis=2)
    put2("router", router.reshape(LAYERS, KD, P, 36).transpose(2, 0, 1, 3).reshape(P, -1))
    put2("lam", a["b_lambda_2"][0].reshape(1, -1))
    put2("subln", a["b_subln_w_2"][0][:, None])
    row = np.arange(P)[:, None, None] + P * np.arange(NT)[None, None, :]
    ids = (2 * row + np.arange(2)[None, :, None]).reshape(P, 8).astype(np.int32)
    return {
        "small2": s2,
        "ids": ids,
        "oob": np.full((P, JOBS), 1 << 20, np.int32),
        "moe_w13": a["moe_w13_2"].reshape(-1, 2 * EFF),
        "moe_w2": a["moe_w2_2"].reshape(-1, D),
        "wstream": np.concatenate(slots, axis=0),
        "small": np.stack(smalls),
        "const": constants(),
        "positions": np.broadcast_to(a["positions"][0][None, :], (P, T)).copy(),
        "xT": a["x"][0].T.reshape(KD, P, T).transpose(1, 0, 2).copy(),
    }


def kernel(**inputs):
    import concourse.bacc as bacc
    from concourse.bass_utils import run_bass_kernel_spmd

    arrays = lay_out({n: np.asarray(v) for n, v in inputs.items()})
    book = Book()
    for _ in range(3):
        nc = bacc.Bacc("TRN2", target_bir_lowering=False, num_devices=1)
        ins = {n: nc.dram_tensor("in_" + n, v.shape, mybir.dt.from_np(v.dtype), kind="ExternalInput").ap()
               for n, v in arrays.items()}
        out = nc.dram_tensor("result", (P, KD, T), F32, kind="ExternalOutput").ap()
        new = Book()
        build(nc, ins, out, book, new)
        book = new
    r = run_bass_kernel_spmd(nc, [{"in_" + n: v for n, v in arrays.items()}], core_ids=[0])
    result = r.results[0]["result"]
    return result.transpose(1, 0, 2).reshape(D, T).T[None].copy()
```

```python
from contextlib import ExitStack, contextmanager
import math

import numpy as np
import concourse.bass as bass
from concourse import mybir

F32 = mybir.dt.float32
I32 = mybir.dt.int32
U32 = mybir.dt.uint32
F32R = mybir.dt.float32r
ALU = mybir.AluOpType
ACT = mybir.ActivationFunctionType
AX = mybir.AxisListType.X

P = 128
T = 512
NT = T // P
D = 1024
KD = D // P
LAYERS = 2
HD = 64
R = 8
HIGHS = 2
FF = 2816
PAIRS = FF // P
NC = 31
BIG = 1e30
TINY = 1e-30
EPS = 1e-6
LN_EPS = 1e-5
ALPHA = (2 * LAYERS) ** 0.25
SCALE = HD ** -0.5

QA, KA, QB, KS, KW, KC, VC, NFM = 0, 4, 5, 9, 10, 11, 12, 13
GATE_C, TM_COLS = 384, 408
S_LAYER = [13, 16, 4, 8, 8, 8, 2 * PAIRS, PAIRS]
LAYER_SLOTS = -(-sum(S_LAYER) // R) * R
LAYER_PAD = LAYER_SLOTS - sum(S_LAYER)

DH = 8
NG, EPG, NE = 4, 8, 32
JOBS = 48
ROUNDS_MAX = 20
EFF = 512

SM = {}
_o = 0
for _n, _w in (("gains", 32), ("sinks", 8), ("conv", 4 * 2 * PAIRS), ("b1", 2), ("pos", 64),
               ("w2k", 256), ("w2v", 256)):
    SM[_n] = (_o, _o + _w)
    _o += _w
SM_COLS = _o
S2 = {}
_o = 0
for _n, _w in (("ab", 8 * 16), ("conv", 24 * 4), ("alog", 8), ("dtb", 8), ("normw", 1), ("ln", 64),
               ("router", 2 * 8 * 36), ("lam", 4 * HD), ("subln", 1)):
    S2[_n] = (_o, _o + _w)
    _o += _w
S2_COLS = _o
CC = {}
_o = 0
for _n, _w in (("ident", 128), ("ones", 128), ("perm", 128), ("tri", 128), ("causal", 128),
               ("band", 128), ("cmp", 4 * NC), ("strictT", 128), ("levels", 7 * 128),
               ("invf", 1), ("eps", 1), ("lneps", 1), ("one", 1), ("iota8", 8), ("iota32", 32), ("jobs", 48)):
    CC[_n] = (_o, _o + _w)
    _o += _w
CC_COLS = _o


class Book:

    def __init__(self):
        self.marks, self.per, self.count = {}, {}, {}


class Sequence:

    def __init__(self, eng, settled, old, new, *channels):
        self.eng, self.settled, self.old, self.new = eng, settled, old, new
        self.n = {c: 0 for c in channels}
        self.chief, self.loops = channels[0], []
        self.passed, self.extra = [], {}

    def step(self, mark=None, ch=None, inc=1):
        ch = ch or self.chief
        self.n[ch] = self.n.get(ch, 0) + inc
        if mark:
            self.new.marks[mark] = {ch: (self.n[ch], [name for name, _ in self.loops], list(self.passed))}
        return inc

    def note(self, mark):
        self.new.marks[mark] = {ch: (n, [name for name, _ in self.loops], list(self.passed))
                                for ch, n in self.n.items() if not ch.startswith("dma")}

    def value(self, ch, n, loops, passed, back=None):
        active = dict(self.loops)
        total, moving = n, None
        for name in list(passed) + list(loops):
            per = self.old.per.get((ch, name), 0)
            if name == back:
                total -= per
            if not per:
                continue
            if name in active:
                more = active[name] * per
            elif name in self.extra:
                more = self.extra[name] * per
            else:
                total += (self.old.count.get(name, 1) - 1) * per
                continue
            moving = more if moving is None else moving + more
        assert total > 0, (ch, n)
        return total if moving is None else moving + total

    def at(self, mark, of=None, back=None, first=False):
        counts = self.old.marks.get(mark)
        if counts is None:
            return 1
        ch = of or next(iter(counts))
        n, loops, passed = counts[ch]
        return self.value(ch, n, [] if first else loops, passed, back)

    def so_far(self, ch=None):
        ch = ch or self.chief
        return self.value(ch, self.n[ch], [name for name, _ in self.loops], self.passed)

    def following(self, ch, plus=1):
        return self.value(ch, self.n[ch] + plus, [name for name, _ in self.loops], self.passed)

    def arrival(self, ch):
        n = self.n[ch]
        value, moving = 16 * (n // R), None
        for name, v in self.loops + [(name, self.extra[name]) for name in self.passed]:
            per = self.old.per.get((ch, name), 0)
            if per:
                assert per % R == 0, name
                moving = v * (16 * per // R) if moving is None else moving + v * (16 * per // R)
        return n % R, value if moving is None else moving + value

    @contextmanager
    def loop(self, name, count):
        start = dict(self.n)
        self.eng.sem_inc(self.settled, 1)
        with self.eng.Fori(0, count) as v:
            self.loops.append((name, v))
            yield v
            self.loops.pop()
        self.new.count[name] = count
        for ch, n in self.n.items():
            per = n - start.get(ch, 0)
            self.new.per[(ch, name)] = per
            self.n[ch] = start.get(ch, 0) + per * count

    def count_of(self, tile, low, high):
        self.eng.sem_inc(self.settled, 1)
        return self.eng.value_load(tile, min_val=low, max_val=high)

    @contextmanager
    def rounds(self, name, count):
        start = dict(self.n)
        self.eng.sem_inc(self.settled, 1)
        self.extra[name] = self.eng.snap(count - 1)
        with self.eng.Fori(0, count) as v:
            self.loops.append((name, v))
            yield v
            self.loops.pop()
        self.new.count[name] = 1
        for ch, n in self.n.items():
            self.new.per[(ch, name)] = n - start.get(ch, 0)
        self.passed.append(name)


def build(nc, ins, out, old, new):
    ctx = ExitStack()
    with ctx:
        def sb(name, shape, dt=F32):
            return ctx.enter_context(nc.sbuf_tensor(name, shape, dt))

        def semaphore(name):
            return ctx.enter_context(nc.semaphore(name))

        pe_done, act_done, dve_done, pool_done = (semaphore(n) for n in ("pe_done", "act_done", "dve_done", "pool_done"))
        slot_used = semaphore("slot_used")
        weights_cast, weights_split = semaphore("weights_cast"), semaphore("weights_split")
        settled = semaphore("settled")
        const_in, positions_in, x_in, small_in, ids_in, result_out = (
            semaphore(n) for n in ("const_in", "positions_in", "x_in", "small_in", "ids_in", "result_out"))
        numbers_placed, table_read = semaphore("numbers_placed"), semaphore("table_read")
        table_filled, rows_gathered, rows_scattered, rows_written, rows_back = (
            [semaphore(f"{n}{i}") for i in range(2)]
            for n in ("table_filled", "rows_gathered", "rows_scattered", "rows_written", "rows_back"))
        slot_in = [semaphore(f"slot_in{r}") for r in range(R)]
        psum = ctx.enter_context(nc.psum_tensor("psum", [P, 8, 512], F32))

        const = sb("const", [P, CC_COLS])
        def cc(name):
            return const[:, CC[name][0]:CC[name][1]]
        ident, ones, perm = cc("ident"), cc("ones"), cc("perm")
        small = sb("small", [P, max(SM_COLS, S2_COLS)])
        ids = sb("ids", [P, 8], I32)
        scratch = sb("scratch", [P, 4, 8], I32)
        def s2(name):
            return small[:, S2[name][0]:S2[name][1]]
        def sm(name):
            return small[:, SM[name][0]:SM[name][1]]
        gains = sm("gains").rearrange("p (a k) -> p a k", a=4)
        sinks = sm("sinks").rearrange("p (j g) -> p j g", j=4)
        conv = sm("conv").rearrange("p (t c) -> p t c", c=4)

        ring = sb("ring", [P, R, D])
        ring_r = nc.alloc_sbuf_tensor_at("ring_rounded", [P, R * D], F32R, offset=nc.sbuf_base - 4 * R * D) \
            .rearrange("p (a c) -> p a c", a=R)
        x = sb("x", [P, KD, T])
        ARENA = 37704
        arena = sb("arena", [P, ARENA])
        arena_start = nc.sbuf_base - 4 * ARENA

        def rounded(name, part):
            tiles, cols = part.shape[1:]
            twin = nc.alloc_sbuf_tensor_at(name, [P, tiles * cols], F32R, offset=arena_start + 4 * part.offset)
            return twin.rearrange("p (a c) -> p a c", a=tiles)

        used = [0]

        def take(*dims):
            n = int(np.prod(dims))
            start = used[0]
            used[0] += -(-n // 8) * 8
            assert used[0] <= ARENA, used[0]
            part = arena[:, start:start + n]
            if len(dims) > 1:
                letters = "abcd"[:len(dims)]
                part = part.rearrange(f"p ({' '.join(letters)}) -> p {' '.join(letters)}",
                                      **dict(zip(letters, dims)))
            return part

        big = take(29 * T)
        siga = big[:, 0:8 * T].rearrange("p (a t) -> p a t", t=T)
        sigb = big[:, 8 * T:16 * T].rearrange("p (a t) -> p a t", t=T)
        fm = big[:, 16 * T:29 * T].rearrange("p (a t) -> p a t", t=T)
        g_ff = big[:, 0:PAIRS * T].rearrange("p (a t) -> p a t", t=T)
        y = siga
        sq = sigb
        h = take(KD, T)
        pads = take(3, NT, 192)
        kpad = take(3, 2, T)
        U = take(4, T + 2)
        zeroed = arena[:, used[0] - 4 * (T + 2) - 3 * 2 * T - 3 * NT * 192:used[0]]
        kcp = take(2, NC)
        vcp = take(2, P)
        gate = take(NT, 24)
        oab = take(2, 4, T)
        cosT, sinT, rs = take(T), take(T), take(T)
        cols = take(2, 8, 2)
        gj = take(NT, 6)
        sj = take(2, 2)
        cj = take(8, 4)
        tmp = take(9, T)
        qs = tmp[:, 0:3]
        rot = tmp[:, 3]
        pbuf = tmp[:, 3:7]
        ptbuf = tmp[:, 7:9]
        posi = tmp[:, 5].bitcast(I32)

        blocks = [v[:, 0:2 * NC * 32].rearrange("p (l g c) -> p l g c", l=32, g=2)
                  for v in (tmp[:, 0:4].rearrange("p a t -> p (a t)"), oab.rearrange("p a b t -> p (a b t)"))]
        hid = tmp[:, 4, 0:4 * NC].rearrange("p (a c) -> p a c", a=2)
        oab8 = oab.rearrange("p a b t -> p (a b) t")
        fm8 = fm[:, 0:KD]
        assert used[0] - 3 * T <= ARENA - HIGHS * D
        highs = rounded("highs", arena[:, ARENA - HIGHS * D:].rearrange("p (a c) -> p a c", a=HIGHS))
        oab8_r, fm8_r, h_r, sigb_r, g_r = (rounded(n, v) for n, v in (
            ("oab_r", oab8), ("fm_r", fm8), ("h_r", h), ("sigb_r", sigb), ("g_r", g_ff)))

        used[0] = 0
        qkvz = take(32 * T)
        sq2 = qkvz[:, 0:KD * T].rearrange("p (a t) -> p a t", t=T)
        zt = qkvz.rearrange("p (h c t) -> p h c t", c=4, t=T)
        U3 = take(4, T + 3)
        cdn = take(4, T)
        rs2 = take(T)
        bg = take(6, 32)
        cj_dn = take(6, 4)
        BETA, G, GC, EKD, EL, NBE = range(6)
        sc = take(6, 32)
        xh, xl = (rounded(f"x_part{i}", arena[:, used[0] + i * KD * T:used[0] + (i + 1) * KD * T]
                          .rearrange("p (a t) -> p a t", t=T)) for i in range(2))
        hb = [dict(zip(("qn", "kn", "qd", "dm", "at", "lt", "M", "X", "T1", "kd", "vb", "ta", "tb"),
                       [take(T) for _ in range(13)])) for _ in range(2)]
        for b_ in hb:
            b_["c"] = take(6, 4)
            b_["R"], b_["vn"], b_["S"] = take(P), take(P), take(P)
            b_["K"] = [b_["ta"], b_["tb"]]

        assert used[0] <= ARENA - HIGHS * D
        used[0] = 0
        sq3 = take(KD, T)
        kda = take(KD * T)
        kda8 = kda.rearrange("p (a t) -> p a t", t=T)
        vda = take(NT, D)
        qda = take(KD * T)
        oda = take(KD, T)
        da_t = take(12, T)
        qz = da_t[:, 0:4]
        pda = da_t[:, 4:10]
        ptd = da_t[:, 10:12]
        va_h = take(2, NT, P)
        rs3 = take(T)
        lam = take(160)
        dcols = take(4, 16)

        sq3_r, oda_r, kda_r = rounded("sq3_r", sq3), rounded("oda_r", oda), rounded("kda_r", kda8)

        used[0] = 0
        sq4 = take(KD, T)
        htm = take(NT, D)
        rs4 = take(T)
        lg = take(NT, 36)
        rt = [take(NT, 32) for _ in range(6)]
        rc = take(24, NT)
        idx = take(JOBS)
        jobs = take(JOBS)
        jwork = take(JOBS, NE)
        dest = take(2, NT)
        gidx = take(2, 1)
        sidx = take(2, 1)
        rnd = take(4)
        xg = take(2, D)
        xT = take(2, KD, P)
        sg = take(2, EFF)
        hs = take(2, EFF)
        hT = take(2, 4, P)
        ym = take(2, D)
        y2 = take(2, 2, D)
        yt = take(NT, D)

        blk = ctx.enter_context(nc.Block())

        tab = {m: nc.dram_tensor(f"table_{m}", (P * JOBS, 1), I32, kind="Internal").ap() for m in ("m0", "m1")}
        hd = {m: nc.dram_tensor(f"rows_in_{m}", (2 * T, D), F32, kind="Internal").ap() for m in ("m0", "m1")}
        yd = {m: nc.dram_tensor(f"rows_out_{m}", (2 * T, D), F32, kind="Internal").ap() for m in ("m0", "m1")}
        wstream = ins["wstream"]

        def units():
            found = []
            for qt in range(NT):
                for g in range(2):
                    found.append(("A", g, qt, [k for k in (qt - 1, qt) if k >= 0]))
                for kind in ("cmp", "slc", "win"):
                    for g in range(2):
                        found.append((kind, g, qt, list(range(qt + 1))))
            return found

        UNITS = units()
        NU = len(UNITS)

        def width(u):
            kind, g, qt, kts = UNITS[u]
            return NC if kind == "cmp" else P * len(kts)

        @blk.sync
        def _(sp):
            seq = Sequence(sp, settled, old, new, "dma_const", "dma_pos", "dma_x", "dma_out", "dma_small")
            sp.dma_start(const[:], ins["const"]).then_inc(const_in, seq.step("const", inc=16))
            sp.dma_start(posi, ins["positions"]).then_inc(positions_in, seq.step("posi", ch="dma_pos", inc=16))
            sp.dma_start(small[:, 0:SM_COLS], ins["small"][0]).then_inc(small_in, seq.step(ch="dma_small", inc=16))
            new.marks["small"] = {"dma_small": (16, ["layer"], [])}
            new.per[("dma_small", "layer")] = 16
            sp.dma_start(x[:], ins["xT"]).then_inc(x_in, seq.step("x0", ch="dma_x", inc=16))
            for r in range(R):
                sp.dma_start(ring[:, r, :], wstream[r]).then_inc(slot_in[r], 16)
            sp.dma_start(ids[:], ins["ids"]).then_inc(ids_in, seq.step("ids", ch="dma_ids", inc=16))
            for i, m in enumerate(("m0", "m1")):
                sp.dma_start(tab[m].rearrange("(p n) o -> p (n o)", p=P), ins["oob"]) \
                    .then_inc(table_filled[i], seq.step(f"{m}.table", ch=f"dma_tab{i}", inc=16))
            per_layer = LAYER_SLOTS // R
            w13 = ins["moe_w13"].rearrange("(n p) c -> n p c", p=P)
            w2 = ins["moe_w2"].rearrange("(n p) c -> n p c", p=P)
            more = []

            def used(turn, r):
                value = turn * R + (r + 1)
                for v in more:
                    value = v + value
                sp.wait_ge(slot_used, value)

            def fill(i0, i1):
                with sp.Fori(i0, i1) as i:
                    for r in range(R):
                        used(i + shift, r)
                        sp.dma_start(ring[:, r, :], wstream[bass.ds(i * R + r, 1)]
                                     .rearrange("o p n -> (o p) n")).then_inc(slot_in[r], 16)

            def fill_experts(m, turn):
                sp.wait_ge(dve_done, seq.at(f"m{m}.rnd"))
                rounds = seq.count_of(rnd[0:1, 0:1].bitcast(I32), 1, ROUNDS_MAX)
                with sp.Fori(0, rounds) as i:
                    experts = [sp.value_load(jobs[0:1, bass.ds(i * 2 + ee, 1)].bitcast(I32), min_val=0, max_val=NE - 1)
                               for ee in range(2)]
                    for n in range(24):
                        used(i * 3 + turn + n // R, n % R)
                        if n < 16:
                            src = w13[bass.ds(experts[n // 8] * 8 + (m * NE * 8 + n % 8), 1)]
                        else:
                            src = w2[bass.ds(experts[(n - 16) // 4] * 4 + (m * NE * 4 + n % 4), 1)]
                        sp.dma_start(ring[:, n % R, :], src.rearrange("o p n -> (o p) n")) \
                            .then_inc(slot_in[n % R], 16)
                return rounds

            shift = 0
            fill(1, per_layer + 1)
            sp.wait_ge(pe_done, seq.at("layer_end.begin.pe", first=True))
            sp.wait_ge(slot_used, seq.at("layer_end.begin.pe", first=True, of="slot"))
            sp.wait_ge(act_done, seq.at("layer_end.begin.act", first=True))
            sp.wait_ge(dve_done, seq.at("layer_end.begin.dve", first=True))
            sp.dma_start(small[:, 0:SM_COLS], ins["small"][1]).then_inc(small_in, seq.step(ch="dma_small", inc=16))
            fill(per_layer + 1, 2 * per_layer)
            sp.wait_ge(pe_done, seq.at("layer_end.begin.pe"))
            sp.wait_ge(slot_used, seq.at("layer_end.begin.pe", of="slot"))
            sp.wait_ge(act_done, seq.at("layer_end.begin.act"))
            sp.wait_ge(dve_done, seq.at("layer_end.begin.dve"))
            sp.dma_start(small[:, 0:S2_COLS], ins["small2"]) \
                .then_inc(small_in, seq.step("small2", ch="dma_small", inc=16))
            turns_pair = 2 * 12 // R
            at_stream = 2 * per_layer
            for m, before in ((0, 40 // R), (1, 32 // R)):
                fill(at_stream, at_stream + before)
                at_stream += before
                turn = at_stream + shift
                rounds = fill_experts(m, turn)
                seq.extra[f"m{m}.ex"] = sp.snap(rounds - 1)
                more.append(sp.snap((rounds - 1) * (turns_pair * R)))
                shift += turns_pair
            sp.wait_ge(dve_done, seq.at("result"))
            sp.dma_start(out, x[:]).then_inc(result_out, seq.step(ch="dma_out", inc=16))
            sp.wait_ge(result_out, seq.so_far("dma_out"))

        @blk.gpsimd
        def _(pool):
            seq = Sequence(pool, settled, old, new, "pool", "dma_t", "dma_i", "dma_g0", "dma_g1", "dma_y0", "dma_y1", "split", "stream_pool")
            seq.step(ch="stream_pool", inc=R)
            pool.sem_inc(pool_done, seq.step(inc=16))
            for i in range(2):
                pool.dma_start(scratch[:, i, :], ins["ids"]).then_inc(rows_gathered[i], seq.step(ch=f"dma_g{i}", inc=16))
                pool.dma_start(scratch[:, 2 + i, :], ins["ids"]) \
                    .then_inc(rows_scattered[i], seq.step(ch=f"dma_y{i}", inc=16))
            pool.memset(zeroed, 0.0).then_inc(pool_done, seq.step())
            seq.note("zeroed")

            def split(n):
                for _ in range(n):
                    c = seq.n["stream_pool"]
                    w = ring[:, c % R, :]
                    pool.wait_ge(weights_cast, seq.following("split"))
                    pool.tensor_tensor(ring_r[:, c % R, :], w, highs[:, c % HIGHS, :].bitcast(F32), ALU.subtract) \
                        .then_inc(weights_split, seq.step(ch="split"))
                    seq.step(ch="stream_pool")

            with seq.loop("layer", LAYERS):
                split(S_LAYER[0])
                with seq.loop("gates", 2):
                    split(8)
                split(S_LAYER[2])
                seq.step(ch="stream_pool", inc=S_LAYER[3])
                split(S_LAYER[4] + S_LAYER[5])
                with seq.loop("up", 5):
                    split(8)
                split(S_LAYER[6] - 40 + S_LAYER[7])
                seq.step(ch="stream_pool", inc=LAYER_PAD)
            with seq.loop("dn", 4):
                split(8)
            split(8)

            def at(table):
                return bass.IndirectOffsetOnAxis(ap=table, axis=0)

            for m in ("m0", "m1"):
                pool.wait_ge(dve_done, seq.at(f"{m}.dest"))
                pool.wait_ge(ids_in, seq.at("ids"))
                pool.wait_ge(table_filled[int(m[1])], seq.at(f"{m}.table"))
                pool.sem_inc(settled, 1)
                for c in range(2):
                    for t in range(NT):
                        pool.indirect_dma_start(out=tab[m], out_offset=at(dest[:, c, t:t + 1].bitcast(U32)),
                                                     in_=ids[:, c * NT + t:c * NT + t + 1], in_offset=None) \
                            .then_inc(numbers_placed, seq.step(ch="dma_t", inc=16))
                pool.wait_ge(numbers_placed, seq.so_far("dma_t"))
                pool.memset(xg, 0.0).then_inc(pool_done, seq.step())
                pool.dma_start(idx.bitcast(I32), tab[m].rearrange("(p n) o -> p (n o)", p=P)) \
                    .then_inc(table_read, seq.step(ch="dma_i", inc=16))
                pool.wait_ge(table_read, seq.so_far("dma_i"))
                pool.wait_ge(pool_done, seq.so_far())
                pool.wait_ge(rows_written[0], seq.at(f"{m}.hd0"))
                pool.wait_ge(rows_written[1], seq.at(f"{m}.hd1"))
                pool.wait_ge(dve_done, seq.at(f"{m}.rnd"))
                pool.wait_ge(pe_done, seq.at(f"{m}.ex.begin.pe"))
                pool.wait_ge(slot_used, seq.at(f"{m}.ex.begin.pe", of="slot"))
                pool.wait_ge(act_done, seq.at(f"{m}.ex.begin.act"))
                pool.wait_ge(dve_done, seq.at(f"{m}.ex.begin.dve"))
                rounds = seq.count_of(rnd[0:1, 0:1].bitcast(I32), 1, ROUNDS_MAX)
                L = f"{m}.ex"

                def number(dst, job):
                    pool.sem_inc(settled, 1)
                    pool.tensor_copy(dst.bitcast(I32), idx[:, bass.ds(job, 1)].bitcast(I32)) \
                        .then_inc(pool_done, seq.step())
                    pool.wait_ge(pool_done, seq.so_far())
                    pool.sem_inc(settled, 1)

                def gather(ee, mark):
                    pool.indirect_dma_start(out=xg[:, ee, :], out_offset=None, in_=hd[m],
                                                 in_offset=at(gidx[:, ee, :].bitcast(U32)),
                                                 bounds_check=2 * T - 1, oob_is_err=False) \
                        .then_inc(rows_gathered[ee], seq.step(f"{m}.{mark}", ch=f"dma_g{ee}", inc=16))

                for ee in range(2):
                    number(gidx[:, ee, :], ee)
                    gather(ee, f"Gpre{ee}")
                with seq.rounds(L, rounds) as i:
                    seq.step(ch="stream_pool", inc=2 * 12)
                    for ee in range(2):
                        if ee:
                            pool.wait_ge(pe_done, seq.at(f"{m}.T1"))
                        else:
                            pool.wait_ge(pe_done, seq.at(f"{m}.Tpre"))
                            pool.wait_ge(pe_done, seq.at(f"{m}.T0n", back=L))
                        pool.wait_ge(rows_gathered[ee], seq.so_far(f"dma_g{ee}"))
                        number(gidx[:, ee, :], i * 2 + (ee + 2))
                        gather(ee, f"G{ee}")
                    for ee in range(2):
                        pool.wait_ge(rows_scattered[ee], seq.so_far(f"dma_y{ee}"))
                        number(sidx[:, ee, :], i * 2 + ee)
                        pool.wait_ge(act_done, seq.at(f"{m}.ya{ee}"))
                        pool.wait_ge(dve_done, seq.at(f"{m}.yd{ee}"))
                        pool.sem_inc(settled, 1)
                        pool.indirect_dma_start(out=yd[m], out_offset=at(sidx[:, ee, :].bitcast(U32)),
                                                     in_=ym[:, ee, :], in_offset=None,
                                                     bounds_check=2 * T - 1, oob_is_err=False) \
                            .then_inc(rows_scattered[ee], seq.step(f"{m}.sc{ee}", ch=f"dma_y{ee}", inc=16))
                for ee in range(2):
                    pool.wait_ge(rows_gathered[ee], seq.so_far(f"dma_g{ee}"))
                    pool.wait_ge(rows_scattered[ee], seq.so_far(f"dma_y{ee}"))
                if m == "m0":
                    split(4 * 8)

        @blk.tensor
        def _(pe):
            seq = Sequence(pe, settled, old, new, "pe", "slot", "split_pe")
            pe.sem_inc(pe_done, seq.step(inc=64))
            pe.sem_inc(slot_used, seq.step(ch="slot", inc=R))

            def meet(stage):
                seq.note(f"{stage}.begin.pe")
                pe.wait_ge(act_done, seq.at(f"{stage}.begin.act"))
                pe.wait_ge(dve_done, seq.at(f"{stage}.begin.dve"))

            def slot():
                r, value = seq.arrival("slot")
                pe.wait_ge(slot_in[r], value)
                return ring[:, r, :]

            def weights():
                c = seq.n["slot"]
                pe.wait_ge(weights_split, seq.following("split_pe"))
                seq.step(ch="split_pe")
                return highs[:, c % HIGHS, :], ring_r[:, c % R, :]

            def product(acc, lhs, rhs, start, stop):
                pe.matmul(acc, lhs[0], rhs[0], start=start, stop=False)
                pe.matmul(acc, lhs[0], rhs[1], start=False, stop=False)
                return pe.matmul(acc, lhs[1], rhs[0], start=False, stop=stop)

            def tile(stage, r, src, inloop=None, drained=act_done, first=None):
                if r >= 4:
                    pe.wait_ge(drained, seq.at(f"{stage}.d{r - 4}"))
                elif inloop:
                    pe.wait_ge(act_done, seq.at(f"{stage}.d{r + 4}", back=inloop))
                w = [v.rearrange("p (k c) -> p k c", c=P) for v in weights()]
                for k in range(KD):
                    if r == 0 and first:
                        pe.wait_ge(dve_done, seq.at(f"{first}.lo{k}"))
                    mm = product(psum[:, r % 4, :], [v[:, k, :] for v in w],
                                 [v[:, k, :] for v in src], k == 0, k == KD - 1)
                mm.then_inc(slot_used, seq.step(f"{stage}.t{r}", ch="slot"))

            def token_major(stage, src, width, banks=(0, 1, 2, 3)):
                for s in range(4):
                    w = [v.rearrange("p (k c) -> p k c", c=512) for v in weights()]
                    for kk in range(2):
                        for t in range(NT):
                            k = 2 * s + kk
                            mm = product(psum[:, banks[t], 0:width],
                                         [v[:, k, t * P:(t + 1) * P] for v in src],
                                         [v[:, kk, 0:width] for v in w], k == 0, k == KD - 1)
                    mm.then_inc(slot_used, seq.step(f"{stage}.s{s}", ch="slot"))

            def column_sums(stage, src, bank=7, pre="sq", done="ss", written=act_done, order=range(KD)):
                for i, k in enumerate(order):
                    pe.wait_ge(written, seq.at(f"{stage}.{pre}{k}"))
                    mm = pe.matmul(psum[:, bank, :], ones, src[:, k, :], start=(i == 0), stop=(i == KD - 1))
                mm.then_inc(pe_done, seq.step(f"{stage}.{done}"))

            pe.wait_ge(const_in, seq.at("const"))
            pe.wait_ge(x_in, seq.at("x0"))
            with seq.loop("layer", LAYERS):
                meet("n1")
                column_sums("n1", sq)
                both = (oab8_r, h_r)
                for r in range(NFM):
                    tile("fm", r, both, first="n1")
                pe.wait_ge(act_done, seq.at(f"fm.d{NFM - 1}"))
                for i, kt in enumerate((KA, KS, KW)):
                    mm = pe.matmul(psum[:, 4 + i, :], perm, fm[:, kt, :], start=True, stop=True)
                    mm.then_inc(pe_done, seq.step(f"rk{i}"))
                with seq.loop("gates", 2):
                    for r in range(8):
                        tile("gates", r, both, inloop="gates")
                pe.wait_ge(act_done, seq.at("gates.d7"))
                token_major("tm", both, TM_COLS)
                meet("cmp")
                for kv in range(2):
                    pe.wait_ge(dve_done, seq.at(f"cmp.b{kv}"))
                    for s in range(4):
                        w = slot().rearrange("p (l c) -> p l c", c=P)
                        for i in range(8):
                            l = 8 * s + i
                            mm = pe.matmul(psum[:, kv, 0:2 * NC], w[:, i, :],
                                           blocks[kv][:, l, :, :].rearrange("p g c -> p (g c)"),
                                           start=(l == 0), stop=(l == 31))
                        mm.then_inc(slot_used, seq.step(f"cmp.u{kv}" if s == 3 else None, ch="slot"))
                pe.wait_ge(act_done, seq.at("cmp.hid1"))
                for g in range(2):
                    w2k = sm("w2k")[:, g * P:(g + 1) * P]
                    w2v = sm("w2v")[:, g * P:(g + 1) * P]
                    pe.matmul(psum[:, 2, g * NC:(g + 1) * NC], w2k, hid[:, 0, g * NC:(g + 1) * NC],
                              start=True, stop=True)
                    mm = pe.matmul(psum[0:NC, 3, g * P:(g + 1) * P], hid[:, 1, g * NC:(g + 1) * NC],
                                   w2v, start=True, stop=True)
                mm.then_inc(pe_done, seq.step("cmp.kv"))
                with seq.loop("heads", 4) as j:
                    for i, base in enumerate((QA, QB)):
                        mm = pe.matmul(psum[:, i, :], perm,
                                       fm[:, bass.ds(j + base, 1), :].rearrange("p o t -> p (o t)"),
                                       start=True, stop=True)
                        mm.then_inc(pe_done, seq.step(f"rq{i}"))

                    def scores(u):
                        kind, g, qt, kts = UNITS[u]
                        q = qs[:, {"A": 0, "cmp": 2}.get(kind, 1), qt * P:(qt + 1) * P]
                        if kind == "cmp":
                            keys = kcp[:, g, :]
                        else:
                            b = {"A": 0, "slc": 1, "win": 2}[kind]
                            keys = kpad[:, b, g, kts[0] * P:(kts[-1] + 1) * P]
                        if u >= 4:
                            pe.wait_ge(act_done, seq.at(f"u{u - 4}.e"))
                        mm = pe.matmul(psum[:, u % 4, 0:width(u)], q, keys, start=True, stop=True)
                        mm.then_inc(pe_done, seq.step(f"u{u}.S"))

                    def turn(u):
                        kind, g, qt, kts = UNITS[u]
                        pe.wait_ge(dve_done, seq.at(f"u{u}.p"))
                        if u >= 2:
                            pe.wait_ge(act_done, seq.at(f"u{u - 2}.t"))
                        if kind == "cmp":
                            mm = pe.transpose(psum[0:NC, 4 + u % 2, 0:P], pbuf[:, u % 4, 0:NC], ident)
                        else:
                            for i in range(len(kts)):
                                mm = pe.transpose(psum[:, 4 + u % 2, i * P:(i + 1) * P],
                                                  pbuf[:, u % 4, i * P:(i + 1) * P], ident)
                        mm.then_inc(pe_done, seq.step(f"u{u}.T"))

                    def weigh(u):
                        kind, g, qt, kts = UNITS[u]
                        pe.wait_ge(act_done, seq.at(f"u{u}.t"))
                        ob = 6 if kind == "A" else 7
                        group = [w for w in range(NU) if UNITS[w][2] == qt and (UNITS[w][0] == "A") == (kind == "A")]
                        acc = psum[:, ob, qt * P:(qt + 1) * P]
                        if kind == "cmp":
                            mm = pe.matmul(acc, vcp[0:NC, g, :], ptbuf[0:NC, u % 2, 0:P],
                                           start=(u == group[0]), stop=False)
                        else:
                            b = {"A": 0, "slc": 1, "win": 2}[kind]
                            for i, kt in enumerate(kts):
                                mm = pe.matmul(acc, pads[:, b, kt, HD * g:HD * g + P],
                                               ptbuf[:, u % 2, i * P:(i + 1) * P],
                                               start=(u == group[0] and i == 0),
                                               stop=(u == group[-1] and i == len(kts) - 1))
                        mm.then_inc(pe_done, seq.step(f"u{u}.o"))

                    pe.wait_ge(dve_done, seq.at("rq.done"))
                    pe.wait_ge(act_done, seq.at("qraw"))
                    for u in range(4):
                        scores(u)
                    for u in range(NU):
                        if u % 2 == 0 and u + 4 < NU:
                            scores(u + 4)
                            scores(u + 5)
                        turn(u)
                        if u >= 1:
                            weigh(u - 1)
                    weigh(NU - 1)
                meet("branch")
                for r in range(8):
                    a, b = 2 * (r % 2), 2 * (r % 2) + 1
                    if r >= 2:
                        pe.wait_ge(dve_done, seq.at(f"branch.d{r - 2}"))
                    w = [v.rearrange("p (k c) -> p k c", c=P) for v in weights()]
                    for br in range(2):
                        for k in range(4):
                            if r == 0:
                                pe.wait_ge(dve_done, seq.at(f"oab.lo{4 * br + k}"))
                            mm = product(psum[:, (a, b)[br], :], [v[:, 4 * br + k, :] for v in w],
                                         [v[:, 4 * br + k, :] for v in (fm8_r, oab8_r)], k == 0, k == 3)
                    mm.then_inc(slot_used, seq.step(f"branch.t{r}", ch="slot"))
                pe.wait_ge(dve_done, seq.at("branch.d7"))
                for r in range(8):
                    tile("out", r, (sigb_r, h_r), first="mix")
                column_sums("n2", oab8)
                column_sums("n3", sq)
                with seq.loop("up", 5):
                    for r in range(8):
                        tile("up", r, (oab8_r, h_r), inloop="up", first="n3")
                pe.wait_ge(act_done, seq.at("up.d7"))
                for r in range(4):
                    tile("up2", r, (oab8_r, h_r))
                meet("down")
                for k in range(PAIRS):
                    w = [v.rearrange("p (k c) -> p k c", c=P) for v in weights()]
                    pe.wait_ge(dve_done, seq.at(f"down.lo{k}"))
                    for c in range(KD):
                        mm = product(psum[:, c, :], [v[:, c, :] for v in w],
                                     [oab8_r[:, k % 8, :], g_r[:, k, :]],
                                     k == 0, k == PAIRS - 1)
                    mm.then_inc(slot_used, seq.step(f"down.t{k}", ch="slot"))
                column_sums("n4", sq, order=(7, 0, 1, 2, 3, 4, 5, 6))
                pe.wait_ge(dve_done, seq.at("down.d0"))
                for _ in range(LAYER_PAD):
                    pe.matmul(psum[:, 0, 0:2], ident, slot()[:, 0:2], start=True, stop=True) \
                        .then_inc(slot_used, seq.step(ch="slot"))
                meet("layer_end")

            def layer_norm_sums(stage, sq):
                column_sums(stage, x, 7, "r", "sum", written=dve_done)
                column_sums(stage, sq, 6)

            meet("ab")
            pe.wait_ge(small_in, seq.at("small2"))
            for t in range(NT):
                for k in range(KD):
                    mm = pe.matmul(psum[:, 4, t * 16:(t + 1) * 16], x[:, k, t * P:(t + 1) * P],
                                   s2("ab")[:, k * 16:(k + 1) * 16], start=(k == 0), stop=(k == KD - 1))
            mm.then_inc(pe_done, seq.step("ab.t"))
            with seq.loop("dn", 4):
                for r in range(8):
                    tile("dn", r, (xh, xl), inloop="dn", first="xdn")
            pe.wait_ge(dve_done, seq.at("ab.g"))
            pe.matmul(psum[:, 5, 0:32], cc("tri"), bg[:, G, :], start=True, stop=True)
            pe.matmul(psum[:, 5, 32:64], ones, bg[:, G, :], start=True, stop=True) \
                .then_inc(pe_done, seq.step("ab.gc"))
            with seq.loop("delta", 4):
                meet("delta")

                def four(hh, bank, lhsT, rhs, mark):
                    for t in range(NT):
                        c = slice(t * P, (t + 1) * P)
                        mm = pe.matmul(psum[:, 4 * hh + bank, c], lhsT[:, c], rhs[:, c], start=True, stop=True)
                    mm.then_inc(pe_done, seq.step(f"d{hh}.{mark}"))

                def turn4(hh, bank, src, mark):
                    for t in range(NT):
                        c = slice(t * P, (t + 1) * P)
                        mm = pe.transpose(psum[:, 4 * hh + bank, c], src[:, c], ident)
                    mm.then_inc(pe_done, seq.step(f"d{hh}.{mark}"))

                for hh in range(2):
                    b = hb[hh]
                    pe.wait_ge(act_done, seq.at(f"d{hh}.sq"))
                    pe.matmul(psum[:, 4 * hh, :], ones, b["ta"], start=True, stop=True)
                    pe.matmul(psum[:, 4 * hh + 1, :], ones, b["tb"], start=True, stop=True) \
                        .then_inc(pe_done, seq.step(f"d{hh}.ss"))
                for hh in range(2):
                    b = hb[hh]
                    pe.wait_ge(dve_done, seq.at(f"d{hh}.norm"))
                    pe.wait_ge(act_done, seq.at(f"d{hh}.vst"))
                    turn4(hh, 2, b["kn"], "kT")
                    turn4(hh, 3, b["vb"], "vT")
                    pe.wait_ge(dve_done, seq.at(f"d{hh}.TG"))
                    pe.matmul(psum[:, 4 * hh, :], ones, b["X"], start=True, stop=True)
                    pe.matmul(psum[:, 4 * hh + 1, :], ones, b["M"], start=True, stop=True) \
                        .then_inc(pe_done, seq.step(f"d{hh}.rows"))
                for hh in range(2):
                    b = hb[hh]
                    pe.wait_ge(dve_done, seq.at(f"d{hh}.kv"))
                    four(hh, 2, b["kn"], b["kn"], "KK")
                    four(hh, 3, b["kn"], b["qn"], "QK")
                for hh in range(2):
                    pe.wait_ge(dve_done, seq.at(f"d{hh}.K0"))
                    turn4(hh, 0, hb[hh]["K"][0], "K0T")
                for lev in range(1, 7):
                    for hh in range(2):
                        b = hb[hh]
                        pe.wait_ge(dve_done, seq.at(f"d{hh}.K{lev}"))
                        pe.wait_ge(dve_done, seq.at(f"d{hh}.X{lev - 1}"))
                        four(hh, 0, b["K"][lev % 2], b["M"], f"T{lev}")
                    for hh in range(2):
                        b = hb[hh]
                        pe.wait_ge(act_done, seq.at(f"d{hh}.Ts{lev}"))
                        four(hh, 1, b["T1"], b["X"], f"XT{lev}")
                        if lev < 6:
                            four(hh, 2, b["X"], b["T1"], f"MT{lev}")
                for t in range(NT):
                    c = slice(t * P, (t + 1) * P)
                    for hh in range(2):
                        b = hb[hh]
                        if t:
                            pe.wait_ge(dve_done, seq.at(f"d{hh}.S{t - 1}"))
                            pe.matmul(psum[:, 4 * hh, 0:P], b["kn"][:, c], b["S"], start=True, stop=True) \
                                .then_inc(pe_done, seq.step(f"d{hh}.kS{t}"))
                    for hh in range(2):
                        b = hb[hh]
                        pe.wait_ge(dve_done, seq.at(f"d{hh}.R{t}"))
                        pe.matmul(psum[:, 4 * hh + 1, 0:P], b["X"][:, c], b["R"] if t else b["vb"][:, c],
                                       start=True, stop=True).then_inc(pe_done, seq.step(f"d{hh}.v{t}"))
                    for hh in range(2):
                        b = hb[hh]
                        pe.wait_ge(act_done, seq.at(f"d{hh}.vn{t}"))
                        if t < NT - 1:
                            pe.matmul(psum[:, 4 * hh + 3, 0:P], b["kd"][:, c], b["vn"], start=True, stop=True) \
                                .then_inc(pe_done, seq.step(f"d{hh}.dS{t}"))
                        if t:
                            pe.matmul(psum[:, 4 * hh + 2, c], b["S"], b["qd"][:, c], start=True, stop=False)
                        pe.matmul(psum[:, 4 * hh + 2, c], b["vn"], b["at"][:, c], start=(t == 0), stop=True) \
                            .then_inc(pe_done, seq.step(f"d{hh}.o{t}"))
                for hh in range(2):
                    pe.wait_ge(act_done, seq.at(f"d{hh}.osq"))
                    pe.matmul(psum[:, 4 * hh, :], ones, hb[hh]["ta"], start=True, stop=True) \
                        .then_inc(pe_done, seq.step(f"d{hh}.oss"))
            meet("wo")
            for r in range(8):
                tile("wo", r, (xh, xl), drained=dve_done, first="zo")
            layer_norm_sums("l0", sq2)

            def experts(m, xsrc):
                meet(f"{m}.route")
                w = s2("router").rearrange("p (l k c) -> p l k c", l=2, c=36)[:, int(m[1])]
                for t in range(NT):
                    for k in range(KD):
                        mm = pe.matmul(psum[:, 0, t * 36:(t + 1) * 36], x[:, k, t * P:(t + 1) * P], w[:, k, :],
                                       start=(k == 0), stop=(k == KD - 1))
                mm.then_inc(pe_done, seq.step(f"{m}.lg"))
                for i in range(8):
                    t, half = i // 2, i % 2
                    if i >= 4:
                        pe.wait_ge(act_done, seq.at(f"{m}.h{i - 4}"))
                    for k in range(4):
                        mm = pe.transpose(psum[:, 4 + i % 4, k * P:(k + 1) * P],
                                          x[:, 4 * half + k, t * P:(t + 1) * P], ident)
                    mm.then_inc(pe_done, seq.step(f"{m}.tm{i}"))
                pe.wait_ge(dve_done, seq.at(f"{m}.chosen"))
                for t in range(NT):
                    for u in range(t):
                        pe.matmul(psum[:, 1, t * 32:(t + 1) * 32], ones, rt[2][:, u, :], start=(u == 0), stop=False)
                    pe.matmul(psum[:, 1, t * 32:(t + 1) * 32], cc("strictT"), rt[2][:, t, :],
                              start=(t == 0), stop=True)
                for t in range(NT):
                    mm = pe.matmul(psum[:, 2, 0:32], ones, rt[2][:, t, :], start=(t == 0), stop=(t == NT - 1))
                mm.then_inc(pe_done, seq.step(f"{m}.rank"))
                pe.wait_ge(dve_done, seq.at(f"{m}.rnd"))
                rounds = seq.count_of(rnd[0:1, 0:1].bitcast(I32), 1, ROUNDS_MAX)
                meet(f"{m}.ex")

                def turn_x(ee, mark):
                    for k in range(KD):
                        mm = pe.transpose(psum[:, k // 4, (k % 4) * P:(k % 4 + 1) * P],
                                          xg[:, ee, k * P:(k + 1) * P], ident)
                    mm.then_inc(pe_done, seq.step(f"{m}.{mark}"))

                L = f"{m}.ex"
                pe.wait_ge(rows_gathered[0], seq.at(f"{m}.Gpre0"))
                turn_x(0, "Tpre")
                pe.wait_ge(dve_done, seq.at(f"{m}.xTpre"))
                up_banks, down_banks = ((2, 3), (4, 7)), ((5, 6), (4, 7))

                def up(ee, k):
                    w = slot()
                    for half in range(2):
                        mm = pe.matmul(psum[:, up_banks[ee][half], :], xT[:, ee, k, :],
                                       w[:, half * EFF:(half + 1) * EFF], start=(k == 0), stop=(k == KD - 1))
                    mm.then_inc(slot_used, seq.step(f"{m}.g{ee}", ch="slot"))

                def turn_h(ee):
                    pe.wait_ge(dve_done, seq.at(f"{m}.hs{ee}"))
                    for f in range(4):
                        mm = pe.transpose(psum[:, 2 + ee, f * P:(f + 1) * P], hs[:, ee, f * P:(f + 1) * P], ident)
                    mm.then_inc(pe_done, seq.step(f"{m}.HT{ee}"))

                def down(ee, f):
                    w = slot()
                    for half in range(2):
                        mm = pe.matmul(psum[:, down_banks[ee][half], :], hT[:, ee, f, :],
                                       w[:, half * 512:(half + 1) * 512], start=(f == 0), stop=(f == 3))
                    mm.then_inc(slot_used, seq.step(f"{m}.z{ee}", ch="slot"))

                with seq.rounds(L, rounds):
                    pe.wait_ge(rows_gathered[1], seq.at(f"{m}.G1", back=L))
                    pe.wait_ge(dve_done, seq.at(f"{m}.xT0n", back=L))
                    turn_x(1, "T1")
                    pe.wait_ge(act_done, seq.at(f"{m}.hT1", back=L))
                    for k in range(KD):
                        up(0, k)
                    pe.wait_ge(dve_done, seq.at(f"{m}.xT1"))
                    pe.wait_ge(act_done, seq.at(f"{m}.ya1", back=L))
                    for k in range(KD):
                        if k == 4:
                            turn_h(0)
                        up(1, k)
                    pe.wait_ge(rows_gathered[0], seq.at(f"{m}.G0"))
                    turn_x(0, "T0n")
                    pe.wait_ge(act_done, seq.at(f"{m}.hT0"))
                    for f in range(4):
                        if f == 2:
                            turn_h(1)
                        down(0, f)
                    pe.wait_ge(act_done, seq.at(f"{m}.hT1"))
                    for f in range(4):
                        down(1, f)
                meet(f"{m}.back")
                for k in range(KD):
                    if k >= 4:
                        pe.wait_ge(dve_done, seq.at(f"{m}.r{k - 4}"))
                    for t in range(NT):
                        if k == 0:
                            pe.wait_ge(dve_done, seq.at(f"{m}.yt{t}"))
                        mm = pe.transpose(psum[:, k % 4, t * P:(t + 1) * P], yt[:, t, k * P:(k + 1) * P], ident)
                    mm.then_inc(pe_done, seq.step(f"{m}.f{k}"))
                layer_norm_sums(m, sq4)

            experts("m0", x)
            meet("kda")
            pe.sem_inc(settled, 1)
            for r in range(8):
                tile("kda", r, (sq3_r, oda_r), first="xda")
            pe.wait_ge(act_done, seq.at("kda.d7"))
            token_major("vda0", (sq3_r, oda_r), 512)
            token_major("vda1", (sq3_r, oda_r), 512, (4, 5, 6, 7))
            pe.wait_ge(act_done, seq.at("vda.out"))
            for r in range(8):
                tile("qda", r, (sq3_r, oda_r))
            with seq.loop("da", 4) as j:
                pe.wait_ge(act_done, seq.at("da.q"))
                pe.wait_ge(dve_done, seq.at("da.v"))

                def scores2(u):
                    hh, qt = u // 4, u % 4
                    if u >= 2:
                        pe.wait_ge(act_done, seq.at(f"a{u - 2}.e"))
                    for s_ in range(2):
                        mm = pe.matmul(psum[:, 2 * (u % 2) + s_, 0:(qt + 1) * P],
                                       qz[:, 2 * hh + s_, qt * P:(qt + 1) * P],
                                       kda[:, bass.ds(j * (2 * T) + hh * T, (qt + 1) * P)], start=True, stop=True)
                    mm.then_inc(pe_done, seq.step(f"a{u}.S"))

                def turn2(u):
                    pe.wait_ge(dve_done, seq.at(f"a{u}.p"))
                    if u >= 2:
                        pe.wait_ge(act_done, seq.at(f"a{u - 2}.t"))
                    for i in range(u % 4 + 1):
                        mm = pe.transpose(psum[:, 4 + u % 2, i * P:(i + 1) * P],
                                          pda[:, 2 * (u % 3), i * P:(i + 1) * P], ident)
                    mm.then_inc(pe_done, seq.step(f"a{u}.T"))

                def weigh2(u):
                    hh, qt = u // 4, u % 4
                    pe.wait_ge(act_done, seq.at(f"a{u}.t"))
                    for i in range(qt + 1):
                        mm = pe.matmul(psum[:, 6 + hh, qt * P:(qt + 1) * P], va_h[:, hh, i, :],
                                       ptd[:, u % 2, i * P:(i + 1) * P], start=(i == 0), stop=(i == qt))
                    mm.then_inc(pe_done, seq.step(f"a{u}.o"))

                scores2(0)
                scores2(1)
                for u in range(8):
                    if u + 2 < 8:
                        scores2(u + 2)
                    turn2(u)
                    if u:
                        weigh2(u - 1)
                weigh2(7)
            meet("dan")
            for hd in range(8):
                pe.wait_ge(act_done, seq.at(f"dan.sq{hd}"))
                pe.matmul(psum[:, hd, :], ones, sq3[:, hd, :], start=True, stop=True) \
                    .then_inc(pe_done, seq.step(f"dan.ss{hd}"))
            pe.wait_ge(dve_done, seq.at("dan.o"))
            meet("wo2")
            pe.sem_inc(settled, 1)
            for r in range(8):
                tile("wo2", r, (kda_r, oda_r), drained=dve_done, first="oo")
            layer_norm_sums("l1", sq3)
            experts("m1", x)

        @blk.scalar
        def _(act):
            seq = Sequence(act, settled, old, new, "act", "dma_h0", "dma_h1", "dma_b0", "dma_b1", "cast", "stream_act")
            seq.step(ch="stream_act", inc=R)
            act.sem_inc(act_done, seq.step(inc=64))

            def meet(stage):
                seq.note(f"{stage}.begin.act")
                act.wait_ge(act_done, seq.so_far())
                act.wait_ge(pe_done, seq.at(f"{stage}.begin.pe"))
                act.wait_ge(slot_used, seq.at(f"{stage}.begin.pe", of="slot"))
                act.wait_ge(dve_done, seq.at(f"{stage}.begin.dve"))

            def cast_weights():
                r, value = seq.arrival("stream_act")
                act.wait_ge(slot_in[r], value)
                act.wait_ge(slot_used, seq.following("stream_act", -1))
                act.activation(highs[:, r % HIGHS, :], ring[:, r, :], ACT.Copy) \
                    .then_inc(weights_cast, seq.step(ch="cast"))
                seq.step(ch="stream_act")

            def high(stage, k, dst, src):
                act.wait_ge(dve_done, seq.at(f"{stage}.h{k}"))
                act.activation(dst[:, k, :], src[:, k, :], ACT.Copy) \
                    .then_inc(act_done, seq.step(f"{stage}.hi{k}"))

            def highs_of(stage, dst, src):
                for k in range(KD):
                    act.activation(dst[:, k, :], src[:, k, :], ACT.Copy) \
                        .then_inc(act_done, seq.step(f"{stage}.hi{k}"))

            def squares(stage, src):
                for k in range(KD):
                    act.activation(sq[:, k, :], src[:, k, :], ACT.Square) \
                        .then_inc(act_done, seq.step(f"{stage}.sq{k}"))

            def rstd(stage, div=D, eps="eps", bank=7):
                act.wait_ge(pe_done, seq.at(f"{stage}.ss"))
                act.activation(rs, psum[:, bank, :], ACT.Ln, bias=cc(eps), scale=1.0 / div) \
                    .then_inc(act_done, seq.step())
                act.wait_ge(act_done, seq.so_far())
                act.activation(rs, rs, ACT.Exp, scale=-0.5).then_inc(act_done, seq.step(f"{stage}.rs"))

            act.wait_ge(const_in, seq.at("const"))
            act.wait_ge(dve_done, seq.at("angle"))
            act.activation(sinT, tmp[:, 0, :], ACT.Sin).then_inc(act_done, seq.step())
            act.activation(cosT, tmp[:, 1, :], ACT.Sin).then_inc(act_done, seq.step("trig"))
            act.wait_ge(x_in, seq.at("x0"))
            with seq.loop("layer", LAYERS):
                meet("n1")
                squares("n1", x)
                cast_weights()
                cast_weights()
                rstd("n1")
                for k in range(KD):
                    high("n1", k, oab8_r, h)
                for r in range(NFM):
                    act.wait_ge(slot_used, seq.at(f"fm.t{r}"))
                    act.activation(fm[:, r, :], psum[:, r % 4, :], ACT.Copy) \
                        .then_inc(act_done, seq.step(f"fm.d{r}"))
                    cast_weights()
                with seq.loop("gates", 2) as i:
                    for r in range(8):
                        act.wait_ge(slot_used, seq.at(f"gates.t{r}"))
                        act.activation(big[:, bass.ds(i * (8 * T) + r * T, T)], psum[:, r % 4, :],
                                            ACT.Sigmoid).then_inc(act_done, seq.step(f"gates.d{r}"))
                        cast_weights()
                cast_weights()
                cast_weights()
                act.wait_ge(slot_used, seq.at("tm.s3"))
                act.wait_ge(pool_done, seq.at("zeroed"))
                for t in range(NT):
                    for b in range(3):
                        act.activation(
                            pads[:, b, t, :].rearrange("p (a c) -> p a c", c=HD)[:, 0:3:2, :],
                            psum[:, t, b * P:(b + 1) * P].rearrange("p (g c) -> p g c", c=HD), ACT.Copy) \
                            .then_inc(act_done, seq.step())
                    act.activation(gate[:, t, :], psum[:, t, GATE_C:TM_COLS], ACT.Sigmoid) \
                        .then_inc(act_done, seq.step())
                meet("cmp")
                seq.step(ch="stream_act", inc=S_LAYER[3])
                for kv in range(2):
                    act.wait_ge(slot_used, seq.at(f"cmp.u{kv}"))
                    act.activation(hid[:, kv, :], psum[:, kv, 0:2 * NC], ACT.Gelu_apprx_tanh,
                                        bias=sm("b1")[:, kv:kv + 1]).then_inc(act_done, seq.step(f"cmp.hid{kv}"))
                act.wait_ge(pe_done, seq.at("cmp.kv"))
                act.activation(kcp.rearrange("p g c -> p (g c)"), psum[:, 2, 0:2 * NC], ACT.Copy) \
                    .then_inc(act_done, seq.step())
                act.activation(vcp[0:NC].rearrange("p g c -> p (g c)"), psum[0:NC, 3, 0:2 * P], ACT.Copy) \
                    .then_inc(act_done, seq.step())
                with seq.loop("heads", 4) as j:
                    act.wait_ge(act_done, seq.so_far())
                    act.activation(qs[:, 2, :], fm[:, bass.ds(j + QB, 1), :].rearrange("p o t -> p (o t)"),
                                        ACT.Copy).then_inc(act_done, seq.step("qraw"))

                    def exps(u):
                        kind, g, qt, kts = UNITS[u]
                        c = cols[:, u // 2 % 2, :, g:g + 1]
                        act.wait_ge(dve_done, seq.at(f"m{u // 2}"))
                        if u >= 4:
                            act.wait_ge(pe_done, seq.at(f"u{u - 4}.T"))
                        if kind == "A":
                            act.activation(c[:, 3, :], c[:, 1, :], ACT.Exp,
                                                bias=sj[:, 0, g:g + 1]).then_inc(act_done, seq.step())
                        act.activation(pbuf[:, u % 4, 0:width(u)], psum[:, u % 4, 0:width(u)], ACT.Exp,
                                            bias=c[:, 1, :], scale=SCALE,
                                            accum_out=c[:, 2, :]).then_inc(act_done, seq.step(f"u{u}.e"))

                    def evict(u):
                        kind, g, qt, kts = UNITS[u]
                        act.wait_ge(pe_done, seq.at(f"u{u}.T"))
                        if u >= 2:
                            act.wait_ge(pe_done, seq.at(f"u{u - 2}.o"))
                        if kind == "cmp":
                            o, i = ptbuf[0:NC, u % 2, 0:P], psum[0:NC, 4 + u % 2, 0:P]
                        else:
                            o, i = ptbuf[:, u % 2, 0:width(u)], psum[:, 4 + u % 2, 0:width(u)]
                        act.activation(o, i, ACT.Copy).then_inc(act_done, seq.step(f"u{u}.t"))

                    exps(0)
                    exps(1)
                    for u in range(NU):
                        if u % 2 == 0 and u + 2 < NU:
                            exps(u + 2)
                            exps(u + 3)
                        evict(u)
                    act.wait_ge(pe_done, seq.at(f"u{NU - 1}.o"))
                    for br in range(2):
                        act.activation(oab[:, br, bass.ds(j, 1), :].rearrange("p o t -> p (o t)"),
                                            psum[:, 6 + br, :], ACT.Copy).then_inc(act_done, seq.step())
                meet("branch")
                cast_weights()
                cast_weights()
                highs_of("oab", fm8_r, oab8)
                for r in range(8):
                    cast_weights()
                    high("mix", r, sigb_r, h)
                for r in range(8):
                    act.wait_ge(slot_used, seq.at(f"out.t{r}"))
                    act.activation(y[:, r, :], psum[:, r % 4, :], ACT.Copy).then_inc(act_done, seq.step())
                    act.activation(oab8[:, r, :], psum[:, r % 4, :], ACT.Square) \
                        .then_inc(act_done, seq.step(f"out.d{r}"))
                    seq.note(f"n2.sq{r}")
                    cast_weights()
                rstd("n2")
                for k in range(KD):
                    act.wait_ge(dve_done, seq.at(f"n2.x{k}"))
                    act.activation(sq[:, k, :], x[:, k, :], ACT.Square).then_inc(act_done, seq.step(f"n3.sq{k}"))
                rstd("n3")
                for k in range(KD):
                    high("n3", k, oab8_r, h)

                def gelu(stage, i, dst):
                    act.wait_ge(dve_done, seq.at(f"{stage}.c{i}"))
                    act.activation(dst, tmp[:, 2 * (i % 2), :], ACT.Gelu_apprx_tanh) \
                        .then_inc(act_done, seq.step(f"{stage}.g{i}"))

                def up_pairs(stage, n, inloop):
                    for r in range(n):
                        act.wait_ge(slot_used, seq.at(f"{stage}.t{r}"))
                        if r >= 4:
                            act.wait_ge(dve_done, seq.at(f"{stage}.v{r - 4}"))
                        elif inloop:
                            act.wait_ge(dve_done, seq.at(f"{stage}.v{r + 4}", back=inloop))
                        act.activation(U[:, r % 4, 2:T + 2], psum[:, r % 4, :], ACT.Copy) \
                            .then_inc(act_done, seq.step(f"{stage}.d{r}"))
                        cast_weights()
                        if r % 2 == 1 and r >= 3:
                            pair = (r - 3) // 2
                            gelu(stage, pair, tmp[:, 4 + pair % 2, :])
                    gelu(stage, n // 2 - 1, tmp[:, 4 + (n // 2 - 1) % 2, :])

                with seq.loop("up", 5):
                    up_pairs("up", 8, "up")
                act.wait_ge(dve_done, seq.at("up.v7"))
                up_pairs("up2", 4, None)
                meet("down")

                def high_g(k):
                    act.activation(oab8_r[:, k % 8, :], g_ff[:, k, :], ACT.Copy) \
                        .then_inc(act_done, seq.step(f"down.hi{k}"))

                for k in range(8):
                    high_g(k)
                for k in range(PAIRS):
                    if k + HIGHS < PAIRS:
                        cast_weights()
                    if k + 8 < PAIRS:
                        act.wait_ge(slot_used, seq.at(f"down.t{k}"))
                        high_g(k + 8)
                seq.step(ch="stream_act", inc=LAYER_PAD)
                for c in (7, 0, 1, 2, 3, 4, 5, 6):
                    act.wait_ge(dve_done, seq.at(f"down.d{c}"))
                    act.activation(sq[:, c, :], psum[:, c, :], ACT.Square).then_inc(act_done, seq.step(f"n4.sq{c}"))
                rstd("n4")
                meet("layer_end")

            def layer_norm(stage, sq_, rs_):
                act.wait_ge(pe_done, seq.at(f"{stage}.sum"))
                act.activation(rs_, psum[:, 7, :], ACT.Copy, scale=1.0 / D) \
                    .then_inc(act_done, seq.step(f"{stage}.mu"))
                for k in range(KD):
                    act.wait_ge(dve_done, seq.at(f"{stage}.c{k}"))
                    act.activation(sq_[:, k, :], x[:, k, :], ACT.Square) \
                        .then_inc(act_done, seq.step(f"{stage}.sq{k}"))
                act.wait_ge(pe_done, seq.at(f"{stage}.ss"))
                act.activation(rs_, psum[:, 6, :], ACT.Ln, bias=cc("lneps"), scale=1.0 / D) \
                    .then_inc(act_done, seq.step())
                act.wait_ge(act_done, seq.so_far())
                act.activation(rs_, rs_, ACT.Exp, scale=-0.5).then_inc(act_done, seq.step(f"{stage}.rs"))

            meet("ab")
            cast_weights()
            cast_weights()
            highs_of("xdn", xh, x)
            act.wait_ge(small_in, seq.at("small2"))
            act.wait_ge(pe_done, seq.at("ab.t"))
            ab = psum[:, 4, 0:64].rearrange("p (t c) -> p t c", c=16)
            def th(v):
                return v.rearrange("p (t h) -> p t h", h=8)
            act.activation(th(bg[:, BETA, :]), ab[:, :, 0:8], ACT.Sigmoid).then_inc(act_done, seq.step("ab.beta"))
            act.activation(sc[:, 3, 0:8], s2("alog"), ACT.Exp).then_inc(act_done, seq.step())
            act.wait_ge(dve_done, seq.at("ab.abs"))
            act.activation(sc[:, 2, :], sc[:, 1, :], ACT.Exp, scale=-1.0).then_inc(act_done, seq.step())
            act.wait_ge(act_done, seq.so_far())
            act.activation(sc[:, 2, :], sc[:, 2, :], ACT.Ln, bias=cc("one")).then_inc(act_done, seq.step("ab.sp"))
            act.wait_ge(dve_done, seq.at("dn.zeros"))
            with seq.loop("dn", 4) as i:
                def silu(r):
                    act.wait_ge(dve_done, seq.at(f"dn.v{r}"))
                    act.activation(qkvz[:, bass.ds(i * (8 * T) + r * T, T)], cdn[:, r % 4, :], ACT.Silu) \
                        .then_inc(act_done, seq.step(f"dn.s{r}"))
                for r in range(8):
                    act.wait_ge(slot_used, seq.at(f"dn.t{r}"))
                    if r % 4 == 3:
                        act.activation(qkvz[:, bass.ds(i * (8 * T) + r * T, T)], psum[:, r % 4, :], ACT.Silu) \
                            .then_inc(act_done, seq.step(f"dn.d{r}"))
                    else:
                        if r >= 4:
                            act.wait_ge(dve_done, seq.at(f"dn.v{r - 4}"))
                        else:
                            act.wait_ge(dve_done, seq.at(f"dn.v{r + 4}", back="dn"))
                        act.activation(U3[:, r % 4, 3:T + 3], psum[:, r % 4, :], ACT.Copy) \
                            .then_inc(act_done, seq.step(f"dn.d{r}"))
                    cast_weights()
                    if r % 4:
                        silu(r - 1)
            act.wait_ge(pe_done, seq.at("ab.gc"))
            act.activation(bg[:, GC, :], psum[:, 5, 0:32], ACT.Copy).then_inc(act_done, seq.step("ab.gcc"))
            act.activation(bg[:, EL, :], psum[:, 5, 32:64], ACT.Exp).then_inc(act_done, seq.step("ab.el"))
            act.activation(sc[:, 4, :], psum[:, 5, 0:32], ACT.Exp).then_inc(act_done, seq.step("ab.egc"))
            act.wait_ge(dve_done, seq.at("ab.dif"))
            act.activation(bg[:, EKD, :], sc[:, 5, :], ACT.Exp).then_inc(act_done, seq.step())
            with seq.loop("delta", 4) as i:
                meet("delta")
                for hh in range(2):
                    b = hb[hh]
                    for c, dst in ((0, "ta"), (1, "tb")):
                        act.activation(b[dst], qkvz[:, bass.ds(i * (8 * T) + (4 * hh + c) * T, T)], ACT.Square) \
                            .then_inc(act_done, seq.step())
                    seq.note(f"d{hh}.sq")
                    act.activation(b["vb"], qkvz[:, bass.ds(i * (8 * T) + (4 * hh + 2) * T, T)], ACT.Copy) \
                        .then_inc(act_done, seq.step(f"d{hh}.vst"))
                for hh in range(2):
                    b = hb[hh]
                    act.wait_ge(pe_done, seq.at(f"d{hh}.ss"))
                    for c, dst in ((0, "ta"), (1, "tb")):
                        act.activation(b[dst], psum[:, 4 * hh + c, :], ACT.Ln, bias=cc("eps")) \
                            .then_inc(act_done, seq.step())
                act.wait_ge(act_done, seq.so_far())
                for hh in range(2):
                    b = hb[hh]
                    for dst in ("ta", "tb"):
                        act.activation(b[dst], b[dst], ACT.Exp, scale=-0.5).then_inc(act_done, seq.step())
                    seq.note(f"d{hh}.rs")
                for hh in range(2):
                    b = hb[hh]
                    act.wait_ge(pe_done, seq.at(f"d{hh}.rows"))
                    act.wait_ge(dve_done, seq.at(f"d{hh}.norm"))
                    act.activation(b["ta"], psum[:, 4 * hh, :], ACT.Exp).then_inc(act_done, seq.step(f"d{hh}.egb"))
                for hh in range(2):
                    b = hb[hh]
                    act.wait_ge(dve_done, seq.at(f"d{hh}.dif"))
                    act.activation(b["dm"], b["dm"], ACT.Exp).then_inc(act_done, seq.step(f"d{hh}.dec"))
                for lev in range(1, 7):
                    for hh in range(2):
                        act.wait_ge(pe_done, seq.at(f"d{hh}.T{lev}"))
                        act.activation(hb[hh]["T1"], psum[:, 4 * hh, :], ACT.Copy) \
                            .then_inc(act_done, seq.step(f"d{hh}.Ts{lev}"))
                for t in range(NT):
                    for hh in range(2):
                        act.wait_ge(pe_done, seq.at(f"d{hh}.v{t}"))
                        if t:
                            act.wait_ge(pe_done, seq.at(f"d{hh}.o{t - 1}"))
                        act.activation(hb[hh]["vn"], psum[:, 4 * hh + 1, 0:P], ACT.Copy) \
                            .then_inc(act_done, seq.step(f"d{hh}.vn{t}"))
                for hh in range(2):
                    act.wait_ge(pe_done, seq.at(f"d{hh}.o{NT - 1}"))
                    act.activation(hb[hh]["ta"], psum[:, 4 * hh + 2, :], ACT.Square) \
                        .then_inc(act_done, seq.step(f"d{hh}.osq"))
                for hh in range(2):
                    act.wait_ge(pe_done, seq.at(f"d{hh}.oss"))
                    act.activation(hb[hh]["tb"], psum[:, 4 * hh, :], ACT.Ln, bias=cc("eps"), scale=1.0 / P) \
                        .then_inc(act_done, seq.step())
                act.wait_ge(act_done, seq.so_far())
                for hh in range(2):
                    act.activation(hb[hh]["tb"], hb[hh]["tb"], ACT.Exp, scale=-0.5) \
                        .then_inc(act_done, seq.step(f"d{hh}.ors"))
            meet("wo")
            highs_of("zo", xh, zt[:, :, 3, :])
            for _ in range(8 - HIGHS):
                cast_weights()
            layer_norm("l0", sq2, rs2)

            def experts(m):
                meet(f"{m}.route")
                act.wait_ge(pe_done, seq.at(f"{m}.lg"))
                act.activation(lg.rearrange("p t c -> p (t c)"), psum[:, 0, 0:NT * 36], ACT.Copy) \
                    .then_inc(act_done, seq.step(f"{m}.lgs"))
                for i in range(8):
                    t, half = i // 2, i % 2
                    act.wait_ge(pe_done, seq.at(f"{m}.tm{i}"))
                    act.activation(htm[:, t, 512 * half:512 * half + 512], psum[:, 4 + i % 4, :], ACT.Copy) \
                        .then_inc(act_done, seq.step(f"{m}.h{i}"))
                act.wait_ge(act_done, seq.so_far())
                rows = hd[m].rearrange("(t p c) d -> c p t d", p=P, c=2)
                for c in range(2):
                    act.dma_start(rows[c], htm) \
                        .then_inc(rows_written[c], seq.step(f"{m}.hd{c}", ch=f"dma_h{c}", inc=16))
                act.wait_ge(dve_done, seq.at(f"{m}.ge"))
                act.activation(rt[1][:, :, 0:NG], rt[0][:, :, 0:NG], ACT.Exp) \
                    .then_inc(act_done, seq.step(f"{m}.gx"))
                act.wait_ge(dve_done, seq.at(f"{m}.d"))
                act.activation(rc[:, 9, :], rc[:, 8, :], ACT.Exp).then_inc(act_done, seq.step(f"{m}.e2"))
                act.wait_ge(dve_done, seq.at(f"{m}.rnd"))
                rounds = seq.count_of(rnd[0:1, 0:1].bitcast(I32), 1, ROUNDS_MAX)
                meet(f"{m}.ex")
                L = f"{m}.ex"
                with seq.rounds(L, rounds):
                    seq.step(ch="stream_act", inc=2 * 12)
                    for ee in range(2):
                        act.wait_ge(slot_used, seq.at(f"{m}.g{ee}"))
                        act.activation(sg[:, ee, :], psum[:, (2, 4)[ee], :], ACT.Silu) \
                            .then_inc(act_done, seq.step(f"{m}.sg{ee}"))
                        act.wait_ge(pe_done, seq.at(f"{m}.HT{ee}"))
                        act.activation(hT[:, ee].rearrange("p f c -> p (f c)"), psum[:, 2 + ee, :], ACT.Copy) \
                            .then_inc(act_done, seq.step(f"{m}.hT{ee}"))
                    for ee in range(2):
                        act.wait_ge(slot_used, seq.at(f"{m}.z{ee}"))
                        act.wait_ge(rows_scattered[ee], seq.at(f"{m}.sc{ee}", back=L))
                        act.activation(ym[:, ee, 0:512], psum[:, (5, 4)[ee], :], ACT.Copy) \
                            .then_inc(act_done, seq.step(f"{m}.ya{ee}"))
                meet(f"{m}.back")
                act.wait_ge(rows_scattered[0], seq.at(f"{m}.sc0"))
                act.wait_ge(rows_scattered[1], seq.at(f"{m}.sc1"))
                rows = yd[m].rearrange("(t p c) d -> t p c d", p=P, c=2)
                for t in range(NT):
                    if t >= 2:
                        act.wait_ge(dve_done, seq.at(f"{m}.yt{t - 2}"))
                    act.dma_start(y2[:, t % 2], rows[t]) \
                        .then_inc(rows_back[t % 2], seq.step(f"{m}.y2{t}", ch=f"dma_b{t % 2}", inc=16))
                layer_norm(m, sq4, rs4)

            experts("m0")
            meet("kda")
            act.sem_inc(settled, 1)
            cast_weights()
            cast_weights()
            highs_of("xda", sq3_r, x)
            for r in range(8):
                act.wait_ge(slot_used, seq.at(f"kda.t{r}"))
                act.activation(kda[:, r * T:(r + 1) * T], psum[:, r % 4, :], ACT.Copy) \
                    .then_inc(act_done, seq.step(f"kda.d{r}"))
                cast_weights()
            for half in range(2):
                for _ in range(4):
                    cast_weights()
                act.wait_ge(slot_used, seq.at(f"vda{half}.s3"))
                for t in range(NT):
                    act.activation(vda[:, t, 512 * half:512 * half + 512], psum[:, 4 * half + t, :], ACT.Copy) \
                        .then_inc(act_done, seq.step())
            seq.note("vda.out")
            for r in range(8):
                act.wait_ge(slot_used, seq.at(f"qda.t{r}"))
                act.activation(qda[:, r * T:(r + 1) * T], psum[:, r % 4, :], ACT.Copy) \
                    .then_inc(act_done, seq.step(f"qda.d{r}"))
                cast_weights()
            act.wait_ge(dve_done, seq.at("lam.s"))
            act.activation(lam[:, 132:134], lam[:, 130:132], ACT.Exp).then_inc(act_done, seq.step("lam.e"))
            act.wait_ge(dve_done, seq.at("qz.zeros"))
            with seq.loop("da", 4) as j:
                act.wait_ge(act_done, seq.so_far())
                for hh in range(2):
                    src = qda[:, bass.ds(j * (2 * T) + hh * T, T)]
                    for s_ in range(2):
                        p0 = HD * s_
                        act.activation(qz[p0:p0 + HD, 2 * hh + s_, :], src[p0:p0 + HD, :], ACT.Copy) \
                            .then_inc(act_done, seq.step())
                seq.note("da.q")
                def exps2(u):
                    w = (u % 4 + 1) * P
                    act.wait_ge(dve_done, seq.at(f"a{u}.m"))
                    if u >= 3:
                        act.wait_ge(pe_done, seq.at(f"a{u - 3}.T"))
                    c = dcols[:, u % 4, :]
                    for s_ in range(2):
                        act.activation(pda[:, 2 * (u % 3) + s_, 0:w], psum[:, 2 * (u % 2) + s_, 0:w], ACT.Exp,
                                            bias=c[:, 2 + s_:3 + s_], scale=SCALE, accum_out=c[:, 4 + s_:5 + s_]) \
                            .then_inc(act_done, seq.step())
                    seq.note(f"a{u}.e")
                exps2(0)
                for u in range(8):
                    if u + 1 < 8:
                        exps2(u + 1)
                    w = (u % 4 + 1) * P
                    act.wait_ge(pe_done, seq.at(f"a{u}.T"))
                    if u >= 2:
                        act.wait_ge(pe_done, seq.at(f"a{u - 2}.o"))
                    act.activation(ptd[:, u % 2, 0:w], psum[:, 4 + u % 2, 0:w], ACT.Copy) \
                        .then_inc(act_done, seq.step(f"a{u}.t"))
                act.wait_ge(pe_done, seq.at("a7.o"))
                for hh in range(2):
                    act.activation(oda.rearrange("p a t -> p (a t)")[:, bass.ds(j * (2 * T) + hh * T, T)],
                                        psum[:, 6 + hh, :], ACT.Copy).then_inc(act_done, seq.step())
            meet("dan")
            for hd_ in range(8):
                act.activation(sq3[:, hd_, :], oda[:, hd_, :], ACT.Square) \
                    .then_inc(act_done, seq.step(f"dan.sq{hd_}"))
            for hd_ in range(8):
                act.wait_ge(pe_done, seq.at(f"dan.ss{hd_}"))
                act.activation(sq3[:, hd_, :], psum[:, hd_, :], ACT.Ln, bias=cc("eps"), scale=1.0 / P) \
                    .then_inc(act_done, seq.step())
            act.wait_ge(act_done, seq.so_far())
            for hd_ in range(8):
                act.activation(sq3[:, hd_, :], sq3[:, hd_, :], ACT.Exp, scale=-0.5) \
                    .then_inc(act_done, seq.step(f"dan.rs{hd_}"))
            meet("wo2")
            highs_of("oo", kda_r, oda)
            for _ in range(8 - HIGHS):
                cast_weights()
            layer_norm("l1", sq3, rs3)
            experts("m1")

        @blk.vector
        def _(dve):
            seq = Sequence(dve, settled, old, new, "dve")
            dve.sem_inc(dve_done, seq.step(inc=64))

            def meet(stage):
                seq.note(f"{stage}.begin.dve")
                dve.wait_ge(dve_done, seq.so_far())
                dve.wait_ge(pe_done, seq.at(f"{stage}.begin.pe"))
                dve.wait_ge(slot_used, seq.at(f"{stage}.begin.pe", of="slot"))
                dve.wait_ge(act_done, seq.at(f"{stage}.begin.act"))

            def low(stage, k, dst, src, hi):
                dve.wait_ge(act_done, seq.at(f"{stage}.hi{k}"))
                dve.tensor_tensor(dst[:, k, :], src[:, k, :], hi[:, k, :].bitcast(F32), ALU.subtract) \
                    .then_inc(dve_done, seq.step(f"{stage}.lo{k}"))

            def scaled(stage, dst, src, gain):
                dve.wait_ge(act_done, seq.at(f"{stage}.rs"))
                for k in range(KD):
                    dve.scalar_tensor_tensor(dst[:, k, :], src[:, k, :], gains[:, gain, k:k + 1], rs,
                                                  ALU.mult, ALU.mult).then_inc(dve_done, seq.step(f"{stage}.h{k}"))

            def residual(stage, src, gain):
                scaled(stage, src, src, gain)
                dve.wait_ge(dve_done, seq.so_far())
                for k in range(KD):
                    dve.tensor_tensor(x[:, k, :], x[:, k, :], src[:, k, :], ALU.add) \
                        .then_inc(dve_done, seq.step(f"{stage}.x{k}"))
                dve.wait_ge(dve_done, seq.so_far())

            dve.wait_ge(const_in, seq.at("const"))
            dve.wait_ge(positions_in, seq.at("posi"))
            pf, ang, turns, red = tmp[:, 2, :], tmp[:, 3, :], tmp[:, 4, :], tmp[:, 0, :]
            dve.tensor_copy(pf, posi).then_inc(dve_done, seq.step())
            dve.wait_ge(dve_done, seq.so_far())
            dve.tensor_scalar(ang, pf, cc("invf"), None, ALU.mult).then_inc(dve_done, seq.step())
            dve.wait_ge(dve_done, seq.so_far())
            MAGIC = 12582912.0
            dve.tensor_scalar(turns, ang, 1.0 / (2 * math.pi), MAGIC, ALU.mult, ALU.add) \
                .then_inc(dve_done, seq.step())
            dve.wait_ge(dve_done, seq.so_far())
            dve.tensor_scalar(turns, turns, MAGIC, None, ALU.subtract).then_inc(dve_done, seq.step())
            dve.wait_ge(dve_done, seq.so_far())
            c1 = 6.28125
            c2 = float(np.float32(2 * math.pi - c1).view(np.int32).__and__(~0xFFF).view(np.float32))
            c3 = 2 * math.pi - c1 - c2
            src = ang
            for c in (c1, c2, c3):
                dve.scalar_tensor_tensor(red, turns, -c, src, ALU.mult, ALU.add).then_inc(dve_done, seq.step())
                dve.wait_ge(dve_done, seq.so_far())
                src = red
            dve.tensor_scalar(red, red, math.pi - 1e-6, -(math.pi - 1e-6), ALU.min, ALU.max) \
                .then_inc(dve_done, seq.step())
            dve.wait_ge(dve_done, seq.so_far())
            dve.tensor_scalar(ang, red, -1.0, None, ALU.mult).then_inc(dve_done, seq.step())
            dve.wait_ge(dve_done, seq.so_far())
            dve.tensor_tensor(ang, ang, red, ALU.min).then_inc(dve_done, seq.step())
            dve.wait_ge(dve_done, seq.so_far())
            dve.tensor_scalar(tmp[:, 1, :], ang, math.pi / 2, None, ALU.add).then_inc(dve_done, seq.step("angle"))
            dve.wait_ge(x_in, seq.at("x0"))
            dve.wait_ge(pool_done, seq.at("zeroed"))
            with seq.loop("layer", LAYERS):
                meet("n1")
                dve.wait_ge(small_in, seq.at("small"))
                scaled("n1", h, x, 0)
                for k in range(KD):
                    low("n1", k, h_r, h, oab8_r)

                def build_blocks(kv):
                    dve.memset(blocks[kv], 0.0).then_inc(dve_done, seq.step())
                    dve.wait_ge(dve_done, seq.so_far())
                    for g in range(2):
                        p0 = HD * g
                        for half in range(2):
                            src = fm[p0:p0 + HD, (KC, VC)[kv], 16 * half:16 * half + 16 * NC] \
                                .rearrange("p (c l) -> p l c", l=16)
                            pos = sm("pos")[p0:p0 + HD, 32 * kv + 16 * half:32 * kv + 16 * half + 16]
                            dve.tensor_tensor(blocks[kv][p0:p0 + HD, 16 * half:16 * half + 16, g, :], src,
                                              pos.unsqueeze(2).to_broadcast([HD, 16, NC]), ALU.add) \
                                .then_inc(dve_done, seq.step())
                    seq.note(f"cmp.b{kv}")

                for i, kt in enumerate((KA, KS, KW)):
                    dve.wait_ge(pe_done, seq.at(f"rk{i}"))
                    dve.tensor_tensor(rs, psum[:, 4 + i, :], sinT, ALU.mult).then_inc(dve_done, seq.step())
                    dve.tensor_tensor(fm[:, kt, :], fm[:, kt, :], cosT, ALU.mult).then_inc(dve_done, seq.step())
                    dve.wait_ge(dve_done, seq.so_far())
                    for g in range(2):
                        p0 = HD * g
                        dve.tensor_tensor(kpad[p0:p0 + HD, i, g, :], fm[p0:p0 + HD, kt, :],
                                          rs[p0:p0 + HD, :], ALU.add).then_inc(dve_done, seq.step())
                    dve.wait_ge(dve_done, seq.so_far())
                build_blocks(0)
                meet("cmp")
                build_blocks(1)
                with seq.loop("heads", 4) as j:
                    dve.wait_ge(dve_done, seq.so_far())
                    for i, base in enumerate((QA, QB)):
                        dve.wait_ge(pe_done, seq.at(f"rq{i}"))
                        dve.tensor_tensor(rot, psum[:, i, :], sinT, ALU.mult).then_inc(dve_done, seq.step())
                        dve.tensor_tensor(qs[:, i, :], fm[:, bass.ds(j + base, 1), :]
                                               .rearrange("p o t -> p (o t)"), cosT, ALU.mult) \
                            .then_inc(dve_done, seq.step())
                        dve.wait_ge(dve_done, seq.so_far())
                        dve.tensor_tensor(qs[:, i, :], qs[:, i, :], rot, ALU.add).then_inc(dve_done, seq.step())
                        dve.wait_ge(dve_done, seq.so_far())
                    dve.tensor_copy(gj, gate[:, :, bass.ds(j * 6, 6)]).then_inc(dve_done, seq.step())
                    dve.tensor_copy(sj[:, 0, :], sinks[:, bass.ds(j, 1), :].rearrange("p o g -> p (o g)")) \
                        .then_inc(dve_done, seq.step())
                    dve.wait_ge(dve_done, seq.so_far())
                    dve.tensor_scalar(sj[:, 1, :], sj[:, 0, :], -1.0, None, ALU.mult).then_inc(dve_done, seq.step())
                    dve.wait_ge(dve_done, seq.so_far())
                    seq.note("rq.done")

                    def maxima(p):
                        u = 2 * p
                        kind, _, qt, _ = UNITS[u]
                        dve.wait_ge(pe_done, seq.at(f"u{u + 1}.S"))
                        banks = psum[:, u % 4:u % 4 + 2, :]
                        if kind == "cmp":
                            s = banks[:, :, 0:NC]
                            m = cc("cmp")[:, NC * qt:NC * (qt + 1)].unsqueeze(1).to_broadcast([P, 2, NC])
                            dve.tensor_tensor(s, s, m, ALU.add).then_inc(dve_done, seq.step())
                        else:
                            d = banks[:, :, width(u) - P:width(u)]
                            dve.tensor_tensor(d, d, cc("causal").unsqueeze(1).to_broadcast([P, 2, P]), ALU.add) \
                                .then_inc(dve_done, seq.step())
                            if kind == "A" and qt:
                                d = banks[:, :, 0:P]
                                dve.tensor_tensor(d, d, cc("band").unsqueeze(1).to_broadcast([P, 2, P]), ALU.add) \
                                    .then_inc(dve_done, seq.step())
                        dve.wait_ge(dve_done, seq.so_far())
                        c = cols[:, p % 2]
                        dve.tensor_reduce(c[:, 0, :], banks[:, :, 0:width(u)], AX, ALU.max) \
                            .then_inc(dve_done, seq.step())
                        dve.wait_ge(dve_done, seq.so_far())
                        if kind == "A":
                            dve.scalar_tensor_tensor(c[:, 1, :], c[:, 0, :], -SCALE, sj[:, 1, :],
                                                     ALU.mult, ALU.min).then_inc(dve_done, seq.step(f"m{p}"))
                        else:
                            dve.tensor_scalar(c[:, 1, :], c[:, 0, :], -SCALE, 1e24, ALU.mult, ALU.min) \
                                .then_inc(dve_done, seq.step(f"m{p}"))

                    def normalise(p):
                        u = 2 * p
                        kind, _, qt, _ = UNITS[u]
                        dve.wait_ge(act_done, seq.at(f"u{u + 1}.e"))
                        c = cols[:, p % 2]
                        if kind == "A":
                            dve.tensor_tensor(c[:, 4, :], c[:, 2, :], c[:, 3, :], ALU.add) \
                                .then_inc(dve_done, seq.step())
                            dve.wait_ge(dve_done, seq.so_far())
                            dve.reciprocal(c[:, 6, :], c[:, 4, :]).then_inc(dve_done, seq.step())
                        else:
                            br = {"cmp": 0, "slc": 1, "win": 2}[kind]
                            dve.tensor_scalar(c[:, 4, :], c[:, 2, :], TINY, None, ALU.max) \
                                .then_inc(dve_done, seq.step())
                            dve.wait_ge(dve_done, seq.so_far())
                            dve.reciprocal(c[:, 6, :], c[:, 4, :]).then_inc(dve_done, seq.step())
                        dve.wait_ge(dve_done, seq.so_far())
                        for g in range(2):
                            pb = pbuf[:, (u + g) % 4, 0:width(u)]
                            if kind == "A":
                                dve.tensor_scalar(pb, pb, c[:, 6, g:g + 1], None, ALU.mult) \
                                    .then_inc(dve_done, seq.step(f"u{u + g}.p"))
                            else:
                                dve.tensor_scalar(pb, pb, c[:, 6, g:g + 1], gj[:, qt, 3 * g + br:3 * g + br + 1],
                                                  ALU.mult, ALU.mult).then_inc(dve_done, seq.step(f"u{u + g}.p"))

                    maxima(0)
                    for p in range(NU // 2):
                        if p + 1 < NU // 2:
                            maxima(p + 1)
                        normalise(p)
                meet("branch")
                for k in range(KD):
                    low("oab", k, oab8_r, oab8, fm8_r)
                for r in range(8):
                    a, b = 2 * (r % 2), 2 * (r % 2) + 1
                    dve.wait_ge(slot_used, seq.at(f"branch.t{r}"))
                    dve.tensor_tensor(tmp[:, r % 2, :], psum[:, a, :], siga[:, r, :], ALU.mult) \
                        .then_inc(dve_done, seq.step())
                    dve.tensor_tensor(h[:, r, :], psum[:, b, :], sigb[:, r, :], ALU.mult) \
                        .then_inc(dve_done, seq.step(f"branch.d{r}"))
                    dve.wait_ge(dve_done, seq.so_far())
                    dve.tensor_tensor(h[:, r, :], h[:, r, :], tmp[:, r % 2, :], ALU.add) \
                        .then_inc(dve_done, seq.step(f"mix.h{r}"))
                    if r:
                        low("mix", r - 1, h_r, h, sigb_r)
                low("mix", 7, h_r, h, sigb_r)
                residual("n2", y, 1)
                scaled("n3", h, x, 2)
                for k in range(KD):
                    low("n3", k, h_r, h, oab8_r)

                def convolve(stage, n, inloop, base):
                    dve.tensor_copy(cj[:, 0:n, :], conv[:, bass.ds(base, n), :] if inloop
                                         else conv[:, base:base + n, :]).then_inc(dve_done, seq.step())
                    dve.wait_ge(dve_done, seq.so_far())

                    def finish(i):
                        dve.wait_ge(act_done, seq.at(f"{stage}.g{i}"))
                        dve.wait_ge(dve_done, seq.so_far())
                        if inloop:
                            dst = big[:, bass.ds(base * (T // 2) + i * T, T)]
                        else:
                            dst = g_ff[:, base // 2 + i, :]
                        dve.tensor_tensor(dst, tmp[:, 4 + i % 2, :], tmp[:, 2 * (i % 2) + 1, :], ALU.mult) \
                            .then_inc(dve_done, seq.step())

                    for r in range(n):
                        pair, half = r // 2, r % 2
                        u, c = U[:, r % 4, :], tmp[:, 2 * (pair % 2) + half, :]
                        w = cj[:, r, :]
                        dve.wait_ge(act_done, seq.at(f"{stage}.d{r}"))
                        dve.wait_ge(dve_done, seq.so_far())
                        dve.tensor_scalar(c, u[:, 2:T + 2], w[:, 2:3], w[:, 3:4], ALU.mult, ALU.add) \
                            .then_inc(dve_done, seq.step())
                        dve.wait_ge(dve_done, seq.so_far())
                        dve.scalar_tensor_tensor(c, u[:, 1:T + 1], w[:, 1:2], c, ALU.mult, ALU.add) \
                            .then_inc(dve_done, seq.step())
                        dve.wait_ge(dve_done, seq.so_far())
                        dve.scalar_tensor_tensor(c, u[:, 0:T], w[:, 0:1], c, ALU.mult, ALU.add) \
                            .then_inc(dve_done, seq.step(f"{stage}.v{r}"))
                        if half == 0:
                            seq.note(f"{stage}.c{pair}")
                        elif pair:
                            finish(pair - 1)
                    finish(n // 2 - 1)
                    dve.wait_ge(dve_done, seq.so_far())

                with seq.loop("up", 5) as i:
                    convolve("up", 8, "up", i * 8)
                convolve("up2", 4, None, 40)
                meet("down")
                for k in range(PAIRS):
                    dve.wait_ge(act_done, seq.at(f"down.hi{k}"))
                    dve.tensor_tensor(g_r[:, k, :], g_ff[:, k, :], oab8_r[:, k % 8, :].bitcast(F32),
                                      ALU.subtract) \
                        .then_inc(dve_done, seq.step(f"down.lo{k}"))
                dve.wait_ge(slot_used, seq.at(f"down.t{PAIRS - 1}"))
                for c in (7, 0, 1, 2, 3, 4, 5, 6):
                    dve.tensor_copy(h[:, c, :], psum[:, c, :]).then_inc(dve_done, seq.step(f"down.d{c}"))
                dve.wait_ge(dve_done, seq.so_far())
                residual("n4", h, 3)
                meet("layer_end")

            def layer_norm(stage, which, rs_):
                g = s2("ln").rearrange("p (a k) -> p a k", k=KD)
                dve.wait_ge(act_done, seq.at(f"{stage}.mu"))
                for k in range(KD):
                    dve.tensor_tensor(x[:, k, :], x[:, k, :], rs_, ALU.subtract) \
                        .then_inc(dve_done, seq.step(f"{stage}.c{k}"))
                dve.wait_ge(act_done, seq.at(f"{stage}.rs"))
                dve.wait_ge(dve_done, seq.so_far())
                for k in range(KD):
                    dve.scalar_tensor_tensor(x[:, k, :], x[:, k, :], g[:, 2 * which, k:k + 1], rs_,
                                                  ALU.mult, ALU.mult).then_inc(dve_done, seq.step())
                dve.wait_ge(dve_done, seq.so_far())
                for k in range(KD):
                    dve.tensor_scalar(x[:, k, :], x[:, k, :], g[:, 2 * which + 1, k:k + 1], None, ALU.add) \
                        .then_inc(dve_done, seq.step())
                seq.note(f"{stage}.x")

            def th(v):
                return v.rearrange("p (t h) -> p t h", h=8)

            def rows(v, n=NT):
                return v.unsqueeze(1).to_broadcast([P, n, v.shape[1]])

            def across(v, w):
                return v.unsqueeze(2).to_broadcast([P, v.shape[1], w])

            def chunks(v):
                return v.rearrange("p (t c) -> p t c", c=P)

            def step(*args, mark=None, op=None):
                op(*args).then_inc(dve_done, seq.step(mark))
                dve.wait_ge(dve_done, seq.so_far())

            meet("ab")
            dve.memset(U3, 0.0).then_inc(dve_done, seq.step("dn.zeros"))
            for k in range(KD):
                low("xdn", k, xl, x, xh)
            dve.wait_ge(small_in, seq.at("small2"))
            dve.wait_ge(pe_done, seq.at("ab.t"))
            ab = psum[:, 4, 0:64].rearrange("p (t c) -> p t c", c=16)
            dve.wait_ge(act_done, seq.at("ab.beta"))
            step(th(sc[:, 0, :]), ab[:, :, 8:16], rows(s2("dtb")), ALU.add, op=dve.tensor_tensor)
            step(sc[:, 1, :], sc[:, 0, :], -1.0, None, ALU.mult, op=dve.tensor_scalar)
            step(sc[:, 1, :], sc[:, 1, :], sc[:, 0, :], ALU.max, op=dve.tensor_tensor, mark="ab.abs")
            step(sc[:, 0, :], sc[:, 0, :], 0.0, None, ALU.max, op=dve.tensor_scalar)
            dve.wait_ge(act_done, seq.at("ab.sp"))
            step(sc[:, 0, :], sc[:, 0, :], sc[:, 2, :], ALU.add, op=dve.tensor_tensor)
            step(th(sc[:, 0, :]), th(sc[:, 0, :]), rows(sc[:, 3, 0:8]), ALU.mult, op=dve.tensor_tensor)
            step(bg[:, G, :], sc[:, 0, :], -1.0, None, ALU.mult, op=dve.tensor_scalar, mark="ab.g")
            cw = s2("conv").rearrange("p (t c) -> p t c", c=4)
            with seq.loop("dn", 4) as i:
                dve.wait_ge(dve_done, seq.so_far())
                dve.tensor_copy(cj_dn, cw[:, bass.ds(i * 6, 6), :]).then_inc(dve_done, seq.step())
                dve.wait_ge(dve_done, seq.so_far())
                for r in range(8):
                    if r % 4 == 3:
                        continue
                    u, c, w = U3[:, r % 4, :], cdn[:, r % 4, :], cj_dn[:, 3 * (r // 4) + r % 4, :]
                    dve.wait_ge(act_done, seq.at(f"dn.d{r}"))
                    if r >= 4:
                        dve.wait_ge(act_done, seq.at(f"dn.s{r - 4}"))
                    else:
                        dve.wait_ge(act_done, seq.at(f"dn.s{r + 4}", back="dn"))
                    dve.tensor_scalar(c, u[:, 3:T + 3], w[:, 3:4], None, ALU.mult).then_inc(dve_done, seq.step())
                    for q in (2, 1, 0):
                        dve.wait_ge(dve_done, seq.so_far())
                        dve.scalar_tensor_tensor(c, u[:, q:T + q], w[:, q:q + 1], c, ALU.mult, ALU.add) \
                            .then_inc(dve_done, seq.step(f"dn.v{r}"))
            dve.wait_ge(act_done, seq.at("ab.gcc"))
            dve.wait_ge(act_done, seq.at("ab.egc"))
            step(sc[:, 5, :], psum[:, 5, 32:64], bg[:, GC, :], ALU.subtract, op=dve.tensor_tensor, mark="ab.dif")
            step(bg[:, NBE, :], sc[:, 4, :], bg[:, BETA, :], ALU.mult, op=dve.tensor_tensor)
            step(bg[:, NBE, :], bg[:, NBE, :], -1.0, None, ALU.mult, op=dve.tensor_scalar)
            with seq.loop("delta", 4) as i:
                meet("delta")
                tri, strict = rows(cc("tri")), rows(cc("strictT"))
                levels = cc("levels").rearrange("p (s c) -> p s c", s=7)
                for hh in range(2):
                    b = hb[hh]
                    dve.tensor_copy(b["c"].unsqueeze(3), bg.rearrange("p q (t h) -> p q t h", h=8)
                                         [:, :, :, bass.ds(i * 2 + hh, 1)]).then_inc(dve_done, seq.step())
                dve.wait_ge(dve_done, seq.so_far())
                for hh in range(2):
                    b, c = hb[hh], hb[hh]["c"]
                    dve.tensor_tensor(chunks(b["X"]), tri, across(c[:, G, :], P), ALU.mult) \
                        .then_inc(dve_done, seq.step())
                    dve.tensor_tensor(chunks(b["M"]), rows(ident), across(c[:, BETA, :], P), ALU.mult) \
                        .then_inc(dve_done, seq.step(f"d{hh}.TG"))
                for hh in range(2):
                    b = hb[hh]
                    dve.wait_ge(act_done, seq.at(f"d{hh}.rs"))
                    qkv = lambda c: qkvz[:, bass.ds(i * (8 * T) + (4 * hh + c) * T, T)]
                    dve.scalar_tensor_tensor(b["qn"], qkv(0), P ** -0.5, b["ta"], ALU.mult, ALU.mult) \
                        .then_inc(dve_done, seq.step())
                    dve.tensor_tensor(b["kn"], qkv(1), b["tb"], ALU.mult) \
                        .then_inc(dve_done, seq.step(f"d{hh}.norm"))
                for hh in range(2):
                    b, c = hb[hh], hb[hh]["c"]
                    dve.wait_ge(pe_done, seq.at(f"d{hh}.kT"))
                    dve.wait_ge(pe_done, seq.at(f"d{hh}.vT"))
                    dve.tensor_tensor(chunks(b["kd"]), chunks(psum[:, 4 * hh + 2, :]), across(c[:, EKD, :], P), ALU.mult) \
                        .then_inc(dve_done, seq.step())
                    dve.tensor_tensor(chunks(b["vb"]), chunks(psum[:, 4 * hh + 3, :]), across(c[:, BETA, :], P), ALU.mult) \
                        .then_inc(dve_done, seq.step(f"d{hh}.kv"))
                for hh in range(2):
                    b, c = hb[hh], hb[hh]["c"]
                    dve.wait_ge(act_done, seq.at(f"d{hh}.egb"))
                    dve.tensor_tensor(chunks(b["dm"]), chunks(psum[:, 4 * hh, :]), across(c[:, GC, :], P), ALU.subtract) \
                        .then_inc(dve_done, seq.step())
                    dve.wait_ge(dve_done, seq.so_far())
                    dve.tensor_scalar(b["dm"], b["dm"], 0.0, None, ALU.min) \
                        .then_inc(dve_done, seq.step(f"d{hh}.dif"))
                    dve.tensor_tensor(b["qd"], b["qn"], b["ta"], ALU.mult).then_inc(dve_done, seq.step(f"d{hh}.qd"))
                for hh in range(2):
                    b = hb[hh]
                    dve.wait_ge(act_done, seq.at(f"d{hh}.dec"))
                    dve.wait_ge(pe_done, seq.at(f"d{hh}.KK"))
                    dve.wait_ge(pe_done, seq.at(f"d{hh}.QK"))
                    step(chunks(b["dm"]), chunks(b["dm"]), tri, ALU.mult, op=dve.tensor_tensor)
                    dve.tensor_tensor(b["at"], psum[:, 4 * hh + 3, :], b["dm"], ALU.mult) \
                        .then_inc(dve_done, seq.step())
                    step(chunks(b["lt"]), chunks(b["dm"]), strict, ALU.mult, op=dve.tensor_tensor)
                    step(b["lt"], psum[:, 4 * hh + 1, :], b["lt"], ALU.mult, op=dve.tensor_tensor)
                    step(b["lt"], psum[:, 4 * hh + 2, :], b["lt"], ALU.mult, op=dve.tensor_tensor)
                    step(chunks(b["K"][0]), chunks(b["lt"]), rows(levels[:, 0, :]), ALU.mult,
                         op=dve.tensor_tensor, mark=f"d{hh}.K0")
                    dve.tensor_tensor(chunks(b["K"][1]), chunks(b["lt"]), rows(levels[:, 1, :]), ALU.mult) \
                        .then_inc(dve_done, seq.step(f"d{hh}.K1"))
                    dve.tensor_tensor(chunks(b["X"]), rows(ident), chunks(b["K"][0]), ALU.subtract) \
                        .then_inc(dve_done, seq.step())
                    dve.wait_ge(pe_done, seq.at(f"d{hh}.K0T"))
                    dve.tensor_tensor(chunks(b["M"]), rows(ident), chunks(psum[:, 4 * hh, :]), ALU.subtract) \
                        .then_inc(dve_done, seq.step(f"d{hh}.X0"))
                for lev in range(1, 7):
                    for hh in range(2):
                        b = hb[hh]
                        if lev < 6:
                            if lev >= 2:
                                dve.wait_ge(pe_done, seq.at(f"d{hh}.T{lev - 1}"))
                            dve.tensor_tensor(chunks(b["K"][(lev + 1) % 2]), chunks(b["lt"]),
                                                   rows(levels[:, lev + 1, :]), ALU.mult) \
                                .then_inc(dve_done, seq.step(f"d{hh}.K{lev + 1}"))
                        dve.wait_ge(pe_done, seq.at(f"d{hh}.XT{lev}"))
                        if lev < 6:
                            dve.wait_ge(pe_done, seq.at(f"d{hh}.MT{lev}"))
                            dve.tensor_tensor(b["M"], b["M"], psum[:, 4 * hh + 2, :], ALU.subtract) \
                                .then_inc(dve_done, seq.step())
                        dve.wait_ge(dve_done, seq.so_far())
                        dve.tensor_tensor(b["X"], b["X"], psum[:, 4 * hh + 1, :], ALU.subtract) \
                            .then_inc(dve_done, seq.step(f"d{hh}.X{lev}"))
                for hh in range(2):
                    seq.note(f"d{hh}.R0")
                for t in range(NT):
                    cs = slice(t * P, (t + 1) * P)
                    if t:
                        for hh in range(2):
                            b, c = hb[hh], hb[hh]["c"]
                            dve.wait_ge(pe_done, seq.at(f"d{hh}.kS{t}"))
                            dve.scalar_tensor_tensor(b["R"], psum[:, 4 * hh, 0:P], c[:, NBE, t:t + 1],
                                                          b["vb"][:, cs], ALU.mult, ALU.add) \
                                .then_inc(dve_done, seq.step(f"d{hh}.R{t}"))
                    if t < NT - 1:
                        for hh in range(2):
                            b, c = hb[hh], hb[hh]["c"]
                            dve.wait_ge(pe_done, seq.at(f"d{hh}.dS{t}"))
                            dve.wait_ge(pe_done, seq.at(f"d{hh}.o{t}"))
                            if t:
                                dve.scalar_tensor_tensor(b["S"], b["S"], c[:, EL, t:t + 1], psum[:, 4 * hh + 3, 0:P],
                                                              ALU.mult, ALU.add) \
                                    .then_inc(dve_done, seq.step(f"d{hh}.S{t}"))
                            else:
                                dve.tensor_copy(b["S"], psum[:, 4 * hh + 3, 0:P]) \
                                    .then_inc(dve_done, seq.step(f"d{hh}.S{t}"))
                for hh in range(2):
                    b = hb[hh]
                    dve.wait_ge(act_done, seq.at(f"d{hh}.ors"))
                    dve.scalar_tensor_tensor(b["tb"], psum[:, 4 * hh + 2, :], s2("normw"), b["tb"], ALU.mult, ALU.mult) \
                        .then_inc(dve_done, seq.step())
                    dve.wait_ge(dve_done, seq.so_far())
                    z = qkvz[:, bass.ds(i * (8 * T) + (4 * hh + 3) * T, T)]
                    dve.tensor_tensor(z, z, b["tb"], ALU.mult).then_inc(dve_done, seq.step())
            meet("wo")
            for k in range(KD):
                low("zo", k, xl, zt[:, :, 3, :], xh)

            def add_mix(stage, r, ps):
                dve.scalar_tensor_tensor(x[:, r, :], x[:, r, :], ALPHA, ps, ALU.mult, ALU.add) \
                    .then_inc(dve_done, seq.step(f"{stage}.r{r}"))

            for r in range(8):
                dve.wait_ge(slot_used, seq.at(f"wo.t{r}"))
                add_mix("l0", r, psum[:, r % 4, :])
                seq.note(f"wo.d{r}")
            layer_norm("l0", 0, rs2)

            def experts(m, which):
                meet(f"{m}.route")
                dve.wait_ge(act_done, seq.at(f"{m}.lgs"))
                TT, TS = dve.tensor_tensor, dve.tensor_scalar
                gl, el = lg[:, :, 0:NG], lg[:, :, NG:NG + NE]
                def col(i):
                    return rc[:, i, :]
                def reduce(dst, src, op):
                    dve.tensor_reduce(dst, src, AX, op).then_inc(dve_done, seq.step())
                    dve.wait_ge(dve_done, seq.so_far())
                g0, g1, g2, g3 = (rt[i][:, :, 0:NG] for i in range(4))
                reduce(col(0), gl, ALU.max)
                step(g0, gl, across(col(0), NG), ALU.subtract, op=TT, mark=f"{m}.ge")
                step(g2, gl, across(col(0), NG), ALU.is_equal, op=TT)
                step(g2, g2, rows(cc("iota8")[:, 0:NG]), ALU.mult, op=TT)
                reduce(col(3), g2, ALU.max)
                step(g2, g2, across(col(3), NG), ALU.is_equal, op=TT)
                step(g3, g2, 1.0, BIG, ALU.subtract, ALU.mult, op=TS)
                dve.wait_ge(act_done, seq.at(f"{m}.gx"))
                reduce(col(1), g1, ALU.add)
                dve.reciprocal(col(2), col(1)).then_inc(dve_done, seq.step())
                dve.wait_ge(dve_done, seq.so_far())
                def groups(v):
                    return v.rearrange("p t (g e) -> p t g e", e=EPG)
                for v, op in ((g2, ALU.mult), (g3, ALU.add)):
                    step(groups(rt[4]), groups(el if op == ALU.mult else rt[4]),
                         v.unsqueeze(3).to_broadcast([P, NT, NG, EPG]), op, op=TT)
                for c in range(2):
                    oh = rt[c]
                    reduce(col(4 + c), rt[4], ALU.max)
                    step(oh, rt[4], across(col(4 + c), NE), ALU.is_equal, op=TT)
                    step(oh, oh, rows(cc("iota32")), ALU.mult, op=TT)
                    reduce(col(6 + c), oh, ALU.max)
                    step(oh, oh, across(col(6 + c), NE), ALU.is_equal, op=TT)
                    if c == 0:
                        flat = lambda v: v.rearrange("p t c -> p (t c)")
                        step(flat(rt[4]), flat(oh), -3 * BIG, flat(rt[4]), ALU.mult, ALU.add,
                             op=dve.scalar_tensor_tensor)
                step(rt[2], rt[0], rt[1], ALU.add, op=TT, mark=f"{m}.chosen")
                step(col(8), col(5), col(4), ALU.subtract, op=TT, mark=f"{m}.d")
                dve.wait_ge(act_done, seq.at(f"{m}.e2"))
                step(col(10), col(9), 1.0, None, ALU.add, op=TS)
                dve.reciprocal(col(11), col(10)).then_inc(dve_done, seq.step())
                dve.wait_ge(dve_done, seq.so_far())
                step(col(12), col(2), col(11), ALU.mult, op=TT)
                step(col(13), col(12), col(9), ALU.mult, op=TT)
                dve.wait_ge(pe_done, seq.at(f"{m}.rank"))
                rank = psum[:, 1, 0:NT * NE].rearrange("p (t c) -> p t c", c=NE)
                count, n_jobs, ends, starts = (psum[:, 2, 0:NE], *(rt[5][:, q, :] for q in range(3)))
                step(n_jobs, count, 1.0, None, ALU.is_ge, op=TS)
                for n in (1, 2, 3):
                    step(starts, count, float(n * P + 1), None, ALU.is_ge, op=TS)
                    step(n_jobs, n_jobs, starts, ALU.add, op=TT)
                step(ends, ones[:, 0:NE], n_jobs, 0.0, ALU.mult, ALU.add, op=dve.tensor_tensor_scan)
                step(starts, ends, n_jobs, ALU.subtract, op=TT)
                for c in range(2):
                    rk, a, b_ = col(14 + c), col(16), col(17)
                    step(rt[3], rank, rt[c], ALU.mult, op=TT)
                    reduce(rk, rt[3], ALU.add)
                    step(a, rk, float(P), None, ALU.is_ge, op=TS)
                    for n in (2, 3):
                        step(b_, rk, float(n * P), None, ALU.is_ge, op=TS)
                        step(a, a, b_, ALU.add, op=TT)
                    step(rt[3], rows(starts), rt[c], ALU.mult, op=TT)
                    reduce(b_, rt[3], ALU.add)
                    step(b_, rk, float(JOBS), b_, ALU.mult, ALU.add, op=dve.scalar_tensor_tensor)
                    step(b_, a, -float(P * JOBS - 1), b_, ALU.mult, ALU.add, op=dve.scalar_tensor_tensor)
                    dve.tensor_copy(dest[:, c, :].bitcast(I32), b_).then_inc(dve_done, seq.step(f"{m}.dest"))
                    dve.wait_ge(dve_done, seq.so_far())
                whole = rt[4].rearrange("p t c -> p (t c)")[:, 0:JOBS].bitcast(I32)
                step(jwork, cc("jobs").unsqueeze(2).to_broadcast([P, JOBS, NE]),
                     ends.unsqueeze(1).to_broadcast([P, JOBS, NE]), ALU.is_ge, op=TT)
                reduce(jobs, jwork, ALU.add)
                step(jobs, jobs, float(NE - 1), None, ALU.min, op=TS)
                dve.tensor_copy(whole, jobs).then_inc(dve_done, seq.step())
                dve.wait_ge(dve_done, seq.so_far())
                step(jobs.bitcast(I32), whole, op=dve.tensor_copy)
                step(rc[:, 20, 0:1], ends[:, NE - 1:NE], 1.0, None, ALU.add, op=TS)
                step(rnd[:, 1:2].bitcast(I32), rc[:, 20, 0:1], op=dve.tensor_copy)
                step(rnd[:, 0:1].bitcast(I32), rnd[:, 1:2].bitcast(I32), 1, None, ALU.logical_shift_right,
                     op=TS, mark=f"{m}.rnd")
                rounds = seq.count_of(rnd[0:1, 0:1].bitcast(I32), 1, ROUNDS_MAX)
                meet(f"{m}.ex")
                L = f"{m}.ex"

                def x_out(ee, mark):
                    for half in range(2):
                        dve.tensor_copy(xT[:, ee].rearrange("p k c -> p (k c)")[:, 512 * half:512 * half + 512],
                                             psum[:, half, :]).then_inc(dve_done, seq.step(f"{m}.{mark}"))

                dve.wait_ge(pe_done, seq.at(f"{m}.Tpre"))
                x_out(0, "xTpre")
                with seq.rounds(L, rounds):
                    dve.wait_ge(pe_done, seq.at(f"{m}.T1"))
                    x_out(1, "xT1")
                    for ee in range(2):
                        dve.wait_ge(slot_used, seq.at(f"{m}.g{ee}"))
                        dve.wait_ge(act_done, seq.at(f"{m}.sg{ee}"))
                        TT(hs[:, ee, :], sg[:, ee, :], psum[:, (3, 7)[ee], :], ALU.mult) \
                            .then_inc(dve_done, seq.step(f"{m}.hs{ee}"))
                    dve.wait_ge(pe_done, seq.at(f"{m}.T0n"))
                    x_out(0, "xT0n")
                    for ee in range(2):
                        dve.wait_ge(slot_used, seq.at(f"{m}.z{ee}"))
                        dve.wait_ge(rows_scattered[ee], seq.at(f"{m}.sc{ee}", back=L))
                        dve.tensor_copy(ym[:, ee, 512:D], psum[:, (6, 7)[ee], :]) \
                            .then_inc(dve_done, seq.step(f"{m}.yd{ee}"))
                meet(f"{m}.back")
                for t in range(NT):
                    dve.wait_ge(rows_back[t % 2], seq.at(f"{m}.y2{t}"))
                    step(yt[:, t, :], y2[:, t % 2, 0, :], col(12)[:, t:t + 1], None, ALU.mult, op=TS)
                    dve.scalar_tensor_tensor(yt[:, t, :], y2[:, t % 2, 1, :], col(13)[:, t:t + 1], yt[:, t, :],
                                                  ALU.mult, ALU.add).then_inc(dve_done, seq.step(f"{m}.yt{t}"))
                for k in range(KD):
                    dve.wait_ge(pe_done, seq.at(f"{m}.f{k}"))
                    add_mix(m, k, psum[:, k % 4, :])
                layer_norm(m, which, rs4)

            experts("m0", 1)
            meet("kda")
            for k in range(KD):
                low("xda", k, oda_r, x, sq3_r)
            LAM_INIT = 0.8 - 0.6 * math.exp(-0.3 * 1)
            lp = s2("lam").rearrange("p (a b d) -> p a b d", a=2, b=2)
            dve.memset(qz, 0.0).then_inc(dve_done, seq.step("qz.zeros"))
            step(lam[:, 0:128].rearrange("p (a d) -> p a d", a=2), lp[:, :, 0, :], lp[:, :, 1, :], ALU.mult,
                 op=dve.tensor_tensor)
            dve.tensor_reduce(lam[:, 130:132], lam[:, 0:128].rearrange("p (a d) -> p a d", a=2), AX, ALU.add) \
                .then_inc(dve_done, seq.step("lam.s"))
            dve.wait_ge(act_done, seq.at("lam.e"))
            step(lam[:, 134:135], lam[:, 133:134], lam[:, 132:133], ALU.subtract, op=dve.tensor_tensor)
            step(lam[:, 134:135], lam[:, 134:135], -LAM_INIT, None, ALU.add, op=dve.tensor_scalar)
            step(lam[:, 135:136], s2("subln"), 1.0 - LAM_INIT, None, ALU.mult, op=dve.tensor_scalar)
            dve.wait_ge(act_done, seq.at("vda.out"))
            with seq.loop("da", 4) as j:
                dve.wait_ge(pe_done, seq.at("a7.o", back="da"))
                dve.wait_ge(dve_done, seq.so_far())
                for hh in range(2):
                    dve.tensor_copy(va_h[:, hh], vda[:, :, bass.ds(j * (2 * P) + hh * P, P)]) \
                        .then_inc(dve_done, seq.step())
                seq.note("da.v")

                def maxima2(u):
                    w = (u % 4 + 1) * P
                    dve.wait_ge(pe_done, seq.at(f"a{u}.S"))
                    c = dcols[:, u % 4, :]
                    banks = psum[:, 2 * (u % 2):2 * (u % 2) + 2, :]
                    dve.tensor_tensor(banks[:, :, w - P:w], banks[:, :, w - P:w], rows(cc("causal"), 2), ALU.add) \
                        .then_inc(dve_done, seq.step())
                    dve.wait_ge(dve_done, seq.so_far())
                    dve.tensor_reduce(c[:, 0:2], banks[:, :, 0:w], AX, ALU.max).then_inc(dve_done, seq.step())
                    dve.wait_ge(dve_done, seq.so_far())
                    dve.tensor_scalar(c[:, 2:4], c[:, 0:2], -SCALE, None, ALU.mult) \
                        .then_inc(dve_done, seq.step(f"a{u}.m"))

                def combine(u):
                    w = (u % 4 + 1) * P
                    dve.wait_ge(act_done, seq.at(f"a{u}.e"))
                    c = dcols[:, u % 4, :]
                    p0, p1 = pda[:, 2 * (u % 3), 0:w], pda[:, 2 * (u % 3) + 1, 0:w]
                    dve.reciprocal(c[:, 6:8], c[:, 4:6]).then_inc(dve_done, seq.step())
                    dve.wait_ge(dve_done, seq.so_far())
                    dve.tensor_tensor(c[:, 8:9], c[:, 7:8], lam[:, 134:135], ALU.mult) \
                        .then_inc(dve_done, seq.step())
                    dve.tensor_scalar(p0, p0, c[:, 6:7], None, ALU.mult).then_inc(dve_done, seq.step())
                    dve.wait_ge(dve_done, seq.so_far())
                    dve.scalar_tensor_tensor(p0, p1, c[:, 8:9], p0, ALU.mult, ALU.add) \
                        .then_inc(dve_done, seq.step(f"a{u}.p"))

                maxima2(0)
                for u in range(8):
                    if u + 1 < 8:
                        maxima2(u + 1)
                    combine(u)
            meet("dan")
            for hd_ in range(8):
                dve.wait_ge(act_done, seq.at(f"dan.rs{hd_}"))
                dve.scalar_tensor_tensor(oda[:, hd_, :], oda[:, hd_, :], lam[:, 135:136], sq3[:, hd_, :],
                                              ALU.mult, ALU.mult).then_inc(dve_done, seq.step("dan.o"))
            meet("wo2")
            for k in range(KD):
                low("oo", k, oda_r, oda, kda_r)
            for r in range(8):
                dve.wait_ge(slot_used, seq.at(f"wo2.t{r}"))
                add_mix("l1", r, psum[:, r % 4, :])
                seq.note(f"wo2.d{r}")
            layer_norm("l1", 2, rs3)
            experts("m1", 3)
            seq.note("result")


def constants():
    c = np.zeros((P, CC_COLS), np.float32)
    def put(name, a):
        c[:, CC[name][0]:CC[name][1]] = a
    i = np.arange(P)
    put("ident", np.eye(P))
    put("ones", np.ones((P, P)))
    perm = np.zeros((P, P))
    for m in range(P):
        b, r = m // HD * HD, m % HD
        if r < HD // 2:
            perm[b + r + HD // 2, m] = -1.0
        else:
            perm[b + r - HD // 2, m] = 1.0
    put("perm", perm)
    put("tri", i[:, None] <= i[None, :])
    put("causal", np.where(i[None, :] <= i[:, None], 0.0, -BIG))
    put("band", np.where(i[None, :] > i[:, None], 0.0, -BIG))
    t = np.arange(NT)[None, :, None] * P + i[:, None, None]
    end = np.arange(NC)[None, None, :] * 16 + 31
    put("cmp", np.where(end <= t, 0.0, -BIG).reshape(P, -1))
    put("strictT", i[:, None] < i[None, :])
    lev = np.zeros((P, 7, P))
    for s in range(7):
        w = 1 << s
        lev[:, s, :] = (i[:, None] // (2 * w) == i[None, :] // (2 * w)) & (i[:, None] // w < i[None, :] // w)
    put("levels", lev.reshape(P, -1))
    inv = 10000.0 ** (-np.arange(HD // 2, dtype=np.float32) / np.float32(HD // 2))
    put("invf", np.tile(inv.astype(np.float32), 4)[:, None])
    put("eps", EPS)
    put("lneps", LN_EPS)
    put("one", 1.0)
    put("iota8", 8.0 - np.arange(8)[None, :])
    put("jobs", np.arange(JOBS)[None, :])
    put("iota32", 32.0 - np.arange(32)[None, :])
    return c


def by_feature(w):
    k, c = w.shape
    return w.reshape(k // P, P, c // P, P).transpose(2, 1, 0, 3).reshape(c // P, P, -1)


def by_token(w, width=512):
    k, c = w.shape
    full = np.zeros((k, width), w.dtype)
    full[:, :c] = w
    return full.reshape(k // (2 * P), 2, P, width).transpose(0, 2, 1, 3).reshape(k // (2 * P), P, -1)


def head_pairs(w, axis):
    s = list(w.shape)
    split = w.reshape(s[:axis] + [2, 4, HD] + s[axis + 1:])
    return np.swapaxes(split, axis, axis + 1).reshape(s)


def lay_out(a):
    slots, smalls = [], []
    for l in range(LAYERS):
        w = a["w_in"][l]
        qa, ka, va, qb, kcb, vcb, ksb, vsb, kwb, vwb, gn, ga, gb = np.split(
            w, np.cumsum([512, 128, 128, 512, 128, 128, 128, 128, 128, 128, 24, 1024])[:12], axis=1)
        slots += [by_feature(head_pairs(qa, 1)), by_feature(ka), by_feature(head_pairs(qb, 1)), by_feature(ksb),
                  by_feature(kwb), by_feature(kcb), by_feature(vcb), by_feature(ga), by_feature(gb)]
        gn = gn.reshape(D, 2, 4, 3).transpose(0, 2, 1, 3).reshape(D, 24)
        slots.append(by_token(np.concatenate([va, vsb, vwb, gn], axis=1)))
        for kv in range(2):
            w1 = a["cmp_w1"][l, kv].reshape(4, 8, HD, P).transpose(0, 2, 1, 3).reshape(4, HD, D)
            slots.append(np.concatenate([w1, w1], axis=1))
        ba = by_feature(head_pairs(a["w_branch_a"][l], 0))
        bb = by_feature(head_pairs(a["w_branch_b"][l], 0))
        slots.append(np.concatenate([ba, bb], axis=2))
        slots.append(by_feature(a["w_out"][l]))
        up = by_feature(a["ffn_w_up"][l]).reshape(2, PAIRS, P, D).transpose(1, 0, 2, 3).reshape(2 * PAIRS, P, D)
        slots.append(up)
        slots.append(a["ffn_w_down"][l].reshape(PAIRS, P, D))
        slots.append(np.zeros((LAYER_PAD, P, D), np.float32))
        s = np.zeros((P, SM_COLS), np.float32)
        def put(name, v):
            s[:, SM[name][0]:SM[name][1]] = v
        gains = np.stack([a[n][l] for n in ("attn_pre_gain", "attn_post_gain", "ffn_pre_gain", "ffn_post_gain")])
        put("gains", gains.reshape(4, KD, P).transpose(2, 0, 1).reshape(P, -1))
        put("sinks", a["attn_sinks"][l].reshape(2, 4).T.reshape(1, 8))
        cw = np.concatenate([a["ffn_conv_w"][l], a["ffn_conv_b"][l][None]], axis=0)
        put("conv", cw.reshape(4, 2, PAIRS, P).transpose(3, 2, 1, 0).reshape(P, -1))
        put("b1", a["cmp_b1"][l].T)
        pos = a["cmp_pos_emb"][l].transpose(2, 0, 1).reshape(HD, 64)
        put("pos", np.concatenate([pos, pos], axis=0))
        for name, kv in (("w2k", 0), ("w2v", 1)):
            w2 = np.zeros((P, 2, P), np.float32)
            w2[:, 0, :HD] = a["cmp_w2"][l, kv]
            w2[:, 1, HD:] = a["cmp_w2"][l, kv]
            put(name, w2.reshape(P, -1))
        smalls.append(s)
    w = a["a_w_in_2"][0]
    heads = by_feature(w[:, :4 * D]).reshape(4, DH, P, D).transpose(1, 0, 2, 3).reshape(4 * DH, P, D)
    slots += [heads, by_feature(a["a_w_out_2"][0]), by_feature(a["kv_w_2"][:, :D])]
    slots += [by_token(a["kv_w_2"][:, D + 512 * half:D + 512 * half + 512]) for half in range(2)]
    slots += [by_feature(a["b_w_q_2"][0]), by_feature(a["b_w_out_2"][0])]
    s2 = np.zeros((P, S2_COLS), np.float32)
    def put2(name, v):
        s2[:, S2[name][0]:S2[name][1]] = v
    put2("ab", w[:, 4 * D:].reshape(KD, P, 16).transpose(1, 0, 2).reshape(P, -1))
    put2("conv", a["a_conv_w_2"][0].reshape(4, 3, DH, P).transpose(3, 2, 1, 0).reshape(P, -1))
    put2("alog", a["a_a_log_2"][0][None])
    put2("dtb", a["a_dt_bias_2"][0][None])
    put2("normw", a["a_norm_w_2"][0][:, None])
    ln = np.stack([a[n][l] for l in range(LAYERS) for n in ("ln_mix_g_2", "ln_mix_b_2", "ln_ffn_g_2", "ln_ffn_b_2")])
    put2("ln", ln.reshape(8, KD, P).transpose(2, 0, 1).reshape(P, -1))
    router = np.concatenate([a["moe_w_group_2"], a["moe_w_expert_2"]], axis=2)
    put2("router", router.reshape(LAYERS, KD, P, 36).transpose(2, 0, 1, 3).reshape(P, -1))
    put2("lam", a["b_lambda_2"][0].reshape(1, -1))
    put2("subln", a["b_subln_w_2"][0][:, None])
    row = np.arange(P)[:, None, None] + P * np.arange(NT)[None, None, :]
    ids = (2 * row + np.arange(2)[None, :, None]).reshape(P, 8).astype(np.int32)
    return {
        "small2": s2,
        "ids": ids,
        "oob": np.full((P, JOBS), 1 << 20, np.int32),
        "moe_w13": a["moe_w13_2"].reshape(-1, 2 * EFF),
        "moe_w2": a["moe_w2_2"].reshape(-1, D),
        "wstream": np.concatenate(slots, axis=0),
        "small": np.stack(smalls),
        "const": constants(),
        "positions": np.broadcast_to(a["positions"][0][None, :], (P, T)).copy(),
        "xT": a["x"][0].T.reshape(KD, P, T).transpose(1, 0, 2).copy(),
    }


def kernel(**inputs):
    import concourse.bacc as bacc
    from concourse.bass_utils import run_bass_kernel_spmd

    arrays = lay_out({n: np.asarray(v) for n, v in inputs.items()})
    book = Book()
    for _ in range(3):
        nc = bacc.Bacc("TRN2", target_bir_lowering=False, num_devices=1)
        ins = {n: nc.dram_tensor("in_" + n, v.shape, mybir.dt.from_np(v.dtype), kind="ExternalInput").ap()
               for n, v in arrays.items()}
        out = nc.dram_tensor("result", (P, KD, T), F32, kind="ExternalOutput").ap()
        new = Book()
        build(nc, ins, out, book, new)
        book = new
    r = run_bass_kernel_spmd(nc, [{"in_" + n: v for n, v in arrays.items()}], core_ids=[0])
    result = r.results[0]["result"]
    return result.transpose(1, 0, 2).reshape(D, T).T[None].copy()
```
